# Optimizing a Trainium2 kernel written in Bass

```python
import jax, jax.numpy as jnp
from jax import lax
import numpy as np

D_MODEL = 1024
BATCH = 1
SEQ = 256
DEPTH = 1
DEC_BATCH = 1
DEC_SEQ = 64
PAST_LEN = 256

CHUNK = 64
A_HEADS = 8
A_HEAD_DIM = 64
A_WIDTH = A_HEADS * A_HEAD_DIM
A_PAST_CHUNKS = 8
A_BAND = (A_PAST_CHUNKS + 1) * CHUNK
A_MAX_REL = 256
MLP_CHUNK = 128
MLP_GROUPS = 8
MLP_WIDTH = 512
MLP_GROUP_DIM = MLP_WIDTH // MLP_GROUPS
N_IN = 3 * A_WIDTH + 2 * MLP_WIDTH + 2 * D_MODEL
SPLIT_POINTS = (A_WIDTH, 2 * A_WIDTH, 3 * A_WIDTH, 3 * A_WIDTH + MLP_WIDTH,
                3 * A_WIDTH + 2 * MLP_WIDTH, 3 * A_WIDTH + 2 * MLP_WIDTH + D_MODEL)
N_EXPERTS = 64
TOP_K = 8
N_GROUPS = 8
TOPK_GROUPS = 4
EXPERT_DIM = 256
SHARED_DIM = 256
ROUTED_SCALE = 2.5
MOE_BLOCK = 256
PLE_DIM = 256
ALPHA = (2 * DEPTH) ** 0.25
BETA = (8 * DEPTH) ** -0.25
LN_EPS = 1e-5

kernel_name = 'streaming_hybrid_chunkattn_gmlp_moe_step'

def layer_norm(x, g, b):
    xf = x.astype(jnp.float32)
    xc = xf - xf.mean(-1, keepdims=True)
    var = jnp.mean(xc * xc, -1, keepdims=True)
    y = xc * lax.rsqrt(var + LN_EPS) * g.astype(jnp.float32) + b.astype(jnp.float32)
    return y.astype(x.dtype)

def relative_bias(table, rel):
    idx = jnp.clip(rel, -A_MAX_REL, A_MAX_REL) + A_MAX_REL
    return table[:, idx].astype(jnp.float32)

def chunk_attention_prompt(q, k, v, rel_table):
    b, s, h, dh = q.shape
    nc = s // CHUNK
    qc = q.reshape(b, nc, CHUNK, h, dh)
    pad = ((0, 0), (A_PAST_CHUNKS, 0), (0, 0), (0, 0), (0, 0))
    kp = jnp.pad(k.reshape(b, nc, CHUNK, h, dh), pad)
    vp = jnp.pad(v.reshape(b, nc, CHUNK, h, dh), pad)
    kb = jnp.concatenate([kp[:, w:w + nc] for w in range(A_PAST_CHUNKS + 1)], axis=2)
    vb = jnp.concatenate([vp[:, w:w + nc] for w in range(A_PAST_CHUNKS + 1)], axis=2)
    rel = (jnp.arange(A_BAND)[None, :] - A_PAST_CHUNKS * CHUNK) - jnp.arange(CHUNK)[:, None]
    bias = relative_bias(rel_table, rel)
    key_chunk = jnp.arange(nc)[:, None] - A_PAST_CHUNKS + jnp.arange(A_BAND)[None, :] // CHUNK
    valid = key_chunk >= 0
    sc = jnp.einsum('bnqhd,bnkhd->bnhqk', qc, kb).astype(jnp.float32) * (A_HEAD_DIM ** -0.5)
    sc = sc + bias[None, None]
    sc = jnp.where(valid[None, :, None, None, :], sc, -jnp.inf)
    pr = jax.nn.softmax(sc, axis=-1).astype(v.dtype)
    o = jnp.einsum('bnhqk,bnkhd->bnqhd', pr, vb)
    return o.reshape(b, s, h * dh)

def chunk_attention_sample(q, k, v, cache_k, cache_v, rel_table):
    b, t, h, dh = q.shape
    L = cache_k.shape[1]
    kk = jnp.concatenate([cache_k.astype(k.dtype), k], axis=1)
    vv = jnp.concatenate([cache_v.astype(v.dtype), v], axis=1)
    rel = jnp.arange(L + t)[None, :] - L - jnp.arange(t)[:, None]
    bias = relative_bias(rel_table, rel)
    sc = jnp.einsum('bqhd,bkhd->bhqk', q, kk).astype(jnp.float32) * (A_HEAD_DIM ** -0.5) + bias[None]
    pr = jax.nn.softmax(sc, axis=-1).astype(v.dtype)
    o = jnp.einsum('bhqk,bkhd->bqhd', pr, vv)
    return o.reshape(b, t, h * dh)

def spatial_gating(u, vn, w_s, b_s):
    b, t, _ = u.shape
    L = min(t, MLP_CHUNK)
    n = t // L
    w = w_s[:, :L, :L] * jnp.tril(jnp.ones((L, L), w_s.dtype))
    vc = vn.reshape(b, n, L, MLP_GROUPS, MLP_GROUP_DIM)
    mixed = jnp.einsum('gts,bnsgc->bntgc', w, vc) + b_s[:, :L].T[:, :, None]
    out = u.reshape(b, n, L, MLP_GROUPS, MLP_GROUP_DIM) * mixed
    return out.reshape(b, t, MLP_WIDTH).astype(u.dtype)

def moe_ffn(h, router_w, router_bias, exp_w1, exp_w3, exp_w2, sh_w1, sh_w3, sh_w2):
    t = h.shape[0]
    scores = jax.nn.sigmoid(jnp.dot(h.astype(jnp.float32), router_w.astype(jnp.float32)))
    sel = scores + router_bias.astype(jnp.float32)
    grp = sel.reshape(t, N_GROUPS, N_EXPERTS // N_GROUPS)
    grp_score = lax.top_k(grp, 2)[0].sum(-1)
    _, grp_idx = lax.top_k(grp_score, TOPK_GROUPS)
    grp_keep = (grp_idx[..., None] == jnp.arange(N_GROUPS)).any(axis=1)
    exp_keep = jnp.repeat(grp_keep, N_EXPERTS // N_GROUPS, axis=1)
    _, top_idx = lax.top_k(jnp.where(exp_keep, sel, -jnp.inf), TOP_K)
    top_w = jnp.take_along_axis(scores, top_idx, axis=-1)
    top_w = top_w / top_w.sum(-1, keepdims=True) * ROUTED_SCALE
    n_assign = t * TOP_K
    flat_e = top_idx.reshape(-1)
    flat_tok = jnp.repeat(jnp.arange(t, dtype=jnp.int32), TOP_K)
    flat_w = top_w.reshape(-1).astype(h.dtype)
    order = jnp.argsort(flat_e, stable=True)
    e_sorted = flat_e[order]
    counts = jnp.bincount(flat_e, length=N_EXPERTS)
    start = jnp.cumsum(counts) - counts
    padded = (counts + MOE_BLOCK - 1) // MOE_BLOCK * MOE_BLOCK
    pad_end = jnp.cumsum(padded)
    pad_start = pad_end - padded
    dest = pad_start[e_sorted] + jnp.arange(n_assign) - start[e_sorted]
    n_blocks = -(-n_assign // MOE_BLOCK) + N_EXPERTS
    n_slots = n_blocks * MOE_BLOCK
    slot_tok = jnp.zeros((n_slots,), jnp.int32).at[dest].set(flat_tok[order])
    slot_w = jnp.zeros((n_slots,), h.dtype).at[dest].set(flat_w[order])
    blk_e = jnp.minimum(jnp.searchsorted(pad_end, jnp.arange(n_blocks) * MOE_BLOCK, side='right'),
                        N_EXPERTS - 1)

    def expert_block(args):
        tok_b, w_b, e = args
        xb = h[tok_b]
        a = xb @ exp_w1[e]
        g = xb @ exp_w3[e]
        return ((jax.nn.silu(a) * g) @ exp_w2[e]) * w_b[:, None]

    y_slots = lax.map(expert_block, (slot_tok.reshape(n_blocks, MOE_BLOCK),
                                     slot_w.reshape(n_blocks, MOE_BLOCK), blk_e))
    routed = jax.ops.segment_sum(y_slots.reshape(n_slots, -1), slot_tok, num_segments=t)
    shared = (jax.nn.silu(h @ sh_w1) * (h @ sh_w3)) @ sh_w2
    return (routed + shared).astype(h.dtype)

def trunk_layer(x, p, cache_k, cache_v, w_in, rel_table, mlp_ln_g, mlp_ln_b, mlp_w_s, mlp_b_s,
                w_branch_a, w_branch_b, w_out, ln1_g, ln1_b, router_w, router_bias,
                exp_w1, exp_w3, exp_w2, sh_w1, sh_w3, sh_w2, ln2_g, ln2_b,
                ple_w_gate, ple_w_proj):
    b, t, d = x.shape
    z = x @ w_in
    q, k, v, u, vs, ga, gb = jnp.split(z, SPLIT_POINTS, axis=-1)
    q = q.reshape(b, t, A_HEADS, A_HEAD_DIM)
    k = k.reshape(b, t, A_HEADS, A_HEAD_DIM)
    v = v.reshape(b, t, A_HEADS, A_HEAD_DIM)
    if cache_k is None:
        oa = chunk_attention_prompt(q, k, v, rel_table)
        keep = min(A_PAST_CHUNKS * CHUNK, t)
        new_k, new_v = k[:, t - keep:], v[:, t - keep:]
    else:
        oa = chunk_attention_sample(q, k, v, cache_k, cache_v, rel_table)
        new_k, new_v = k, v
    un = jax.nn.gelu(u)
    vn = layer_norm(jax.nn.gelu(vs), mlp_ln_g, mlp_ln_b)
    ob = spatial_gating(un, vn, mlp_w_s, mlp_b_s)
    new_mlp_v = vn[:, ((t - 1) // MLP_CHUNK) * MLP_CHUNK:]
    mix = jax.nn.sigmoid(ga) * (oa @ w_branch_a) + jax.nn.sigmoid(gb) * (ob @ w_branch_b)
    x = layer_norm(ALPHA * x + mix @ w_out, ln1_g, ln1_b)
    ff = moe_ffn(x.reshape(b * t, d), router_w, router_bias, exp_w1, exp_w3, exp_w2,
                 sh_w1, sh_w3, sh_w2).reshape(b, t, d)
    x = layer_norm(ALPHA * x + ff, ln2_g, ln2_b)
    x = x + jax.nn.sigmoid(x @ ple_w_gate) * (p @ ple_w_proj)
    return x, new_k, new_v, new_mlp_v

def setup_inputs(seed: int = 0) -> dict:
    key = jax.random.key(seed)
    ks = jax.random.split(key, 40)
    f32 = jnp.float32

    def nrm(k, shape, scale=1.0):
        return jax.random.normal(k, shape, f32) * scale

    cache_rows = min(A_PAST_CHUNKS * CHUNK, PAST_LEN)
    return {
        'x_prompt': nrm(ks[0], (BATCH, SEQ, D_MODEL)),
        'x_sample': nrm(ks[1], (DEC_BATCH, DEC_SEQ, D_MODEL)),
        'cache_attn_k': nrm(ks[2], (DEPTH, DEC_BATCH, cache_rows, A_HEADS, A_HEAD_DIM)),
        'cache_attn_v': nrm(ks[3], (DEPTH, DEC_BATCH, cache_rows, A_HEADS, A_HEAD_DIM)),
        'p_prompt': nrm(ks[4], (DEPTH, BATCH, SEQ, PLE_DIM)),
        'p_sample': nrm(ks[5], (DEPTH, DEC_BATCH, DEC_SEQ, PLE_DIM)),
        'ln_in_g': 1.0 + nrm(ks[6], (D_MODEL,), 0.05),
        'ln_in_b': nrm(ks[7], (D_MODEL,), 0.05),
        'w_in': nrm(ks[8], (DEPTH, D_MODEL, N_IN), D_MODEL ** -0.5),
        'attn_rel_bias': nrm(ks[9], (DEPTH, A_HEADS, 2 * A_MAX_REL + 1), 0.1),
        'mlp_ln_g': 1.0 + nrm(ks[10], (DEPTH, MLP_WIDTH), 0.05),
        'mlp_ln_b': nrm(ks[11], (DEPTH, MLP_WIDTH), 0.05),
        'mlp_w_s': nrm(ks[12], (DEPTH, MLP_GROUPS, MLP_CHUNK, MLP_CHUNK), MLP_CHUNK ** -0.5),
        'mlp_b_s': 1.0 + nrm(ks[13], (DEPTH, MLP_GROUPS, MLP_CHUNK), 0.1),
        'w_branch_a': nrm(ks[14], (DEPTH, A_WIDTH, D_MODEL), A_WIDTH ** -0.5),
        'w_branch_b': nrm(ks[15], (DEPTH, MLP_WIDTH, D_MODEL), MLP_WIDTH ** -0.5),
        'w_out': nrm(ks[16], (DEPTH, D_MODEL, D_MODEL), BETA * D_MODEL ** -0.5),
        'ln1_g': 1.0 + nrm(ks[17], (DEPTH, D_MODEL), 0.05),
        'ln1_b': nrm(ks[18], (DEPTH, D_MODEL), 0.05),
        'router_w': nrm(ks[19], (DEPTH, D_MODEL, N_EXPERTS), D_MODEL ** -0.5),
        'router_bias': nrm(ks[20], (DEPTH, N_EXPERTS), 0.01),
        'exp_w1': nrm(ks[21], (DEPTH, N_EXPERTS, D_MODEL, EXPERT_DIM), D_MODEL ** -0.5),
        'exp_w3': nrm(ks[22], (DEPTH, N_EXPERTS, D_MODEL, EXPERT_DIM), D_MODEL ** -0.5),
        'exp_w2': nrm(ks[23], (DEPTH, N_EXPERTS, EXPERT_DIM, D_MODEL), BETA * EXPERT_DIM ** -0.5),
        'shared_w1': nrm(ks[24], (DEPTH, D_MODEL, SHARED_DIM), D_MODEL ** -0.5),
        'shared_w3': nrm(ks[25], (DEPTH, D_MODEL, SHARED_DIM), D_MODEL ** -0.5),
        'shared_w2': nrm(ks[26], (DEPTH, SHARED_DIM, D_MODEL), BETA * SHARED_DIM ** -0.5),
        'ln2_g': 1.0 + nrm(ks[27], (DEPTH, D_MODEL), 0.05),
        'ln2_b': nrm(ks[28], (DEPTH, D_MODEL), 0.05),
        'ple_w_gate': nrm(ks[29], (DEPTH, D_MODEL, D_MODEL), D_MODEL ** -0.5),
        'ple_w_proj': nrm(ks[30], (DEPTH, PLE_DIM, D_MODEL), PLE_DIM ** -0.5),
    }

def reference(x_prompt, x_sample, cache_attn_k, cache_attn_v, p_prompt, p_sample,
              ln_in_g, ln_in_b, w_in, attn_rel_bias, mlp_ln_g, mlp_ln_b, mlp_w_s, mlp_b_s,
              w_branch_a, w_branch_b, w_out, ln1_g, ln1_b, router_w, router_bias,
              exp_w1, exp_w3, exp_w2, shared_w1, shared_w3, shared_w2, ln2_g, ln2_b,
              ple_w_gate, ple_w_proj):
    xp = layer_norm(x_prompt, ln_in_g, ln_in_b)
    xs = layer_norm(x_sample, ln_in_g, ln_in_b)
    kp_l, vp_l, ks_l, vs_l, mp_l, ms_l = [], [], [], [], [], []
    for i in range(DEPTH):
        lw = (w_in[i], attn_rel_bias[i], mlp_ln_g[i], mlp_ln_b[i], mlp_w_s[i], mlp_b_s[i],
              w_branch_a[i], w_branch_b[i], w_out[i], ln1_g[i], ln1_b[i], router_w[i],
              router_bias[i], exp_w1[i], exp_w3[i], exp_w2[i], shared_w1[i], shared_w3[i],
              shared_w2[i], ln2_g[i], ln2_b[i], ple_w_gate[i], ple_w_proj[i])
        xp, kp, vp, mp = trunk_layer(xp, p_prompt[i], None, None, *lw)
        xs, ksn, vsn, msn = trunk_layer(xs, p_sample[i], cache_attn_k[i], cache_attn_v[i], *lw)
        kp_l.append(kp)
        vp_l.append(vp)
        ks_l.append(ksn)
        vs_l.append(vsn)
        mp_l.append(mp)
        ms_l.append(msn)
    return (xp, xs, jnp.stack(kp_l), jnp.stack(vp_l), jnp.stack(ks_l), jnp.stack(vs_l),
            jnp.stack(mp_l), jnp.stack(ms_l))


_drawn_inputs = setup_inputs


def setup_inputs(seed=0):
    import zlib

    import numpy as np

    out = dict(_drawn_inputs(seed))
    spreads = {}
    factors = {'attn_rel_bias': 3.143}
    for name, (base, spread) in spreads.items():
        noise = np.random.default_rng([zlib.crc32(name.encode()), seed]).standard_normal(out[name].shape)
        drawn = base * np.exp(spread * noise) if base else spread * noise
        out[name] = __import__('jax').numpy.asarray(drawn.astype(out[name].dtype))
    for name, factor in factors.items():
        out[name] = (out[name] * factor).astype(out[name].dtype)
    return out
```

```python
from contextlib import ExitStack

import concourse.bass as bass
from concourse import mybir

F32 = mybir.dt.float32
F32R = mybir.dt.float32r
BF16 = mybir.dt.bfloat16
I32 = mybir.dt.int32
U32 = mybir.dt.uint32
ALU = mybir.AluOpType
ACT = mybir.ActivationFunctionType
AX = mybir.AxisListType
ds = bass.ds

P = 128
ROWS = (128, 128, 64)
TOK = sum(ROWS)
HEADS, DH = 8, 64
EPS = 1e-5
ALPHA = 2.0 ** 0.25
SCALE = DH ** -0.5
ROUTED_SCALE = 2.5
MASKED = -1.0e30


def trunk_step(nc, x_prompt, x_sample, cache_k, cache_v, p_prompt, p_sample, ln_in_g, ln_in_b, w_in,
               rel_bias, mlp_g, mlp_b, mlp_w_s, mlp_b_s, w_a, w_b, w_out, ln1_g, ln1_b, router_w,
               router_bias, exp_w1, exp_w3, exp_w2, sh_w1, sh_w3, sh_w2, ln2_g, ln2_b, ple_gate,
               ple_proj, y_prompt, y_sample, new_k_prompt, new_v_prompt, new_k_sample, new_v_sample,
               new_mlp_prompt, new_mlp_sample):
    D = x_prompt.shape[2]
    KD = D // P
    N_IN = w_in.shape[2]
    FT = N_IN // P
    CH = 256
    AW = HEADS * DH
    JW = AW // P
    NE = router_w.shape[2]
    HID = exp_w1.shape[3]
    GROUPS, PER_GROUP, KEEP_GROUPS = 8, NE // 8, 4
    SLOTS = 64
    PAIRS = NE // 2
    STEPS = PAIRS // 2
    MAX_ROUNDS = -(-TOK // SLOTS)
    TP = 3 * P
    REL = rel_bias.shape[2]
    PAD = 64
    PEXP = 2 * KD * HID + 2 * D
    Q0, K0, V0, U0, S0, GA0, GB0 = 0, 4, 8, 12, 16, 20, 28

    with ExitStack() as ctx:
        def sb(name, shape, dt=F32):
            return ctx.enter_context(nc.sbuf_tensor(name, shape, dt))

        def sem(name):
            return ctx.enter_context(nc.semaphore(name))

        ring = sb("expert_ring", [P, 2 * 2 * PEXP])
        z = sb("z", [P, FT * TOK])
        xs = sb("xs", [P, 3, D])
        xT = sb("xT", [P, KD, TOK])
        wr = sb("weight_ring", [P, 2, KD, CH])
        ysplit = sb("y_split", [P, 2, 2, D], F32R)
        scat = sb("scatter", [P, 2, TP], F32R)
        ident = sb("ident", [P, P])
        ones = sb("ones", [1, DH])
        tri = sb("tri", [P, P], BF16)
        onesb = sb("ones_bf", [P, P], BF16)
        stats = sb("stats", [P, 3, 2, 6])
        meanvar = sb("meanvar", [P, 3, 2])
        vareps = sb("vareps", [P, 3])
        std = sb("std", [P, 3])
        rstd = sb("rstd", [P, 3])
        smax = sb("smax", [P, 3, HEADS])
        snegmax = sb("snegmax", [P, 3, HEADS])
        ssum = sb("ssum", [P, 3, HEADS])
        srec = sb("srec", [P, 3, HEADS])
        idx_now = sb("idx_now", [P, 2], U32)
        round_thr = sb("round_thr", [1, MAX_ROUNDS - 1])
        round_gt = sb("round_gt", [1, MAX_ROUNDS - 1])
        rounds_f = sb("rounds_f", [1, 2])
        rounds_i = sb("rounds_i", [1, 1], I32)
        PS = ctx.enter_context(nc.psum_tensor("PS", [P, 8, 512], F32))

        def early(at, *shape, rows=P):
            n = 1
            for s in shape:
                n *= s
            v = ring[0:rows, at:at + n]
            if len(shape) == 2:
                return v.rearrange("p (a b) -> p a b", a=shape[0])
            if len(shape) == 3:
                return v.rearrange("p (a b c) -> p a b c", a=shape[0], b=shape[1])
            return v

        prob1 = early(0, HEADS, 256)
        prob0 = early(2048, HEADS, P)
        probs = early(3072, HEADS, TOK, rows=DH)
        probT = early(5632, 4, 3, 384)
        relpad = early(5632, PAD + REL, rows=HEADS)
        v_tok = early(10240, 3, AW)
        k_tok = early(11776, 3, AW)
        ck = early(13312, 2, AW)
        cv = early(14336, 2, AW)
        ckT = early(15360, JW, 256)
        ws = early(16384, 8, P)
        wsT = early(17408, 8, P)
        vn = early(18432, 3, AW)
        mlpvec = early(19968, 2, AW)
        bsrow = early(20992, 8, P, rows=1)
        lninvec = early(22016, 2, D)
        HO = [(h % 2) * 4 + h // 2 for h in range(HEADS)]

        zt = z[:, :].rearrange("p (a t) -> p a t", t=TOK)
        oaT = zt[:, Q0:Q0 + JW, :]
        obT = zt[:, U0:U0 + JW, :]
        mT = zt[:, K0:K0 + KD, :]

        def zv(at, n):
            return z[:, at:at + n]

        lnvec = zv(6400, 2 * D).rearrange("p (a d) -> p a d", a=2)
        rw = zv(8448, KD * NE).rearrange("p (k e) -> p k e", k=KD)
        hsT = zv(8960, 2 * TOK).rearrange("p (a t) -> p a t", a=2)
        rtemp = [zv(3840 + 192 * i, 192).rearrange("p (a e) -> p a e", a=3) for i in range(8)]
        score, sel, msel, replaced, maskf, wt, wres, gmax = rtemp
        rsmall = zv(3840 + 8 * 192, 192).rearrange("p (a e) -> p a e", a=3)
        mask = zv(3840 + 9 * 192, 96).bitcast(BF16).rearrange("p (a e) -> p a e", a=3)
        rbias = zv(3840 + 10 * 192, NE)
        maxcnt = zv(3840 + 11 * 192, 8)
        onehot = zv(0, 3 * NE * SLOTS // 2).bitcast(BF16).rearrange("p (a e s) -> p a e s", a=3, s=SLOTS)
        xg = zv(0, 2 * D).rearrange("p (a d) -> p a d", a=2)
        xgT = zv(2048, 2 * D).rearrange("p (a k s) -> p a k s", a=2, k=KD)
        act_h = zv(4096, 2 * HID).rearrange("p (a d) -> p a d", a=2)
        hid = zv(4608, 2 * HID).rearrange("p (a d) -> p a d", a=2)
        hidT = zv(5120, 2 * HID).rearrange("p (a k s) -> p a k s", a=2, k=2)
        keep = 9984
        pos = zv(keep, 192).rearrange("p (a e) -> p a e", a=3)
        attrs = zv(keep + 192, 480).bitcast(BF16).rearrange("p (a e f) -> p a e f", a=3, f=5)
        table = zv(keep + 672, 320).rearrange("p (i f) -> p i f", f=10)
        slot_tok = zv(keep + 992, PAIRS)
        slot_w = zv(keep + 1024, PAIRS)
        slot_idx = zv(keep + 1056, PAIRS).bitcast(U32)
        iota_slot = zv(keep + 1088, SLOTS)
        iota_tok = zv(keep + 1152, TP)
        acc = xs

        gate_w = [ring[:, PEXP * e:PEXP * e + 4 * D].rearrange("p (k d) -> p k d", k=4) for e in range(2)]
        ple = ring[:, 2 * PEXP:2 * PEXP + 3 * D].rearrange("p (a d) -> p a d", a=3)
        sgate = ring[:, 3 * PEXP:3 * PEXP + 3 * D].rearrange("p (a d) -> p a d", a=3)
        wr0 = wr[:, 0, :, :].rearrange("p k c -> p (k c)")
        p_tok = wr0[:, 0:768].rearrange("p (a d) -> p a d", a=3)
        pT = wr0[:, 768:768 + 2 * TOK].rearrange("p (a t) -> p a t", a=2)
        proj_w = wr[:, 1, :, :].rearrange("p k c -> p (k c)").rearrange("p (k d) -> p k d", k=2)
        sw2 = wr0.rearrange("p (k d) -> p k d", k=2)

        def w13(pair, e, k):
            o = (2 * pair + e) * PEXP
            return ring[:, o:o + 2 * KD * HID].rearrange("p (m k h) -> p m k h", m=2, k=KD)[:, :, k, :]

        def w2(pair, e, k, half):
            o = (2 * pair + e) * PEXP + 2 * KD * HID + k * D + 512 * half
            return ring[:, o:o + 512]

        x1_rows = nc.dram_tensor("x1_rows", (TOK, D), F32, kind="Internal")
        RW = PAD + REL
        rel_dram = nc.dram_tensor("rel_rows", (HEADS, P, RW), F32, kind="Internal")

        x_loaded = sem("x_loaded")
        lnin_loaded = sem("lnin_loaded")
        w_loaded = [sem(f"w_loaded{c}") for c in range(2)]
        cache_loaded = sem("cache_loaded")
        ws_loaded = sem("ws_loaded")
        mlpvec_loaded = sem("mlpvec_loaded")
        bs_loaded = sem("bs_loaded")
        rel_loaded = sem("rel_loaded")
        rel_stored = sem("rel_stored")
        bias_loaded = sem("bias_loaded")
        route_loaded = sem("route_loaded")
        ln2_loaded = sem("ln2_loaded")
        w13_loaded = [sem(f"w13_loaded{j}") for j in range(2)]
        w2_loaded = [sem(f"w2_loaded{j}") for j in range(2)]
        xg_loaded = [sem(f"xg_loaded{j}") for j in range(2)]
        ple_loaded = sem("ple_loaded")
        gate_loaded = sem("gate_loaded")
        kv_stored = sem("kv_stored")
        x1_stored = sem("x1_stored")
        y_stored = sem("y_stored")
        const_zero = sem("const_zero")
        const_ready = sem("const_ready")
        wsmask_ready = sem("wsmask_ready")
        dve_step = sem("dve_step")
        dve_last_step = sem("dve_last_step")
        table_copied = sem("table_copied")
        var_ready = sem("var_ready")
        std_ready = sem("std_ready")
        ln_done = sem("ln_done")
        xT_ps = sem("xT_ps")
        xT_ready = sem("xT_ready")
        prep_ps = sem("prep_ps")
        prep_ready = sem("prep_ready")
        w_used = [sem(f"w_used{c}") for c in range(2)]
        proj_ps = sem("proj_ps")
        proj_free = sem("proj_free")
        tok_ps = sem("tok_ps")
        tok_ready_act = sem("tok_ready_act")
        tok_ready_dve = sem("tok_ready_dve")
        gelu_u = sem("gelu_u")
        score_ps = sem("score_ps")
        score_ready = sem("score_ready")
        negmax_ready = sem("negmax_ready")
        exp_done = sem("exp_done")
        prob_ready = sem("prob_ready")
        mix_ps = sem("mix_ps")
        mix_ready = sem("mix_ready")
        sig_done = sem("sig_done")
        probT_ps = sem("probT_ps")
        probT_act = sem("probT_act")
        probT_dve = sem("probT_dve")
        oa_ps = sem("oa_ps")
        oa_ready = sem("oa_ready")
        branch_ps = sem("branch_ps")
        branch_free = sem("branch_free")
        out_ps = sem("out_ps")
        out_free = sem("out_free")
        x1T_ps = sem("x1T_ps")
        x1T_ready = sem("x1T_ready")
        logits_ps = sem("logits_ps")
        score_sig = sem("score_sig")
        shared_up = sem("shared_up")
        shared_silu = sem("shared_silu")
        shared_hid = sem("shared_hid")
        shared_ps = sem("shared_ps")
        acc_init = sem("acc_init")
        mask_ready = sem("mask_ready")
        pos_ps = sem("pos_ps")
        rounds_ready = sem("rounds_ready")
        pT_ps = sem("pT_ps")
        pT_ready = sem("pT_ready")
        onehot_ready = sem("onehot_ready")
        table_ps = sem("table_ps")
        table_ready = sem("table_ready")
        slots_ready = sem("slots_ready")
        idx_ready = sem("idx_ready")
        gathers_begun = sem("gathers_begun")
        pool_rounds = sem("pool_rounds")
        pe_rounds = sem("pe_rounds")
        xgT_ps = sem("xgT_ps")
        xgT_ready = sem("xgT_ready")
        up_done = [sem(f"up_done{j}") for j in range(2)]
        silu_done = sem("silu_done")
        hid_ready = sem("hid_ready")
        hidT_ps = sem("hidT_ps")
        hidT_ready = sem("hidT_ready")
        y_ps = sem("y_ps")
        y_high = sem("y_high")
        y_low = sem("y_low")
        scat_ready = sem("scat_ready")
        scat_ps = sem("scat_ps")
        acc_added = sem("acc_added")
        ple_ps = sem("ple_ps")
        ple_ready = sem("ple_ready")
        x2T_ps = sem("x2T_ps")
        x2T_ready = sem("x2T_ready")
        gate_ps = sem("gate_ps")
        gate_sig = sem("gate_sig")
        y_ready = sem("y_ready")

        CHUNK_STEPS = N_IN // CH // 2
        FIRST_STEPS = (S0 + JW) * P // CH // 2
        W_IN_LOADS = 16

        block = ctx.enter_context(nc.Block())

        def cols(t):
            return slice(P * t, P * t + ROWS[t])

        @block.sync
        def _(sp):
            sp.dma_start(xs[:, 0:2, :], x_prompt[0].rearrange("(a p) d -> p a d", p=P)).then_inc(x_loaded, 16)
            sp.dma_start(xs[0:ROWS[2], 2, :], x_sample[0]).then_inc(x_loaded, 16)
            w_in_v = w_in[0].rearrange("(p k) n -> p k n", k=KD)
            for c in range(2):
                sp.dma_start(wr[:, c, :, :], w_in_v[:, :, c * CH:(c + 1) * CH]).then_inc(w_loaded[c], W_IN_LOADS)
            with sp.Fori(1, CHUNK_STEPS) as i:
                for c in range(2):
                    sp.wait_ge(w_used[c], i)
                    sp.dma_start(wr[:, c, :, :], w_in_v[:, :, ds((2 * i + c) * CH, CH)])\
                        .then_inc(w_loaded[c], W_IN_LOADS)

            w1_v = exp_w1[0].rearrange("e (p k) h -> e p (k h)", k=KD)
            w3_v = exp_w3[0].rearrange("e (p k) h -> e p (k h)", k=KD)
            w2_v = exp_w2[0].rearrange("e (p k) d -> e p (k d)", k=2)

            def expert_loads(pair, first):
                for e in range(2):
                    o = (2 * pair + e) * PEXP
                    for m, wv in enumerate((w1_v, w3_v)):
                        yield (ring[:, o + m * KD * HID:o + (m + 1) * KD * HID], wv, e, w13_loaded[pair])

            def down_loads(pair):
                for e in range(2):
                    o = (2 * pair + e) * PEXP + 2 * KD * HID
                    yield (ring[:, o:o + 2 * D], w2_v, e, w2_loaded[pair])

            first = [(2 * j, x) for j in range(2) for x in expert_loads(j, 0)]
            first += [(2 * j, x) for j in range(2) for x in down_loads(j)]

            def first_expert_load():
                if first:
                    base, (dst, wv, e, s) = first.pop(0)
                    sp.dma_start(dst, wv[base + e]).then_inc(s, 16)

            wa_v = w_a[0].rearrange("(j p) n -> p j n", p=P)
            wb_v = w_b[0].rearrange("(j p) n -> p j n", p=P)
            step = CHUNK_STEPS
            for i in range(2):
                for c in range(2):
                    sp.wait_ge(w_used[c], step + i)
                    n = (2 * i + c) * CH
                    sp.dma_start(wr[:, c, 0:JW, :], wa_v[:, :, n:n + CH]).then_inc(w_loaded[c], 16)
                    sp.dma_start(wr[:, c, JW:KD, :], wb_v[:, :, n:n + CH]).then_inc(w_loaded[c], 16)
                    if i == 1:
                        if c == 0:
                            sp.wait_ge(oa_ps, 4)
                            sp.wait_ge(mix_ps, 1)
                            sp.wait_ge(kv_stored, 16 * 6)
                        first_expert_load()
            step += 2
            wo_v = w_out[0].rearrange("(j p) n -> p j n", p=P)
            for i in range(2):
                for c in range(2):
                    sp.wait_ge(w_used[c], step + i)
                    n = (2 * i + c) * CH
                    sp.dma_start(wr[:, c, :, :], wo_v[:, :, n:n + CH]).then_inc(w_loaded[c], 16)
                    first_expert_load()
            step += 2
            sp.wait_ge(branch_free, 4 + KD)
            sp.dma_start(lnvec[:, 0, :], ln1_g[0].partition_broadcast(P)).then_inc(route_loaded, 16)
            sp.dma_start(lnvec[:, 1, :], ln1_b[0].partition_broadcast(P)).then_inc(route_loaded, 16)
            sp.dma_start(rw[:, :, :], router_w[0].rearrange("(p k) e -> p k e", k=KD)).then_inc(route_loaded, 16)
            sp.dma_start(rbias[:, :], router_bias[0].partition_broadcast(P)).then_inc(route_loaded, 16)
            for c, w in enumerate((sh_w1, sh_w3)):
                sp.wait_ge(w_used[c], step)
                sp.dma_start(wr[:, c, :, :], w[0].rearrange("(p k) h -> p k h", k=KD)).then_inc(w_loaded[c], 16)
                first_expert_load()
            step += 1
            sp.wait_ge(w_used[0], step)
            sp.dma_start(sw2, sh_w2[0].rearrange("(j p) d -> p j d", p=P)).then_inc(w_loaded[0], 16)
            sp.wait_ge(w_used[1], step)
            sp.dma_start(proj_w, ple_proj[0].rearrange("(j p) d -> p j d", p=P)).then_inc(ple_loaded, 16)
            while first:
                first_expert_load()
            sp.wait_ge(w_used[0], step + 1)
            sp.dma_start(p_tok[:, 0:2, :], p_prompt[0, 0].rearrange("(a p) d -> p a d", p=P)).then_inc(ple_loaded, 16)
            sp.dma_start(p_tok[0:ROWS[2], 2, :], p_sample[0, 0]).then_inc(ple_loaded, 16)

            def expert_step(n, expert):
                for j in range(2):
                    sp.wait_ge(up_done[j], n)
                    for dst, wv, e, s in expert_loads(j, 0):
                        sp.dma_start(dst, wv[ds(expert + 2 * j + e, 1)].rearrange("o p n -> (o p) n")).then_inc(s, 16)
                for j in range(2):
                    sp.wait_ge(y_ps, 4 * n - 2 + 2 * j)
                    for dst, wv, e, s in down_loads(j):
                        sp.dma_start(dst, wv[ds(expert + 2 * j + e, 1)].rearrange("o p n -> (o p) n")).then_inc(s, 16)

            with sp.Fori(1, STEPS) as i:
                expert_step(i, 4 * i)
            sp.wait_ge(rounds_ready, 1)
            rounds = sp.value_load(rounds_i[0:1, 0:1], min_val=1, max_val=MAX_ROUNDS)
            with sp.If(rounds > 1):
                with sp.Fori(1, rounds) as r:
                    with sp.Fori(0, STEPS) as i:
                        expert_step(r * STEPS + i, 4 * i)
            sp.wait_ge(up_done[0], rounds * STEPS)
            gw_v = ple_gate[0].rearrange("(p k) n -> p k n", k=KD)
            for e in range(2):
                sp.dma_start(gate_w[e], gw_v[:, 4 * e:4 * e + 4, :]).then_inc(gate_loaded, 16)
            for t in range(3):
                sp.wait_ge(y_ready, t + 1)
                out = y_prompt[0, P * t:P * (t + 1), :] if t < 2 else y_sample[0]
                sp.dma_start(out, sgate[0:ROWS[t], t, :]).then_inc(y_stored, 16)
            sp.wait_ge(y_stored, 16 * 3)

        @block.gpsimd
        def _(pool):
            pool.memset(ident[:, :], 0.0).then_inc(const_zero, 1)
            pool.memset(tri[:, :], 1.0).then_inc(const_zero, 1)
            pool.memset(onesb[:, :], 1.0)
            pool.memset(ones[:, :], 1.0)
            pool.wait_ge(const_zero, 2)
            pool.affine_select(out=ident[:, :], in_=ident[:, :], compare_op=ALU.not_equal, fill=1.0, base=0,
                               pattern=[[-1, P]], channel_multiplier=1)
            pool.affine_select(out=tri[:, :], in_=tri[:, :], compare_op=ALU.is_gt, fill=0.0, base=0,
                               pattern=[[1, P]], channel_multiplier=-1)
            pool.iota(round_thr[:, :], pattern=[[SLOTS, MAX_ROUNDS - 1]], base=SLOTS, channel_multiplier=0,
                      allow_small_or_imprecise_dtypes=True).then_inc(const_ready, 1)
            pool.wait_ge(ws_loaded, 16)
            pool.affine_select(out=ws, in_=ws, compare_op=ALU.is_ge, fill=0.0, base=0,
                               pattern=[[0, 8], [-1, P]], channel_multiplier=1).then_inc(wsmask_ready, 1)
            pool.wait_ge(tok_ready_act, 3)
            pool.dma_start(new_k_prompt[0, 0].rearrange("(a p) h d -> p a (h d)", p=P), k_tok[:, 0:2, :]).then_inc(kv_stored, 16)
            pool.dma_start(new_k_sample[0, 0].rearrange("p h d -> p (h d)"), k_tok[0:ROWS[2], 2, :]).then_inc(kv_stored, 16)
            pool.wait_ge(tok_ready_dve, 3)
            pool.dma_start(new_v_prompt[0, 0].rearrange("(a p) h d -> p a (h d)", p=P), v_tok[:, 0:2, :]).then_inc(kv_stored, 16)
            pool.dma_start(new_v_sample[0, 0].rearrange("p h d -> p (h d)"), v_tok[0:ROWS[2], 2, :]).then_inc(kv_stored, 16)
            pool.wait_ge(ln_done, 6)
            pool.dma_start(new_mlp_prompt[0, 0], vn[:, 1, :]).then_inc(kv_stored, 16)
            pool.dma_start(new_mlp_sample[0, 0], vn[0:ROWS[2], 2, :]).then_inc(kv_stored, 16)
            pool.wait_ge(branch_free, 4 + KD)
            pool.iota(iota_slot, pattern=[[1, SLOTS]], base=0, channel_multiplier=0, allow_small_or_imprecise_dtypes=True)
            pool.iota(iota_tok, pattern=[[1, TP]], base=0, channel_multiplier=0, allow_small_or_imprecise_dtypes=True)
            for t in range(3):
                pool.iota(attrs[:, t, :, 3], pattern=[[0, NE]], base=0, channel_multiplier=1, allow_small_or_imprecise_dtypes=True)
                last = pool.memset(attrs[:, t, :, 4], float(P * t))
            last.then_inc(const_ready, 1)
            for t in range(3):
                pool.wait_ge(ln_done, 7 + t)
                pool.dma_start(x1_rows.ap()[P * t:P * t + ROWS[t], :], xs[0:ROWS[t], t, :]).then_inc(x1_stored, 16)
            pool.dma_start(lnvec[:, 0, :], ln2_g[0].partition_broadcast(P)).then_inc(ln2_loaded, 16)
            pool.dma_start(lnvec[:, 1, :], ln2_b[0].partition_broadcast(P)).then_inc(ln2_loaded, 16)
            pool.wait_ge(x1_stored, 16 * 3)
            pool.wait_ge(rounds_ready, 1)
            rounds = pool.value_load(rounds_i[0:1, 0:1], min_val=1, max_val=MAX_ROUNDS)
            with pool.Fori(0, rounds) as r:
                pool.wait_ge(slots_ready, r + 1)
                pool.sem_inc(pool_rounds, 1)
                with pool.Fori(0, STEPS) as i:
                    n = r * STEPS + i
                    for j in range(2):
                        pool.wait_ge(xgT_ps, 2 * n + j + 1)
                        pool.tensor_copy(idx_now[:, j:j + 1], slot_idx[:, ds(2 * i + j, 1)]).then_inc(idx_ready, 1)
                        pool.wait_ge(idx_ready, 2 * n + j + 1)
                        pool.sem_inc(gathers_begun, 1)
                        pool.indirect_dma_start(
                            out=xg[:, j, :], out_offset=None, in_=x1_rows.ap(),
                            in_offset=bass.IndirectOffsetOnAxis(ap=idx_now[:, j:j + 1], axis=0),
                        ).then_inc(xg_loaded[j], 16)

        @block.scalar
        def _(act):
            for i, v in enumerate((ln_in_g, ln_in_b)):
                act.dma_start(lninvec[:, i, :], v.partition_broadcast(P)).then_inc(lnin_loaded, 16)
            act.dma_start(ck, cache_k[0, 0].rearrange("(a p) h d -> p a (h d)", p=P)).then_inc(cache_loaded, 16)
            act.dma_start(ws, mlp_w_s[0].rearrange("g t s -> t g s")).then_inc(ws_loaded, 16)
            act.dma_start(relpad[:, PAD:PAD + REL], rel_bias[0]).then_inc(rel_loaded, 16)
            act.dma_start(cv, cache_v[0, 0].rearrange("(a p) h d -> p a (h d)", p=P)).then_inc(cache_loaded, 16)
            for i, v in enumerate((mlp_g, mlp_b)):
                act.dma_start(mlpvec[:, i, :], v[0].partition_broadcast(P)).then_inc(mlpvec_loaded, 16)
            act.dma_start(bsrow, mlp_b_s[0:1]).then_inc(bs_loaded, 16)

            def norm_std(n):
                act.wait_ge(var_ready, n)
                nc.scalar.activation(std[:, :], vareps[:, :], ACT.Sqrt).then_inc(std_ready, 1)

            norm_std(1)
            act.wait_ge(rel_loaded, 16)
            nc.scalar.activation(relpad[:, 0:PAD], relpad[:, PAD:PAD + 1].to_broadcast([HEADS, PAD]), ACT.Copy)\
                .then_inc(rel_stored, 1)
            act.wait_ge(rel_stored, 1)
            act.dma_start(rel_dram.ap(), relpad.unsqueeze(1).to_broadcast([HEADS, P, RW])).then_inc(rel_stored, 16)
            act.wait_ge(rel_stored, 17)

            def toeplitz(dst, rows, par, keys, first):
                src = bass.AP(tensor=rel_dram, offset=par * P * RW + first,
                              ap=[[RW - 1, rows], [2 * P * RW, 4], [1, keys]])
                act.dma_start(dst, src).then_inc(bias_loaded, 16)

            for par in range(2):
                toeplitz(prob1[:, 4 * par:4 * par + 4, :], P, par, 256, PAD + 256 - P)
                toeplitz(prob0[:, 4 * par:4 * par + 4, :], P, par, P, PAD + 256)
                toeplitz(probs[:, 4 * par:4 * par + 4, :], DH, par, TOK, PAD)

            def evacuate_xT(ps_sem, first, ready, bank):
                for t in range(3):
                    act.wait_ge(ps_sem, first + t + 1)
                    b = bank(t)
                    src = PS[:, b:b + 2, :].rearrange("p b (k s) -> p (b k) s", k=4)[:, :, 0:ROWS[t]]
                    nc.scalar.activation(xT[:, :, cols(t)], src, ACT.Copy).then_inc(ready, 1)

            evacuate_xT(xT_ps, 0, xT_ready, lambda t: 2 * (t % 2))

            def evacuate_projection(steps, base):
                with act.Fori(0, steps) as i:
                    for b in range(4):
                        act.wait_ge(proj_ps, base + 4 * i + b + 1)
                        nc.scalar.activation(zt[:, ds(base + 4 * i + b, 1), :].rearrange("p o t -> p (o t)"),
                                             PS[:, b, 0:TOK], ACT.Copy).then_inc(proj_free, 1)

            evacuate_projection(FIRST_STEPS, 0)
            for t in range(3):
                act.wait_ge(tok_ps, t + 1)
                nc.scalar.activation(k_tok[0:ROWS[t], t, :], PS[0:ROWS[t], 4 + t, :], ACT.Copy).then_inc(tok_ready_act, 1)
            for t in range(3):
                act.wait_ge(tok_ps, 7 + t)
                nc.scalar.activation(vn[0:ROWS[t], t, :], PS[0:ROWS[t], (6, 7, 4)[t], :], ACT.Gelu_apprx_tanh)\
                    .then_inc(tok_ready_act, 1)
            act.wait_ge(proj_free, 4 + FIRST_STEPS * 4)
            nc.scalar.activation(obT, obT, ACT.Gelu_apprx_tanh).then_inc(gelu_u, 1)
            group = ((prob1, P), (prob0, P), (probs, DH))
            for i in range(4 * (CHUNK_STEPS - FIRST_STEPS)):
                tile = 4 * FIRST_STEPS + i
                act.wait_ge(proj_ps, tile + 1)
                nc.scalar.activation(zt[:, tile, :], PS[:, i % 4, 0:TOK], ACT.Copy).then_inc(proj_free, 1)
                if i // 4 < 3:
                    t = i // 4
                    pr, n = group[t]
                    if i % 4 == 0:
                        act.wait_ge(negmax_ready, t + 1)
                    for h in (2 * (i % 4), 2 * (i % 4) + 1):
                        last = nc.scalar.activation(pr[:, h, :], pr[:, h, :], ACT.Exp, bias=snegmax[0:n, t, h:h + 1],
                                                    accum_out=ssum[0:n, t, h:h + 1])
                    if i % 4 == 3:
                        last.then_inc(exp_done, 1)
                if i == 11:
                    norm_std(2)
            act.wait_ge(proj_free, 4 + CHUNK_STEPS * 4)
            nc.scalar.activation(zt[:, GA0:FT, :], zt[:, GA0:FT, :], ACT.Sigmoid).then_inc(sig_done, 1)
            for j in range(4):
                act.wait_ge(probT_ps, j + 1)
                b = 4 if j % 2 == 0 else 0
                nc.scalar.activation(probT[:, j, 0:2, :], PS[:, b:b + 2, 0:384], ACT.Copy).then_inc(probT_act, 1)
            norm_std(3)
            evacuate_xT(x1T_ps, 0, x1T_ready, lambda t: 2 * t)
            for t in range(3):
                act.wait_ge(logits_ps, 3)
                nc.scalar.activation(score[0:ROWS[t], t, :], PS[0:ROWS[t], 6, NE * t:NE * (t + 1)], ACT.Sigmoid)\
                    .then_inc(score_sig, 1)
            for m in range(2):
                act.wait_ge(shared_up, m + 1)
                nc.scalar.activation(hsT[:, m, :], PS[:, m, 0:TOK], ACT.Silu).then_inc(shared_silu, 1)
            act.wait_ge(pT_ps, 1)
            nc.scalar.activation(pT, PS[:, 0:2, 0:TOK], ACT.Copy).then_inc(pT_ready, 1)
            nc.scalar.preload_act_table(ACT.Silu)
            act.wait_ge(rounds_ready, 1)
            rounds = act.value_load(rounds_i[0:1, 0:1], min_val=1, max_val=MAX_ROUNDS)
            with act.Fori(0, rounds) as r:
                with act.Fori(0, STEPS) as i:
                    n = r * STEPS + i

                    def rows_T(j):
                        act.wait_ge(xgT_ps, 2 * n + j + 3)
                        nc.scalar.activation(xgT[:, j, :, :].rearrange("p k s -> p (k s)"),
                                             PS[:, 0:2, :].rearrange("p b s -> p (b s)"), ACT.Copy).then_inc(xgT_ready, 1)

                    def silu(j):
                        act.wait_ge(up_done[j], n + 1)
                        nc.scalar.activation(act_h[:, j, :], PS[:, 2 + j, 0:HID], ACT.Silu).then_inc(silu_done, 1)

                    def hidden_T(j):
                        act.wait_ge(hidT_ps, 2 * n + j + 1)
                        nc.scalar.activation(hidT[:, j, :, :].rearrange("p k s -> p (k s)"),
                                             PS[:, 4, HID * j:HID * (j + 1)], ACT.Copy).then_inc(hidT_ready, 1)

                    def high(j, half):
                        act.wait_ge(y_ps, 4 * n + 2 * j + half + 1)
                        nc.scalar.activation(ysplit[:, j, 0, 512 * half:512 * half + 512], PS[:, 5 + half, :], ACT.Copy)\
                            .then_inc(y_high, 1)

                    rows_T(0)
                    rows_T(1)
                    silu(0)
                    hidden_T(0)
                    silu(1)
                    high(0, 0)
                    hidden_T(1)
                    high(0, 1)
                    high(1, 0)
                    high(1, 1)
            for t in range(3):
                act.wait_ge(ple_ps, t + 1)
                nc.scalar.activation(ple[0:ROWS[t], t, :], PS[0:ROWS[t], 2 + 2 * t:4 + 2 * t, :].rearrange("p b s -> p (b s)"),
                                     ACT.Copy).then_inc(ple_ready, 1)
            norm_std(4)
            evacuate_xT(x2T_ps, 0, x2T_ready, lambda t: 2 * t)
            for t in range(3):
                act.wait_ge(gate_ps, t + 1)
                b = (6, 0, 2)[t]
                nc.scalar.activation(sgate[0:ROWS[t], t, :], PS[0:ROWS[t], b:b + 2, :].rearrange("p b s -> p (b s)"),
                                     ACT.Sigmoid).then_inc(gate_sig, 1)

        @block.vector
        def _(dve):
            steps = {dve_step: 0, dve_last_step: 0}
            own = [dve_step]

            def step(ins):
                ins.then_inc(own[0], 1)
                steps[own[0]] += 1
                return steps[own[0]]

            def after(n):
                dve.wait_ge(own[0], n)

            def norm(x, width, vec, loaded, n):
                halves = width // 512
                for t in range(3):
                    for h in range(halves):
                        ins = nc.vector.bn_stats(stats[0:ROWS[t], t, h, :], x[0:ROWS[t], t, 512 * h:512 * h + 512])
                    done = step(ins)
                after(done)
                for t in range(3):
                    done = step(nc.vector.bn_aggr(meanvar[0:ROWS[t], t, :], stats[0:ROWS[t], t, 0:halves, :].rearrange("p a b -> p (a b)")))
                after(done)
                nc.vector.tensor_scalar(vareps[:, :], meanvar[:, :, 1], EPS, None, ALU.add).then_inc(var_ready, 1)
                dve.wait_ge(std_ready, n)
                after(step(nc.vector.reciprocal(rstd[:, :], std[:, :])))
                dve.wait_ge(*loaded)
                a = [step(nc.vector.tensor_scalar(x[0:ROWS[t], t, :], x[0:ROWS[t], t, :], meanvar[0:ROWS[t], t, 0:1],
                                                  rstd[0:ROWS[t], t:t + 1], ALU.subtract, ALU.mult)) for t in range(3)]
                b = []
                for t in range(3):
                    after(a[t])
                    b.append(step(nc.vector.tensor_tensor(x[0:ROWS[t], t, :], x[0:ROWS[t], t, :], vec[0:ROWS[t], 0, :], ALU.mult)))
                for t in range(3):
                    after(b[t])
                    nc.vector.tensor_tensor(x[0:ROWS[t], t, :], x[0:ROWS[t], t, :], vec[0:ROWS[t], 1, :], ALU.add)\
                        .then_inc(ln_done, 1)

            after(step(nc.vector.memset(meanvar[:, :, :], 1.0)))
            dve.wait_ge(x_loaded, 32)
            norm(xs, D, lninvec, (lnin_loaded, 32), 1)

            for c in range(2):
                dve.wait_ge(prep_ps, c + 1)
                nc.vector.tensor_copy(ckT[:, :, P * c:P * (c + 1)], PS[:, 4 + c, :].rearrange("p (j s) -> p j s", j=4))\
                    .then_inc(prep_ready, 1)
            dve.wait_ge(prep_ps, 3)
            nc.vector.tensor_copy(wsT.rearrange("p g s -> p (g s)"), PS[:, 6:8, :].rearrange("p b s -> p (b s)"))\
                .then_inc(prep_ready, 1)
            dve.wait_ge(bias_loaded, 16 * 6)
            nc.vector.memset(prob1[0:64, :, 192:256], MASKED)
            masked = step(nc.vector.memset(prob0[0:64, :, 64:P], MASKED))
            after(masked)

            def scores(pr, ps, t):
                nc.vector.scalar_tensor_tensor(out=pr, in0=ps, scalar=SCALE, in1=pr, op0=ALU.mult, op1=ALU.add)\
                    .then_inc(score_ready, 1)

            dve.wait_ge(score_ps, 1)
            scores(prob1, PS[:, 0:4, :].rearrange("p b (i k) -> p (b i) k", i=2), 0)
            for t in range(3):
                dve.wait_ge(tok_ps, 4 + t)
                nc.vector.tensor_copy(v_tok[0:ROWS[t], t, :], PS[0:ROWS[t], (7, 4, 5)[t], :]).then_inc(tok_ready_dve, 1)
            dve.wait_ge(score_ps, 2)
            scores(prob0, PS[:, 0:2, :].rearrange("p b (i k) -> p (b i) k", i=4), 1)
            for w in range(2):
                dve.wait_ge(score_ps, 3 + w)
                for par in range(2):
                    nc.vector.scalar_tensor_tensor(
                        out=probs[:, 4 * par + 2 * w:4 * par + 2 * w + 2, :], in0=PS[0:DH, 4 + 2 * par:6 + 2 * par, 0:TOK],
                        scalar=SCALE, in1=probs[:, 4 * par + 2 * w:4 * par + 2 * w + 2, :], op0=ALU.mult, op1=ALU.add)\
                        .then_inc(score_ready, 1)
            dve.wait_ge(score_ready, 6)
            group = ((prob1, P), (prob0, P), (probs, DH))
            for t, (pr, n) in enumerate(group):
                m = step(nc.vector.tensor_reduce(smax[0:n, t, :], pr, AX.X, ALU.max))
                after(m)
                nc.vector.tensor_scalar(snegmax[0:n, t, :], smax[0:n, t, :], -1.0, None, ALU.mult).then_inc(negmax_ready, 1)
            dve.wait_ge(tok_ready_act, 6)
            norm(vn, AW, mlpvec, (mlpvec_loaded, 32), 2)
            for t, (pr, n) in enumerate(group):
                dve.wait_ge(exp_done, t + 1)
                after(step(nc.vector.reciprocal(srec[0:n, t, :], ssum[0:n, t, :])))
                nc.vector.tensor_tensor(pr, pr, srec[0:n, t, :].unsqueeze(2).to_broadcast([n, HEADS, pr.shape[2]]), ALU.mult)\
                    .then_inc(prob_ready, 1)
            dve.wait_ge(mix_ps, 1)
            dve.wait_ge(gelu_u, 1)
            nc.vector.tensor_tensor(obT, PS[:, 0:4, 0:TOK], obT, ALU.mult).then_inc(mix_ready, 1)

            def sample_probT(j):
                dve.wait_ge(probT_ps, j + 1)
                b = 6 if j % 2 == 0 else 2
                ps = PS[:, b, 0:384].rearrange("p (e k) -> p e k", e=2)
                dst = probT[:, j, 2, :].rearrange("p (e k) -> p e k", e=2)
                nc.vector.tensor_copy(dst[:, :, 0:128], ps[:, :, 0:128])
                nc.vector.tensor_copy(dst[0:DH, :, 128:192], ps[0:DH, :, 128:192]).then_inc(probT_dve, 1)

            def attention_out(j):
                dve.wait_ge(oa_ps, j + 1)
                nc.vector.tensor_copy(oaT[:, j, :], PS[:, 7 if j % 2 == 0 else 3, 0:TOK]).then_inc(oa_ready, 1)

            sample_probT(0)
            sample_probT(1)
            for j in range(4):
                attention_out(j)
                if j < 2:
                    sample_probT(j + 2)
            dve.wait_ge(sig_done, 1)
            base = steps[dve_step]
            with dve.Fori(0, 2) as i:
                for b in range(4):
                    tile = 4 * i + b
                    ga = zt[:, ds(GA0 + tile, 1), :].rearrange("p o t -> p (o t)")
                    gb = zt[:, ds(GB0 + tile, 1), :].rearrange("p o t -> p (o t)")
                    m = mT[:, ds(tile, 1), :].rearrange("p o t -> p (o t)")
                    dve.wait_ge(branch_ps, tile + 1)
                    nc.vector.tensor_tensor(ga, PS[:, 2 * b, 0:TOK], ga, ALU.mult)
                    nc.vector.tensor_tensor(gb, PS[:, 2 * b + 1, 0:TOK], gb, ALU.mult).then_inc(dve_step, 1)
                    dve.wait_ge(dve_step, base + tile + 1)
                    nc.vector.tensor_tensor(m, ga, gb, ALU.add).then_inc(branch_free, 1)
            steps[dve_step] = base + KD
            with dve.Fori(0, 2) as i:
                for c in range(2):
                    for t in range(3):
                        dve.wait_ge(out_ps, 6 * i + 3 * c + t + 1)
                        x = xs[0:ROWS[t], t, ds((2 * i + c) * CH, CH)]
                        nc.vector.scalar_tensor_tensor(out=x, in0=x, scalar=ALPHA, in1=PS[0:ROWS[t], 4 * c + t, 0:CH],
                                                       op0=ALU.mult, op1=ALU.add).then_inc(out_free, 1)
            dve.wait_ge(out_free, 6 + 12)
            norm(xs, D, lnvec, (route_loaded, 64), 3)

            def stage(f):
                done = [step(f(t, ROWS[t])) for t in range(3)]
                after(done[-1])

            gm = lambda t, n: gmax[0:n, t, :]
            stage(lambda t, n: nc.vector.memset(pos[:, t, :], -1.0))
            stage(lambda t, n: nc.vector.memset(attrs[:, t, :, 0:3], 0.0))
            stage(lambda t, n: nc.vector.memset(rsmall[:, t, :], MASKED))
            for t in range(3):
                dve.wait_ge(score_sig, t + 1)
                m = step(nc.vector.tensor_tensor(sel[0:ROWS[t], t, :], score[0:ROWS[t], t, :], rbias[0:ROWS[t], :], ALU.add))
            after(m)
            for t in range(3):
                for g in range(GROUPS):
                    last = nc.vector.max(out=gmax[0:ROWS[t], t, 8 * g:8 * g + 8],
                                         in_=sel[0:ROWS[t], t, PER_GROUP * g:PER_GROUP * (g + 1)])
                m = step(last)
            after(m)
            stage(lambda t, n: nc.vector.tensor_tensor(rsmall[0:n, t, 0:8], gmax[0:n, t, 0:64:8], gmax[0:n, t, 1:64:8], ALU.add))
            stage(lambda t, n: nc.vector.max(out=rsmall[0:n, t, 16:24], in_=rsmall[0:n, t, 0:8]))
            stage(lambda t, n: nc.vector.memset(rsmall[0:n, t, 16 + KEEP_GROUPS:24], MASKED))
            stage(lambda t, n: nc.vector.match_replace(out=rsmall[0:n, t, 32:44], in_to_replace=rsmall[0:n, t, 16:24],
                                                       in_values=rsmall[0:n, t, 0:12], imm_value=2 * MASKED))
            stage(lambda t, n: nc.vector.tensor_scalar(rsmall[0:n, t, 48:56], rsmall[0:n, t, 32:40], 1.5 * MASKED, MASKED,
                                                       ALU.is_ge, ALU.mult))
            stage(lambda t, n: nc.vector.tensor_tensor(
                msel[0:n, t, :].rearrange("p (g i) -> p g i", g=GROUPS), sel[0:n, t, :].rearrange("p (g i) -> p g i", g=GROUPS),
                rsmall[0:n, t, 48:56].unsqueeze(2).to_broadcast([n, GROUPS, PER_GROUP]), ALU.add))
            stage(lambda t, n: nc.vector.max(out=rsmall[0:n, t, 16:24], in_=msel[0:n, t, :]))
            stage(lambda t, n: nc.vector.match_replace(out=replaced[0:n, t, :], in_to_replace=rsmall[0:n, t, 16:24],
                                                       in_values=msel[0:n, t, :], imm_value=3 * MASKED))
            stage(lambda t, n: nc.vector.tensor_scalar(maskf[0:n, t, :], replaced[0:n, t, :], 2 * MASKED, None, ALU.is_lt))
            for t in range(3):
                nc.vector.tensor_copy(mask[0:ROWS[t], t, :], maskf[0:ROWS[t], t, :]).then_inc(mask_ready, 1)
            stage(lambda t, n: nc.vector.tensor_tensor(wt[0:n, t, :], maskf[0:n, t, :], score[0:n, t, :], ALU.mult))
            stage(lambda t, n: nc.vector.tensor_reduce(rsmall[0:n, t, 60:61], wt[0:n, t, :], AX.X, ALU.add))
            stage(lambda t, n: nc.vector.reciprocal(rsmall[0:n, t, 61:62], rsmall[0:n, t, 60:61]))
            stage(lambda t, n: nc.vector.tensor_scalar(wt[0:n, t, :], wt[0:n, t, :], rsmall[0:n, t, 61:62], ROUTED_SCALE,
                                                       ALU.mult, ALU.mult))
            for i in range(3):
                stage(lambda t, n: nc.vector.tensor_copy(attrs[0:n, t, :, i], wt[0:n, t, :]))
                if i < 2:
                    stage(lambda t, n: nc.vector.tensor_tensor(wt[0:n, t, :], wt[0:n, t, :], attrs[0:n, t, :, i], ALU.subtract))
            for m in range(2):
                dve.wait_ge(shared_silu, m + 1)
                dve.wait_ge(shared_up, m + 3)
                nc.vector.tensor_tensor(hsT[:, m, :], hsT[:, m, :], PS[:, 2 + m, 0:TOK], ALU.mult).then_inc(shared_hid, 1)
            dve.wait_ge(pos_ps, 1)
            stage(lambda t, n: nc.vector.scalar_tensor_tensor(out=wres[0:n, t, :], in0=PS[0:n, 7, NE * t:NE * (t + 1)], scalar=1.0,
                                                              in1=maskf[0:n, t, :], op0=ALU.add, op1=ALU.mult))
            stage(lambda t, n: nc.vector.tensor_scalar(pos[0:n, t, :], wres[0:n, t, :], -1.0, None, ALU.add))
            after(step(nc.vector.tensor_reduce(rounds_f[:, 0:1], PS[0:1, 7, 3 * NE:4 * NE], AX.X, ALU.max)))
            dve.wait_ge(const_ready, 2)
            after(step(nc.vector.tensor_scalar(round_gt[:, :], round_thr[:, :], rounds_f[:, 0:1], None, ALU.is_lt)))
            after(step(nc.vector.tensor_reduce(rounds_f[:, 1:2], round_gt[:, :], AX.X, ALU.add)))
            nc.vector.tensor_scalar(rounds_i[:, :], rounds_f[:, 1:2], 1.0, None, ALU.add).then_inc(rounds_ready, 1)
            dve.wait_ge(x1_stored, 16 * 3)
            for t in range(3):
                dve.wait_ge(shared_ps, t + 1)
                x = acc[0:ROWS[t], t, :]
                nc.vector.scalar_tensor_tensor(out=x, in0=x, scalar=ALPHA, in1=PS[0:ROWS[t], 2 * t:2 * t + 2, :].rearrange("p b s -> p (b s)"),
                                               op0=ALU.mult, op1=ALU.add).then_inc(acc_init, 1)
            dve.wait_ge(acc_init, 3)
            dve.wait_ge(rounds_ready, 1)
            rounds = dve.value_load(rounds_i[0:1, 0:1], min_val=1, max_val=MAX_ROUNDS)
            with dve.Fori(0, rounds) as r:
                dve.wait_ge(acc_added, r * (12 * STEPS) + 1)
                for t in range(3):
                    nc.vector.tensor_tensor(
                        onehot[:, t, :, :], iota_slot.unsqueeze(1).to_broadcast([P, NE, SLOTS]),
                        pos[:, t, :].unsqueeze(2).to_broadcast([P, NE, SLOTS]), ALU.is_equal).then_inc(onehot_ready, 1)
                dve.wait_ge(onehot_ready, 3 * r + 3)
                nc.vector.tensor_scalar(pos[:, :, :], pos[:, :, :], -float(SLOTS), None, ALU.add)
                dve.wait_ge(table_ps, r + 1)
                nc.vector.tensor_copy(table.rearrange("p i f -> p (i f)"), PS[:, 6, 0:PAIRS * 10]).then_inc(table_copied, 1)
                dve.wait_ge(table_copied, r + 1)
                for e in range(2):
                    h = slice(64 * e, 64 * e + 64)
                    nc.vector.tensor_reduce(slot_w[h, :], table[h, :, 5 * e:5 * e + 3], AX.X, ALU.add)
                    nc.vector.tensor_tensor(slot_idx[h, :], table[h, :, 5 * e + 3], table[h, :, 5 * e + 4], ALU.add)
                    last = nc.vector.tensor_tensor(slot_tok[h, :], table[h, :, 5 * e + 3], table[h, :, 5 * e + 4], ALU.add)
                last.then_inc(slots_ready, 1)
                with dve.Fori(0, STEPS) as i:
                    n = r * STEPS + i
                    dve.wait_ge(slots_ready, r + 1)
                    dve.wait_ge(acc_added, 12 * n + 1)
                    for j in range(2):
                        nc.vector.tensor_scalar(scat[:, j, :], iota_tok, slot_tok[:, ds(2 * i + j, 1)], None, ALU.is_equal)\
                            .then_inc(scat_ready, 1)
                    for j in range(2):
                        dve.wait_ge(silu_done, 2 * n + j + 1)
                        nc.vector.scalar_tensor_tensor(out=hid[:, j, :], in0=PS[:, 2 + j, HID:2 * HID],
                                                       scalar=slot_w[:, ds(2 * i + j, 1)], in1=act_h[:, j, :],
                                                       op0=ALU.mult, op1=ALU.mult).then_inc(hid_ready, 1)
                    for j in range(2):
                        for half in range(2):
                            dve.wait_ge(y_high, 4 * n + 2 * j + half + 1)
                            c = slice(512 * half, 512 * half + 512)
                            nc.vector.tensor_tensor(ysplit[:, j, 1, c], PS[:, 5 + half, :], ysplit[:, j, 0, c].bitcast(F32),
                                                    ALU.subtract).then_inc(y_low, 1)
                    for q in range(12):
                        t, half = q % 6 // 2, q % 2
                        dve.wait_ge(scat_ps, 12 * n + q + 1)
                        if q >= 6:
                            dve.wait_ge(acc_added, 12 * n + q - 4)
                        a = acc[0:ROWS[t], t, 512 * half:512 * half + 512]
                        nc.vector.tensor_tensor(a, a, PS[0:ROWS[t], (7, 0, 1)[q % 3], :], ALU.add).then_inc(acc_added, 1)
            dve.wait_ge(acc_added, rounds * (12 * STEPS) + 1)
            own[0] = dve_last_step
            norm(xs, D, lnvec, (ln2_loaded, 32), 4)
            dve.wait_ge(ple_ready, 3)
            for t in range(3):
                dve.wait_ge(gate_sig, t + 1)
                s = sgate[0:ROWS[t], t, :]
                after(step(nc.vector.tensor_tensor(s, s, ple[0:ROWS[t], t, :], ALU.mult)))
                nc.vector.tensor_tensor(s, s, xs[0:ROWS[t], t, :], ALU.add).then_inc(y_ready, 1)

        @block.tensor
        def _(pe):
            def transpose_rows(src, t, bank, signal):
                for k in range(KD):
                    ins = pe.transpose(PS[:, bank + k // 4, P * (k % 4):P * (k % 4) + ROWS[t]],
                                       src[0:ROWS[t], t, k::KD], ident[0:ROWS[t], 0:ROWS[t]])
                ins.then_inc(signal, 1)

            pe.wait_ge(const_ready, 1)
            for t in range(3):
                pe.wait_ge(ln_done, t + 1)
                if t == 2:
                    pe.wait_ge(xT_ready, 1)
                transpose_rows(xs, t, 2 * (t % 2), xT_ps)
            pe.wait_ge(cache_loaded, 32)
            for c in range(2):
                for j in range(JW):
                    ins = pe.transpose(PS[:, 4 + c, P * j:P * (j + 1)], ck[:, c, P * j:P * (j + 1)], ident[:, :])
                ins.then_inc(prep_ps, 1)
            pe.wait_ge(wsmask_ready, 1)
            for g in range(8):
                ins = pe.transpose(PS[:, 6 + g // 4, P * (g % 4):P * (g % 4 + 1)], ws[:, g, :], ident[:, :])
            ins.then_inc(prep_ps, 1)
            pe.wait_ge(xT_ready, 3)
            pe.sem_inc(proj_free, 4)

            def project(first, end):
                with pe.Fori(first, end) as i:
                    for c in range(2):
                        pe.wait_ge(w_loaded[c], W_IN_LOADS * (i + 1))
                        for m in range(2):
                            b = 2 * c + m
                            pe.wait_ge(proj_free, 4 * i + b + 1)
                            for k in range(KD):
                                ins = pe.matmul(PS[:, b, 0:TOK], wr[:, c, k, P * m:P * (m + 1)], xT[:, k, :],
                                                start=(k == 0), stop=(k == KD - 1))
                            ins.then_inc(proj_ps, 1)
                        pe.wait_ge(proj_ps, 4 * i + 2 * c + 2)
                        pe.sem_inc(w_used[c], 1)

            def rows_of(first, t, bank):
                for j in range(JW):
                    ins = pe.transpose(PS[0:ROWS[t], bank, P * j:P * (j + 1)], zt[:, first + j, cols(t)], ident[:, :])
                ins.then_inc(tok_ps, 1)

            def head(tile, h, c):
                return zt[64 * (h % 2):64 * (h % 2) + 64, tile + h // 2, c]

            project(0, FIRST_STEPS)
            pe.wait_ge(proj_free, 4 + 4 * FIRST_STEPS)
            pe.wait_ge(prep_ready, 3)
            for t in range(3):
                rows_of(K0, t, 4 + t)
            for h in range(HEADS):
                par, i = h % 2, h // 2
                ins = pe.matmul(PS[:, 2 * par + i // 2, 256 * (i % 2):256 * (i % 2) + 256],
                                head(Q0, h, slice(P, 2 * P)), head(K0, h, slice(0, 2 * P)), start=True, stop=True)
            ins.then_inc(score_ps, 1)
            for t in range(3):
                if t:
                    pe.wait_ge(tok_ready_act, t)
                rows_of(V0, t, (7, 4, 5)[t])
            for t in range(3):
                if t < 2:
                    pe.wait_ge(*((tok_ready_act, 3), (tok_ready_dve, 1))[t])
                else:
                    pe.wait_ge(tok_ready_dve, 2)
                rows_of(S0, t, (6, 7, 4)[t])
            pe.wait_ge(score_ready, 1)
            for h in range(HEADS):
                ins = pe.matmul(PS[:, h % 2, P * (h // 2):P * (h // 2 + 1)],
                                head(Q0, h, slice(0, P)), head(K0, h, slice(0, P)), start=True, stop=True)
            ins.then_inc(score_ps, 1)
            pe.wait_ge(tok_ready_act, 6)
            pe.wait_ge(tok_ready_dve, 3)
            for w in range(2):
                if w:
                    pe.wait_ge(score_ready, 4)
                for h in range(4 * w, 4 * w + 4):
                    par, i = h % 2, h // 2
                    for c, (key, n) in enumerate(((ckT[64 * par:64 * par + 64, i, :], 256), (head(K0, h, slice(256, TOK)), DH))):
                        ins = pe.matmul(PS[0:DH, 4 + 2 * par + i % 2, 256 * c:256 * c + n], head(Q0, h, slice(256, TOK)), key,
                                        start=True, stop=True)
                ins.then_inc(score_ps, 1)
            pe.wait_ge(score_ready, 2)
            project(FIRST_STEPS, CHUNK_STEPS)
            pe.wait_ge(ln_done, 6)
            pe.wait_ge(bs_loaded, 16)
            pe.wait_ge(proj_free, 4 + 4 * CHUNK_STEPS)
            for g in range(8):
                par = slice(64 * (g % 2), 64 * (g % 2) + 64)
                for t in range(3):
                    n = ROWS[t]
                    pe.matmul(PS[par, g // 2, cols(t)], ones[0:1, :], bsrow[0:1, g, 0:n], start=True, stop=False)
                    ins = pe.matmul(PS[par, g // 2, cols(t)], vn[0:n, t, 64 * g:64 * g + 64], wsT[0:n, g, 0:n],
                                    start=False, stop=True)
            ins.then_inc(mix_ps, 1)

            def turn_probs(j):
                b = 4 if j % 2 == 0 else 0
                for e in range(2):
                    h = 4 * e + j
                    pe.transpose(PS[:, b + e, 0:P], prob0[:, h, :], ident[:, :])
                    for c in range(2):
                        pe.transpose(PS[:, b + e, P * (c + 1):P * (c + 2)], prob1[:, h, P * c:P * (c + 1)], ident[:, :])
                        pe.transpose(PS[:, b + 2, 192 * e + 64 * c:192 * e + 64 * c + 64], probs[:, h, P * c:P * (c + 1)],
                                     ident[0:DH, 0:DH])
                    ins = pe.transpose(PS[0:DH, b + 2, 192 * e + 128:192 * e + 192], probs[:, h, 256:TOK], ident[0:DH, 0:DH])
                ins.then_inc(probT_ps, 1)

            def attend(j):
                pe.wait_ge(probT_act, j + 1)
                pe.wait_ge(probT_dve, j + 1)
                bank = 7 if j % 2 == 0 else 3
                if j >= 2:
                    pe.wait_ge(oa_ready, j - 1)
                for e in range(2):
                    rows, c = slice(64 * e, 64 * e + 64), slice(64 * (2 * j + e), 64 * (2 * j + e) + 64)
                    pt, ps = probT[:, j, e, :], probT[:, j, 2, :]
                    pe.matmul(PS[rows, bank, 0:P], v_tok[:, 0, c], pt[:, 0:P], start=True, stop=True)
                    pe.matmul(PS[rows, bank, P:2 * P], v_tok[:, 0, c], pt[:, P:2 * P], start=True, stop=False)
                    pe.matmul(PS[rows, bank, P:2 * P], v_tok[:, 1, c], pt[:, 2 * P:3 * P], start=False, stop=True)
                    o = 192 * e
                    pe.matmul(PS[rows, bank, 256:TOK], cv[:, 0, c], ps[:, o:o + 64], start=True, stop=False)
                    pe.matmul(PS[rows, bank, 256:TOK], cv[:, 1, c], ps[:, o + 64:o + 128], start=False, stop=False)
                    ins = pe.matmul(PS[rows, bank, 256:TOK], v_tok[0:DH, 2, c], ps[0:DH, o + 128:o + 192], start=False, stop=True)
                ins.then_inc(oa_ps, 1)

            pe.wait_ge(prob_ready, 3)
            turn_probs(0)
            pe.wait_ge(mix_ready, 1)
            turn_probs(1)
            for j in range(4):
                attend(j)
                if j < 2:
                    turn_probs(j + 2)
            pe.wait_ge(oa_ready, 4)
            pe.sem_inc(branch_free, 4)
            with pe.Fori(0, 2) as i:
                for c in range(2):
                    pe.wait_ge(w_loaded[c], W_IN_LOADS * CHUNK_STEPS + 32 * (i + 1))
                    for m in range(2):
                        b = 2 * c + m
                        pe.wait_ge(branch_free, 4 * i + b + 1)
                        for br, x in enumerate((oaT, obT)):
                            for k in range(JW):
                                ins = pe.matmul(PS[:, 2 * b + br, 0:TOK], wr[:, c, JW * br + k, P * m:P * (m + 1)], x[:, k, :],
                                                start=(k == 0), stop=(k == JW - 1))
                        ins.then_inc(branch_ps, 1)
                    pe.wait_ge(branch_ps, 4 * i + 2 * c + 2)
                    pe.sem_inc(w_used[c], 1)
            loaded = W_IN_LOADS * CHUNK_STEPS + 64
            pe.wait_ge(branch_free, 4 + KD)
            pe.sem_inc(out_free, 6)
            with pe.Fori(0, 2) as i:
                for c in range(2):
                    pe.wait_ge(w_loaded[c], loaded + 16 * (i + 1))
                    for t in range(3):
                        pe.wait_ge(out_free, 6 * i + 3 * c + t + 1)
                        for k in range(KD):
                            ins = pe.matmul(PS[0:ROWS[t], 4 * c + t, 0:CH], mT[:, k, cols(t)], wr[:, c, k, :],
                                            start=(k == 0), stop=(k == KD - 1))
                        ins.then_inc(out_ps, 1)
                    pe.wait_ge(out_ps, 6 * i + 3 * c + 3)
                    pe.sem_inc(w_used[c], 1)
            loaded += 32
            pe.wait_ge(out_free, 6 + 12)
            for t in range(3):
                pe.wait_ge(ln_done, 7 + t)
                transpose_rows(xs, t, 2 * t, x1T_ps)
            pe.wait_ge(route_loaded, 64)
            for t in range(3):
                pe.wait_ge(x1T_ready, t + 1)
                for k in range(KD):
                    ins = pe.matmul(PS[0:ROWS[t], 6, NE * t:NE * (t + 1)], xT[:, k, cols(t)], rw[:, k, :],
                                    start=(k == 0), stop=(k == KD - 1))
                ins.then_inc(logits_ps, 1)
            for c in range(2):
                pe.wait_ge(w_loaded[c], loaded + 16)
                for m in range(2):
                    for k in range(KD):
                        ins = pe.matmul(PS[:, 2 * c + m, 0:TOK], wr[:, c, k, P * m:P * (m + 1)], xT[:, k, :],
                                        start=(k == 0), stop=(k == KD - 1))
                    ins.then_inc(shared_up, 1)
                pe.wait_ge(shared_up, 2 * c + 2)
                pe.sem_inc(w_used[c], 1)
            for t in range(3):
                pe.wait_ge(mask_ready, t + 1)
                for u in range(t + 1):
                    lhs = tri[0:ROWS[u], 0:ROWS[t]] if u == t else onesb[:, 0:ROWS[t]]
                    pe.matmul(PS[0:ROWS[t], 7, NE * t:NE * (t + 1)], lhs, mask[0:ROWS[u], u, :], start=(u == 0), stop=(u == t))
            for t in range(3):
                ins = pe.matmul(PS[:, 7, 3 * NE:4 * NE], onesb[0:ROWS[t], :], mask[0:ROWS[t], t, :], start=(t == 0), stop=(t == 2))
            ins.then_inc(pos_ps, 1)
            pe.wait_ge(w_loaded[0], loaded + 32)
            pe.wait_ge(shared_hid, 2)
            for t in range(3):
                for half in range(2):
                    for m in range(2):
                        ins = pe.matmul(PS[0:ROWS[t], 2 * t + half, :], hsT[:, m, cols(t)], sw2[:, m, 512 * half:512 * half + 512],
                                        start=(m == 0), stop=(m == 1))
                ins.then_inc(shared_ps, 1)
            pe.wait_ge(shared_ps, 3)
            pe.sem_inc(w_used[0], 1)
            pe.wait_ge(ple_loaded, 48)
            pe.wait_ge(acc_init, 1)
            for t in range(3):
                for m in range(2):
                    ins = pe.transpose(PS[:, m, cols(t)], p_tok[0:ROWS[t], t, P * m:P * (m + 1)], ident[0:ROWS[t], 0:ROWS[t]])
            ins.then_inc(pT_ps, 1)
            pe.wait_ge(rounds_ready, 1)
            pe.wait_ge(pT_ready, 1)
            pe.wait_ge(acc_init, 3)
            pe.sem_inc(acc_added, 1)
            pe.sem_inc(xgT_ps, 2)
            rounds = pe.value_load(rounds_i[0:1, 0:1], min_val=1, max_val=MAX_ROUNDS)
            with pe.Fori(0, rounds) as r:
                pe.wait_ge(onehot_ready, 3 * r + 3)
                pe.sem_inc(pe_rounds, 1)
                with pe.Fori(0, PAIRS // 4) as q:
                    for s in range(4):
                        for t in range(3):
                            ins = pe.matmul(PS[:, 6, ds((4 * q + s) * 10, 10)],
                                            onehot[:, t, ds((4 * q + s) * 2, 2), :].rearrange("p e s -> p (e s)"),
                                            attrs[:, t, ds((4 * q + s) * 2, 2), :].rearrange("p e f -> p (e f)"),
                                            start=(t == 0), stop=(t == 2))
                pe.transpose(PS[0:1, 7, 0:1], ident[0:1, 0:1], ident[0:1, 0:1]).then_inc(table_ps, 1)
                with pe.Fori(0, STEPS) as i:
                    n = r * STEPS + i

                    def turn_gathered(j):
                        pe.wait_ge(xg_loaded[j], 16 * (n + 1))
                        for k in range(KD):
                            ins = pe.transpose(PS[:, k // 4, P * (k % 4):P * (k % 4 + 1)], xg[:, j, k::KD], ident[:, :])
                        ins.then_inc(xgT_ps, 1)

                    def up(j, ks):
                        for k in ks:
                            for e in range(2):
                                c = slice(64 * e, 64 * e + 64)
                                ins = pe.matmul(PS[c, 2 + j, :], xgT[:, j, k, c], w13(j, e, k), start=(k == 0), stop=(k == KD - 1))
                        if KD - 1 in ks:
                            ins.then_inc(up_done[j], 1)

                    def turn_hidden(j):
                        pe.wait_ge(hid_ready, 2 * n + j + 1)
                        for k in range(2):
                            ins = pe.transpose(PS[:, 4, HID * j + P * k:HID * j + P * (k + 1)], hid[:, j, k::2], ident[:, :])
                        ins.then_inc(hidT_ps, 1)

                    def down(j, half):
                        for k in range(2):
                            for e in range(2):
                                c = slice(64 * e, 64 * e + 64)
                                ins = pe.matmul(PS[c, 5 + half, :], hidT[:, j, k, c], w2(j, e, k, half), start=(k == 0), stop=(k == 1))
                        ins.then_inc(y_ps, 1)

                    def scatter(j):
                        for p in range(6):
                            q, t, half = 6 * j + p, p // 2, p % 2
                            if q >= 3:
                                pe.wait_ge(acc_added, 12 * n + q - 1)
                            for part in range(2):
                                ins = pe.matmul(PS[:, (7, 0, 1)[q % 3], :], scat[:, j, P * t:P * (t + 1)],
                                                ysplit[:, j, part, 512 * half:512 * half + 512], start=(part == 0), stop=(part == 1))
                            ins.then_inc(scat_ps, 1)

                    pe.wait_ge(acc_added, 12 * n + 1)
                    turn_gathered(0)
                    pe.wait_ge(xgT_ready, 2 * n + 1)
                    pe.wait_ge(w13_loaded[0], 64 * (n + 1))
                    up(0, range(4))
                    turn_gathered(1)
                    up(0, range(4, KD))
                    pe.wait_ge(xgT_ready, 2 * n + 2)
                    pe.wait_ge(w13_loaded[1], 64 * (n + 1))
                    up(1, range(4))
                    turn_hidden(0)
                    up(1, range(4, KD))
                    pe.wait_ge(hidT_ready, 2 * n + 1)
                    pe.wait_ge(w2_loaded[0], 32 * (n + 1))
                    down(0, 0)
                    turn_hidden(1)
                    down(0, 1)
                    pe.wait_ge(hidT_ready, 2 * n + 2)
                    pe.wait_ge(w2_loaded[1], 32 * (n + 1))
                    for half in range(2):
                        pe.wait_ge(y_high, 4 * n + half + 1)
                        pe.wait_ge(y_low, 4 * n + half + 1)
                        down(1, half)
                    pe.wait_ge(scat_ready, 2 * n + 2)
                    scatter(0)
                    pe.wait_ge(y_high, 4 * n + 4)
                    pe.wait_ge(y_low, 4 * n + 4)
                    scatter(1)
            pe.wait_ge(acc_added, rounds * (12 * STEPS) + 1)
            for t in range(3):
                for half in range(2):
                    for m in range(2):
                        ins = pe.matmul(PS[0:ROWS[t], 2 + 2 * t + half, :], pT[:, m, cols(t)], proj_w[:, m, 512 * half:512 * half + 512],
                                        start=(m == 0), stop=(m == 1))
                ins.then_inc(ple_ps, 1)
            for t in range(3):
                pe.wait_ge(ln_done, 10 + t)
                if t:
                    pe.wait_ge(ple_ready, t)
                transpose_rows(xs, t, 2 * t, x2T_ps)
            pe.wait_ge(gate_loaded, 32)
            pe.wait_ge(ple_ready, 3)
            pe.wait_ge(x2T_ready, 2)
            for t in range(3):
                pe.wait_ge(x2T_ready, t + 1)
                for half in range(2):
                    for k in range(KD):
                        ins = pe.matmul(PS[0:ROWS[t], (6, 0, 2)[t] + half, :], xT[:, k, cols(t)],
                                        gate_w[k // 4][:, k % 4, 512 * half:512 * half + 512], start=(k == 0), stop=(k == KD - 1))
                ins.then_inc(gate_ps, 1)


_INS = ["x_prompt", "x_sample", "cache_attn_k", "cache_attn_v", "p_prompt", "p_sample", "ln_in_g", "ln_in_b", "w_in",
        "attn_rel_bias", "mlp_ln_g", "mlp_ln_b", "mlp_w_s", "mlp_b_s", "w_branch_a", "w_branch_b", "w_out", "ln1_g", "ln1_b",
        "router_w", "router_bias", "exp_w1", "exp_w3", "exp_w2", "shared_w1", "shared_w3", "shared_w2", "ln2_g", "ln2_b",
        "ple_w_gate", "ple_w_proj"]


def kernel(**inputs):
    import numpy as _np
    import concourse.bacc as _bacc
    from concourse import mybir as _mybir
    from concourse.bass_utils import run_bass_kernel_spmd as _run

    x, s = inputs["x_prompt"].shape, inputs["x_sample"].shape
    kv = inputs["cache_attn_k"].shape
    width = inputs["mlp_ln_g"].shape[-1]
    outs = [x, s, (1, x[0], x[1], *kv[3:]), (1, x[0], x[1], *kv[3:]), (1, s[0], s[1], *kv[3:]), (1, s[0], s[1], *kv[3:]),
            (1, x[0], 128, width), (1, s[0], s[1], width)]
    nc = _bacc.Bacc("TRN2", target_bir_lowering=False, num_devices=1)
    arrays, args = {}, []
    for name in _INS:
        a = _np.ascontiguousarray(inputs[name])
        arrays[f"in_{name}_dram"] = a
        args.append(nc.dram_tensor(f"in_{name}_dram", a.shape, _mybir.dt.from_np(a.dtype), kind="ExternalInput").ap())
    for i, shape in enumerate(outs):
        args.append(nc.dram_tensor(f"out_{i}_dram", shape, _mybir.dt.float32, kind="ExternalOutput").ap())
    trunk_step(nc, *args)
    r = _run(nc, [arrays], core_ids=[0])
    return tuple(r.results[0][f"out_{i}_dram"] for i in range(len(outs)))
```

```python
from contextlib import ExitStack

import concourse.bass as bass
from concourse import mybir

F32 = mybir.dt.float32
F32R = mybir.dt.float32r
BF16 = mybir.dt.bfloat16
I32 = mybir.dt.int32
ALU = mybir.AluOpType
ACT = mybir.ActivationFunctionType
AX = mybir.AxisListType
ds = bass.ds

P = 128
ROWS = (128, 128, 64)
TOK = sum(ROWS)
HEADS, DH = 8, 64
EPS = 1e-5
ALPHA = 2.0 ** 0.25
SCALE = DH ** -0.5
ROUTED_SCALE = 2.5
MASKED = -1.0e30


def trunk_step(nc, x_prompt, x_sample, cache_k, cache_v, p_prompt, p_sample, ln_in_g, ln_in_b, w_in,
               rel_bias, mlp_g, mlp_b, mlp_w_s, mlp_b_s, w_a, w_b, w_out, ln1_g, ln1_b, router_w,
               router_bias, exp_w1, exp_w3, exp_w2, sh_w1, sh_w3, sh_w2, ln2_g, ln2_b, ple_gate,
               ple_proj, y_prompt, y_sample, new_k_prompt, new_v_prompt, new_k_sample, new_v_sample,
               new_mlp_prompt, new_mlp_sample):
    D = x_prompt.shape[2]
    KD = D // P
    N_IN = w_in.shape[2]
    FT = N_IN // P
    CH = 256
    AW = HEADS * DH
    JW = AW // P
    NE = router_w.shape[2]
    HID = exp_w1.shape[3]
    GROUPS, PER_GROUP, KEEP_GROUPS = 8, NE // 8, 4
    SLOTS = 64
    PAIRS = NE // 2
    STEPS = PAIRS // 2
    MAX_ROUNDS = -(-TOK // SLOTS)
    TP = 3 * P
    REL = rel_bias.shape[2]
    PAD = 64
    PEXP = 2 * KD * HID + 2 * D
    Q0, K0, V0, U0, S0 = 0, 4, 8, 12, 16
    ZT = 28
    GATE_A = [V0 + j for j in range(4)] + [S0 + j for j in range(4)]
    GB0 = 20
    W_TILES = N_IN // P
    BRANCH_T = W_TILES
    OUT_T = BRANCH_T + KD
    SHARED_T = OUT_T + KD

    with ExitStack() as ctx:
        def sb(name, shape, dt=F32):
            return ctx.enter_context(nc.sbuf_tensor(name, shape, dt))

        def sem(name):
            return ctx.enter_context(nc.semaphore(name))

        ring = sb("expert_ring", [P, 2 * 2 * PEXP])
        z = sb("z", [P, ZT * TOK])
        xs = sb("xs", [P, 3, D])
        parts = sb("parts", [P, 2 * 3 * D], F32R)
        xT = parts[:, 0:2 * KD * TOK].rearrange("p (h k t) -> p h k t", h=2, k=KD)
        xrows = parts[:, :].rearrange("p (h t k c) -> p h t k c", h=2, t=3, k=KD)
        wr = sb("weight_ring", [P, 2, KD, CH])
        split = sb("split", [P, 4, 2, 4 * P], F32R)
        ysplit = split[:, :, :, :].rearrange("p (a b) h c -> p a (b h c)", a=2).rearrange("p a (h c) -> p a h c", h=2)
        scat = sb("scatter", [P, 2, TP], F32R)
        pick = sb("pick", [P, 3, 4 * SLOTS], F32R)
        ident = sb("ident", [P, P])
        ones = sb("ones", [1, DH])
        tri = sb("tri", [P, P], BF16)
        onesb = sb("ones_bf", [P, P], BF16)
        stats = sb("stats", [P, 3, 2, 6])
        meanvar = sb("meanvar", [P, 3, 2])
        vareps = sb("vareps", [P, 3])
        std = sb("std", [P, 3])
        rstd = sb("rstd", [P, 3])
        smax = sb("smax", [P, 3, HEADS])
        snegmax = sb("snegmax", [P, 3, HEADS])
        ssum = sb("ssum", [P, 3, HEADS])
        srec = sb("srec", [P, 3, HEADS])
        round_thr = sb("round_thr", [1, MAX_ROUNDS - 1])
        round_gt = sb("round_gt", [1, MAX_ROUNDS - 1])
        rounds_f = sb("rounds_f", [1, 2])
        rounds_i = sb("rounds_i", [1, 1], I32)
        PS = ctx.enter_context(nc.psum_tensor("PS", [P, 8, 512], F32))

        def early(at, *shape, rows=P):
            n = 1
            for s in shape:
                n *= s
            v = ring[0:rows, at:at + n]
            if len(shape) == 2:
                return v.rearrange("p (a b) -> p a b", a=shape[0])
            if len(shape) == 3:
                return v.rearrange("p (a b c) -> p a b c", a=shape[0], b=shape[1])
            return v

        prob1 = early(0, HEADS, 256)
        prob0 = early(2048, HEADS, P)
        probs = early(3072, HEADS, TOK, rows=DH)
        probT = early(5632, 4, 3, 384)
        relpad = early(5632, PAD + REL, rows=HEADS)
        v_tok = early(10240, 3, AW)
        k_tok = early(11776, 3, AW)
        ck = early(13312, 2, AW)
        cv = early(14336, 2, AW)
        ckT = early(15360, JW, 256)
        ws = early(16384, 8, P)
        wsT = early(17408, 8, P)
        vn = early(18432, 3, AW)
        mlpvec = early(19968, 2, AW)
        bsrow = early(20992, 8, P, rows=1)
        lninvec = early(22016, 2, D)
        HO = [(h % 2) * 4 + h // 2 for h in range(HEADS)]

        zt = z[:, :].rearrange("p (a t) -> p a t", t=TOK)
        obT = zt[:, U0:U0 + JW, :]
        mT = zt[:, 0:KD, :]
        woT = zt[:, KD:2 * KD, :]

        def zv(at, n):
            return z[:, at:at + n]

        lnvec = zv(5376, 2 * D).rearrange("p (a d) -> p a d", a=2)
        hsT = zv(0, 2 * TOK).rearrange("p (a t) -> p a t", a=2)
        rw = zv(640, KD * NE).rearrange("p (k e) -> p k e", k=KD)
        rbias = zv(1152, NE)
        rtemp = [zv(1280 + 192 * i, 192).rearrange("p (a e) -> p a e", a=3) for i in range(8)]
        score, sel, msel, replaced, maskf, wt, wres, gmax = rtemp
        rsmall = zv(1280 + 8 * 192, 192).rearrange("p (a e) -> p a e", a=3)
        mask = zv(1280 + 9 * 192, 96).bitcast(BF16).rearrange("p (a e) -> p a e", a=3)
        xgT = zv(0, KD * 4 * SLOTS).rearrange("p (k s) -> p k s", k=KD)
        act_h = zv(4096, 2 * HID).rearrange("p (a d) -> p a d", a=2)
        hid = zv(4608, 2 * HID).rearrange("p (a d) -> p a d", a=2)
        hidT = zv(5120, 2 * HID).rearrange("p (a k s) -> p a k s", a=2, k=2)
        keep = ZT * TOK - 1536
        pos = zv(keep, 3 * (NE + 8)).rearrange("p (a e) -> p a e", a=3)
        attrs = zv(keep + 216, 3 * (NE + 4) * 2).rearrange("p (a e f) -> p a e f", a=3, f=2)
        slots = zv(keep + 624, 4).rearrange("p (j f) -> p j f", j=2)
        iota_slot = zv(keep + 628, SLOTS)
        iota_tok = zv(keep + 692, TP)
        acc = xs

        gate_w = [ring[:, PEXP * e:PEXP * e + 4 * D].rearrange("p (k d) -> p k d", k=4) for e in range(2)]
        ple = ring[:, 2 * PEXP:2 * PEXP + 3 * D].rearrange("p (a d) -> p a d", a=3)
        ln2vec = ring[:, 2 * KD * HID:PEXP].rearrange("p (a d) -> p a d", a=2)
        sgT = ring[:, 3 * PEXP:3 * PEXP + KD * TOK].rearrange("p (a t) -> p a t", a=KD)
        wr0 = wr[:, 0, :, :].rearrange("p k c -> p (k c)")
        p_tok = wr0[:, 0:768].rearrange("p (a d) -> p a d", a=3)
        pT = wr0[:, 768:768 + 2 * TOK].rearrange("p (a t) -> p a t", a=2)
        proj_w = wr[:, 1, :, :].rearrange("p k c -> p (k c)").rearrange("p (k d) -> p k d", k=2)
        sw2 = wr0.rearrange("p (k d) -> p k d", k=2)

        def w13(pair, e, k):
            o = (2 * pair + e) * PEXP
            return ring[:, o:o + 2 * KD * HID].rearrange("p (m k h) -> p m k h", m=2, k=KD)[:, :, k, :]

        def w2(pair, e, k, half):
            o = (2 * pair + e) * PEXP + 2 * KD * HID + k * D + 512 * half
            return ring[:, o:o + 512]

        RW = PAD + REL
        rel_dram = nc.dram_tensor("rel_rows", (HEADS, P, RW), F32, kind="Internal")

        x_loaded = sem("x_loaded")
        lnin_loaded = sem("lnin_loaded")
        w_loaded = [sem(f"w_loaded{c}") for c in range(2)]
        cache_loaded = sem("cache_loaded")
        ws_loaded = sem("ws_loaded")
        mlpvec_loaded = sem("mlpvec_loaded")
        bs_loaded = sem("bs_loaded")
        rel_loaded = sem("rel_loaded")
        rel_stored = sem("rel_stored")
        bias_loaded = sem("bias_loaded")
        route_loaded = sem("route_loaded")
        ln2_loaded = sem("ln2_loaded")
        sw2_loaded = sem("sw2_loaded")
        w13_loaded = [sem(f"w13_loaded{j}") for j in range(2)]
        w2_loaded = [sem(f"w2_loaded{j}") for j in range(2)]
        ple_loaded = sem("ple_loaded")
        gate_loaded = sem("gate_loaded")
        kv_stored = sem("kv_stored")
        y_stored = sem("y_stored")
        const_zero = sem("const_zero")
        const_ready = sem("const_ready")
        wsmask_ready = sem("wsmask_ready")
        dve_step = sem("dve_step")
        dve_last_step = sem("dve_last_step")
        var_ready = sem("var_ready")
        std_ready = sem("std_ready")
        ln_done = sem("ln_done")
        xT_ps = sem("xT_ps")
        xT_ready = sem("xT_ready")
        prep_ps = sem("prep_ps")
        prep_ready = sem("prep_ready")
        w_high = sem("w_high")
        w_low = sem("w_low")
        half_used = sem("half_used")
        xT_high = sem("xT_high")
        proj_free = sem("proj_free")
        tok_ps = sem("tok_ps")
        tok_ready_act = sem("tok_ready_act")
        tok_ready_dve = sem("tok_ready_dve")
        gelu_u = sem("gelu_u")
        score_ps = sem("score_ps")
        score_ready = sem("score_ready")
        negmax_ready = sem("negmax_ready")
        exp_done = sem("exp_done")
        prob_ready = sem("prob_ready")
        mix_ps = sem("mix_ps")
        mix_ready = sem("mix_ready")
        sig_done = sem("sig_done")
        ob_high = sem("ob_high")
        ob_low = sem("ob_low")
        probT_ps = sem("probT_ps")
        probT_act = sem("probT_act")
        probT_dve = sem("probT_dve")
        oa_ps = sem("oa_ps")
        oa_ready = sem("oa_ready")
        oa_high = sem("oa_high")
        m_high = sem("m_high")
        m_low = sem("m_low")
        branch_free = sem("branch_free")
        out_free = sem("out_free")
        out_ps = sem("out_ps")
        residual = sem("residual")
        x1T_ps = sem("x1T_ps")
        x1T_high = sem("x1T_high")
        x1T_ready = sem("x1T_ready")
        logits_ps = sem("logits_ps")
        score_sig = sem("score_sig")
        shared_silu = sem("shared_silu")
        shared_hid = sem("shared_hid")
        shared_ps = sem("shared_ps")
        acc_init = sem("acc_init")
        mask_ready = sem("mask_ready")
        pos_ps = sem("pos_ps")
        rounds_ready = sem("rounds_ready")
        pT_ps = sem("pT_ps")
        pT_ready = sem("pT_ready")
        table_ps = sem("table_ps")
        slots_ready = sem("slots_ready")
        dve_rounds = sem("dve_rounds")
        pos_moved = sem("pos_moved")
        pick_ready = sem("pick_ready")
        xrows_high = sem("xrows_high")
        xrows_ready = sem("xrows_ready")
        gather_ps = sem("gather_ps")
        gathered_ready = sem("gathered_ready")
        up_done = [sem(f"up_done{j}") for j in range(2)]
        silu_done = sem("silu_done")
        hid_ready = sem("hid_ready")
        hidT_ps = sem("hidT_ps")
        hidT_ready = sem("hidT_ready")
        y_ps = sem("y_ps")
        y_high = sem("y_high")
        y_low = sem("y_low")
        scat_ready = sem("scat_ready")
        scat_ps = sem("scat_ps")
        acc_added = sem("acc_added")
        ple_ps = sem("ple_ps")
        ple_ready = sem("ple_ready")
        x2T_ps = sem("x2T_ps")
        x2T_high = sem("x2T_high")
        x2T_ready = sem("x2T_ready")
        gate_high = sem("gate_high")
        gate_low = sem("gate_low")
        gate_used = sem("gate_used")
        gate_sig = sem("gate_sig")
        gate_rows = sem("gate_rows")
        y_ready = sem("y_ready")

        SCAT_BANK = (2, 3, 7, 2, 3, 7)
        CHUNK_STEPS = N_IN // CH // 2
        FIRST_STEPS = (S0 + JW) * P // CH // 2
        WL = 32

        block = ctx.enter_context(nc.Block())

        def cols(t):
            return slice(P * t, P * t + ROWS[t])

        @block.sync
        def _(sp):
            sp.dma_start(xs[:, 0:2, :], x_prompt[0].rearrange("(a p) d -> p a d", p=P)).then_inc(x_loaded, 16)
            sp.dma_start(xs[0:ROWS[2], 2, :], x_sample[0]).then_inc(x_loaded, 16)
            w_in_v = w_in[0].rearrange("(p k) n -> p k n", k=KD)

            def load_chunk(c, first, second):
                sp.dma_start(wr[:, c, 0:4, :], first).then_inc(w_loaded[c], 16)
                sp.dma_start(wr[:, c, 4:KD, :], second).then_inc(w_loaded[c], 16)

            for c in range(2):
                n = slice(c * CH, (c + 1) * CH)
                load_chunk(c, w_in_v[:, 0:4, n], w_in_v[:, 4:KD, n])
            with sp.Fori(0, CHUNK_STEPS - 1) as i:
                for c in range(2):
                    sp.wait_ge(w_low, 8 * i + 4 * c + 4)
                    n = ds((2 * i + c + 2) * CH, CH)
                    load_chunk(c, w_in_v[:, 0:4, n], w_in_v[:, 4:KD, n])

            w1_v = exp_w1[0].rearrange("e (p k) h -> e p (k h)", k=KD)
            w3_v = exp_w3[0].rearrange("e (p k) h -> e p (k h)", k=KD)
            w2_v = exp_w2[0].rearrange("e (p k) d -> e p (k d)", k=2)

            def expert_loads(pair, first):
                for e in range(2):
                    o = (2 * pair + e) * PEXP
                    for m, wv in enumerate((w1_v, w3_v)):
                        yield (ring[:, o + m * KD * HID:o + (m + 1) * KD * HID], wv, e, w13_loaded[pair])

            def down_loads(pair):
                for e in range(2):
                    o = (2 * pair + e) * PEXP + 2 * KD * HID
                    yield (ring[:, o:o + 2 * D], w2_v, e, w2_loaded[pair])

            first = [(2 * j, x) for j in range(2) for x in expert_loads(j, 0)]
            first += [(2 * j, x) for j in range(2) for x in down_loads(j)]

            def first_expert_load():
                if first:
                    base, (dst, wv, e, s) = first.pop(0)
                    sp.dma_start(dst, wv[base + e]).then_inc(s, 16)

            wa_v = w_a[0].rearrange("(j p) n -> p j n", p=P)
            wb_v = w_b[0].rearrange("(j p) n -> p j n", p=P)
            for i in range(2):
                for c in range(2):
                    sp.wait_ge(w_low, 2 * BRANCH_T + 8 * i + 4 * c - 4)
                    n = slice((2 * i + c) * CH, (2 * i + c + 1) * CH)
                    load_chunk(c, wa_v[:, :, n], wb_v[:, :, n])
                    if i == 1:
                        if c == 0:
                            sp.wait_ge(oa_ps, 4)
                            sp.wait_ge(mix_ps, 1)
                            sp.wait_ge(kv_stored, 16 * 6)
                        first_expert_load()
            wo_v = w_out[0].rearrange("(j p) n -> p j n", p=P)
            for i in range(2):
                for c in range(2):
                    sp.wait_ge(w_low, 2 * OUT_T + 8 * i + 4 * c - 4)
                    n = slice((2 * i + c) * CH, (2 * i + c + 1) * CH)
                    load_chunk(c, wo_v[:, 0:4, n], wo_v[:, 4:KD, n])
                    first_expert_load()
            sp.wait_ge(branch_free, 4 + KD)
            sp.dma_start(lnvec[:, 0, :], ln1_g[0].partition_broadcast(P)).then_inc(route_loaded, 16)
            sp.dma_start(lnvec[:, 1, :], ln1_b[0].partition_broadcast(P)).then_inc(route_loaded, 16)
            sp.wait_ge(m_low, 2)
            sp.dma_start(rw[:, :, :], router_w[0].rearrange("(p k) e -> p k e", k=KD)).then_inc(route_loaded, 16)
            sp.dma_start(rbias, router_bias[0].partition_broadcast(P)).then_inc(route_loaded, 16)
            for c, w in enumerate((sh_w1, sh_w3)):
                sp.wait_ge(w_low, 2 * SHARED_T + 4 * c - 4)
                w_v = w[0].rearrange("(p k) h -> p k h", k=KD)
                load_chunk(c, w_v[:, 0:4, :], w_v[:, 4:KD, :])
                first_expert_load()
            sp.wait_ge(w_low, 2 * SHARED_T + 4)
            sp.dma_start(sw2, sh_w2[0].rearrange("(j p) d -> p j d", p=P)).then_inc(sw2_loaded, 16)
            sp.wait_ge(w_low, 2 * SHARED_T + 8)
            sp.dma_start(proj_w, ple_proj[0].rearrange("(j p) d -> p j d", p=P)).then_inc(ple_loaded, 16)
            while first:
                first_expert_load()
            sp.wait_ge(shared_ps, 3)
            sp.dma_start(p_tok[:, 0:2, :], p_prompt[0, 0].rearrange("(a p) d -> p a d", p=P)).then_inc(ple_loaded, 16)
            sp.dma_start(p_tok[0:ROWS[2], 2, :], p_sample[0, 0]).then_inc(ple_loaded, 16)

            def expert_step(n, expert):
                for j in range(2):
                    sp.wait_ge(up_done[j], n)
                    for dst, wv, e, s in expert_loads(j, 0):
                        sp.dma_start(dst, wv[ds(expert + 2 * j + e, 1)].rearrange("o p n -> (o p) n")).then_inc(s, 16)
                for j in range(2):
                    sp.wait_ge(y_ps, 4 * n - 2 + 2 * j)
                    for dst, wv, e, s in down_loads(j):
                        sp.dma_start(dst, wv[ds(expert + 2 * j + e, 1)].rearrange("o p n -> (o p) n")).then_inc(s, 16)

            with sp.Fori(1, STEPS) as i:
                expert_step(i, 4 * i)
            sp.wait_ge(rounds_ready, 1)
            rounds = sp.value_load(rounds_i[0:1, 0:1], min_val=1, max_val=MAX_ROUNDS)
            with sp.If(rounds > 1):
                with sp.Fori(1, rounds) as r:
                    with sp.Fori(0, STEPS) as i:
                        expert_step(r * STEPS + i, 4 * i)
            sp.wait_ge(up_done[0], rounds * STEPS)
            gw_v = ple_gate[0].rearrange("(p k) n -> p k n", k=KD)
            for e in range(2):
                sp.dma_start(gate_w[e], gw_v[:, 4 * e:4 * e + 4, :]).then_inc(gate_loaded, 16)
            sp.wait_ge(y_ps, rounds * (4 * STEPS))
            sp.dma_start(ln2vec[:, 0, :], ln2_g[0].partition_broadcast(P)).then_inc(ln2_loaded, 16)
            sp.dma_start(ln2vec[:, 1, :], ln2_b[0].partition_broadcast(P)).then_inc(ln2_loaded, 16)
            for half in range(2):
                c = slice(512 * half, 512 * half + 512)
                for t in range(3):
                    sp.wait_ge(y_ready, 3 * half + t + 1)
                    out = y_prompt[0, P * t:P * (t + 1), c] if t < 2 else y_sample[0, :, c]
                    sp.dma_start(out, xs[0:ROWS[t], t, c]).then_inc(y_stored, 16)
            sp.wait_ge(y_stored, 16 * 6)

        @block.gpsimd
        def _(pool):
            pool.memset(ident[:, :], 0.0).then_inc(const_zero, 1)
            pool.memset(tri[:, :], 1.0).then_inc(const_zero, 1)
            pool.memset(onesb[:, :], 1.0)
            pool.memset(ones[:, :], 1.0)
            pool.wait_ge(const_zero, 2)
            pool.affine_select(out=ident[:, :], in_=ident[:, :], compare_op=ALU.not_equal, fill=1.0, base=0,
                               pattern=[[-1, P]], channel_multiplier=1)
            pool.affine_select(out=tri[:, :], in_=tri[:, :], compare_op=ALU.is_gt, fill=0.0, base=0,
                               pattern=[[1, P]], channel_multiplier=-1)
            pool.iota(round_thr[:, :], pattern=[[SLOTS, MAX_ROUNDS - 1]], base=SLOTS, channel_multiplier=0,
                      allow_small_or_imprecise_dtypes=True).then_inc(const_ready, 1)
            pool.wait_ge(ws_loaded, 16)
            pool.affine_select(out=ws, in_=ws, compare_op=ALU.is_ge, fill=0.0, base=0,
                               pattern=[[0, 8], [-1, P]], channel_multiplier=1).then_inc(wsmask_ready, 1)
            pool.wait_ge(tok_ready_act, 3)
            pool.dma_start(new_k_prompt[0, 0].rearrange("(a p) h d -> p a (h d)", p=P), k_tok[:, 0:2, :]).then_inc(kv_stored, 16)
            pool.dma_start(new_k_sample[0, 0].rearrange("p h d -> p (h d)"), k_tok[0:ROWS[2], 2, :]).then_inc(kv_stored, 16)
            pool.wait_ge(tok_ready_dve, 3)
            pool.dma_start(new_v_prompt[0, 0].rearrange("(a p) h d -> p a (h d)", p=P), v_tok[:, 0:2, :]).then_inc(kv_stored, 16)
            pool.dma_start(new_v_sample[0, 0].rearrange("p h d -> p (h d)"), v_tok[0:ROWS[2], 2, :]).then_inc(kv_stored, 16)
            pool.wait_ge(ln_done, 6)
            pool.dma_start(new_mlp_prompt[0, 0], vn[:, 1, :]).then_inc(kv_stored, 16)
            pool.dma_start(new_mlp_sample[0, 0], vn[0:ROWS[2], 2, :]).then_inc(kv_stored, 16)
            pool.wait_ge(branch_free, 4 + KD)
            pool.iota(iota_slot, pattern=[[1, SLOTS]], base=0, channel_multiplier=0, allow_small_or_imprecise_dtypes=True)
            pool.iota(iota_tok, pattern=[[1, TP]], base=0, channel_multiplier=0, allow_small_or_imprecise_dtypes=True)
            for t in range(3):
                last = pool.iota(attrs[:, t, :, 1], pattern=[[0, NE + 4]], base=P * t, channel_multiplier=1,
                                 allow_small_or_imprecise_dtypes=True)
            last.then_inc(const_ready, 1)
            for t in range(3):
                pool.wait_ge(xrows_high, t + 1)
                x = xs[0:ROWS[t], t, :].rearrange("p (c k) -> p k c", k=KD)
                pool.tensor_tensor(xrows[0:ROWS[t], 1, t, :, :], x, xrows[0:ROWS[t], 0, t, :, :].bitcast(F32), ALU.subtract)\
                    .then_inc(xrows_ready, 1)

        @block.scalar
        def _(act):
            for i, v in enumerate((ln_in_g, ln_in_b)):
                act.dma_start(lninvec[:, i, :], v.partition_broadcast(P)).then_inc(lnin_loaded, 16)
            act.dma_start(ck, cache_k[0, 0].rearrange("(a p) h d -> p a (h d)", p=P)).then_inc(cache_loaded, 16)
            act.dma_start(ws, mlp_w_s[0].rearrange("g t s -> t g s")).then_inc(ws_loaded, 16)
            act.dma_start(relpad[:, PAD:PAD + REL], rel_bias[0]).then_inc(rel_loaded, 16)
            act.dma_start(cv, cache_v[0, 0].rearrange("(a p) h d -> p a (h d)", p=P)).then_inc(cache_loaded, 16)
            for i, v in enumerate((mlp_g, mlp_b)):
                act.dma_start(mlpvec[:, i, :], v[0].partition_broadcast(P)).then_inc(mlpvec_loaded, 16)
            act.dma_start(bsrow, mlp_b_s[0:1]).then_inc(bs_loaded, 16)

            def norm_std(n):
                nc.scalar.preload_act_table(ACT.Sqrt)
                act.wait_ge(var_ready, n)
                nc.scalar.activation(std[:, :], vareps[:, :], ACT.Sqrt).then_inc(std_ready, 1)

            def high(tile, half, load, reused, place=None):
                place = (tile if place is None else place) % 4
                act.wait_ge(w_loaded[place // 2], load)
                if reused:
                    act.wait_ge(half_used, 2 * (tile - 2) + half + 1)
                c = place // 2
                raw = wr[:, c, 4 * half:4 * half + 4, P * (place % 2):P * (place % 2) + P]
                nc.scalar.activation(split[:, 2 * (place % 2) + half, 0, :].rearrange("p (k n) -> p k n", k=4), raw, ACT.Copy)\
                    .then_inc(w_high, 1)

            for tile in range(2):
                for half in range(2):
                    high(tile, half, WL, False)
            norm_std(1)
            act.wait_ge(rel_loaded, 16)
            nc.scalar.activation(relpad[:, 0:PAD], relpad[:, PAD:PAD + 1].to_broadcast([HEADS, PAD]), ACT.Copy)\
                .then_inc(rel_stored, 1)
            act.wait_ge(rel_stored, 1)
            act.dma_start(rel_dram.ap(), relpad.unsqueeze(1).to_broadcast([HEADS, P, RW])).then_inc(rel_stored, 16)
            act.wait_ge(rel_stored, 17)

            def toeplitz(dst, rows, par, keys, first):
                src = bass.AP(tensor=rel_dram, offset=par * P * RW + first,
                              ap=[[RW - 1, rows], [2 * P * RW, 4], [1, keys]])
                act.dma_start(dst, src).then_inc(bias_loaded, 16)

            for par in range(2):
                toeplitz(prob1[:, 4 * par:4 * par + 4, :], P, par, 256, PAD + 256 - P)
                toeplitz(prob0[:, 4 * par:4 * par + 4, :], P, par, P, PAD + 256)
                toeplitz(probs[:, 4 * par:4 * par + 4, :], DH, par, TOK, PAD)

            def high_xT(ps_sem, ready, bank):
                for t in range(3):
                    act.wait_ge(ps_sem, t + 1)
                    b = bank(t)
                    src = PS[:, b:b + 2, :].rearrange("p b (k s) -> p (b k) s", k=4)[:, :, 0:ROWS[t]]
                    nc.scalar.activation(xT[:, 0, :, cols(t)], src, ACT.Copy).then_inc(ready, 1)

            high_xT(xT_ps, xT_high, lambda t: 2 * (t % 2))
            with act.Fori(0, FIRST_STEPS) as i:
                for b in range(4):
                    tile = 4 * i + b
                    for half in range(2):
                        high(tile + 2, half, WL * (i + 1) + WL * (b // 2), True, b + 2)
                    act.wait_ge(half_used, 2 * tile + 2)
                    nc.scalar.activation(zt[:, ds(tile, 1), :].rearrange("p o t -> p (o t)"), PS[:, b, 0:TOK], ACT.Copy)\
                        .then_inc(proj_free, 1)
            for t in range(3):
                act.wait_ge(tok_ps, t + 1)
                nc.scalar.activation(k_tok[0:ROWS[t], t, :], PS[0:ROWS[t], 4 + t, :], ACT.Copy).then_inc(tok_ready_act, 1)
            for t in range(3):
                act.wait_ge(tok_ps, 7 + t)
                nc.scalar.activation(vn[0:ROWS[t], t, :], PS[0:ROWS[t], (6, 7, 4)[t], :], ACT.Gelu_apprx_tanh)\
                    .then_inc(tok_ready_act, 1)
            act.wait_ge(proj_free, 4 + FIRST_STEPS * 4)
            nc.scalar.activation(obT, obT, ACT.Gelu_apprx_tanh).then_inc(gelu_u, 1)
            group = ((prob1, P), (prob0, P), (probs, DH))
            for i in range(4 * (CHUNK_STEPS - FIRST_STEPS)):
                tile = 4 * FIRST_STEPS + i
                for half in range(2):
                    high(tile + 2, half, WL * ((tile + 2) // 4 + 1), True)
                act.wait_ge(half_used, 2 * tile + 2)
                place = GATE_A[i] if i < KD else GB0 + i - KD
                nc.scalar.activation(zt[:, place, :], PS[:, i % 4, 0:TOK], ACT.Copy).then_inc(proj_free, 1)
                if i // 4 < 3:
                    t = i // 4
                    pr, n = group[t]
                    if i % 4 == 0:
                        act.wait_ge(negmax_ready, t + 1)
                    for h in (2 * (i % 4), 2 * (i % 4) + 1):
                        last = nc.scalar.activation(pr[:, h, :], pr[:, h, :], ACT.Exp, bias=snegmax[0:n, t, h:h + 1],
                                                    accum_out=ssum[0:n, t, h:h + 1])
                    if i % 4 == 3:
                        last.then_inc(exp_done, 1)
                if i == 12:
                    norm_std(2)
            act.wait_ge(proj_free, 4 + CHUNK_STEPS * 4)
            nc.scalar.activation(zt[:, V0:V0 + 4, :], zt[:, V0:V0 + 4, :], ACT.Sigmoid)
            nc.scalar.activation(zt[:, S0:ZT, :], zt[:, S0:ZT, :], ACT.Sigmoid).then_inc(sig_done, 1)
            act.wait_ge(mix_ready, 1)
            nc.scalar.activation(xT[:, 0, JW:KD, :], obT, ACT.Copy).then_inc(ob_high, 1)

            def turned_probs(j):
                act.wait_ge(probT_ps, j + 1)
                b = 4 if j % 2 == 0 else 0
                nc.scalar.activation(probT[:, j, 0:2, :], PS[:, b:b + 2, 0:384], ACT.Copy).then_inc(probT_act, 1)

            turned_probs(0)
            turned_probs(1)
            for j in range(4):
                act.wait_ge(oa_ps, j + 1)
                nc.scalar.activation(xT[:, 0, j, :], PS[:, 7 if j % 2 == 0 else 3, 0:TOK], ACT.Copy).then_inc(oa_high, 1)
                if j < 2:
                    turned_probs(j + 2)
            with act.Fori(0, 2) as i:
                for b in range(4):
                    for half in range(2):
                        high(BRANCH_T + 4 * i + b + 2, half, WL * (BRANCH_T // 4 + b // 2) + WL * (i + 1) , True, b + 2)
            for j in range(2):
                act.wait_ge(branch_free, 4 + 4 * (j + 1))
                nc.scalar.activation(xT[:, 0, 4 * j:4 * j + 4, :], mT[:, 4 * j:4 * j + 4, :], ACT.Copy).then_inc(m_high, 1)
            with act.Fori(0, 2) as i:
                for b in range(4):
                    tile = OUT_T + 4 * i + b
                    for half in range(2):
                        high(tile + 2, half, WL * (OUT_T // 4 + b // 2) + WL * (i + 1), True, b + 2)
                    act.wait_ge(half_used, 2 * tile + 2)
                    nc.scalar.activation(woT[:, ds(4 * i + b, 1), :].rearrange("p o t -> p (o t)"), PS[:, b, 0:TOK], ACT.Copy)\
                        .then_inc(out_free, 1)
            norm_std(3)
            high_xT(x1T_ps, x1T_high, lambda t: 2 * t)
            for t in range(3):
                act.wait_ge(logits_ps, 3)
                nc.scalar.activation(score[0:ROWS[t], t, :], PS[0:ROWS[t], 6, NE * t:NE * (t + 1)], ACT.Sigmoid)\
                    .then_inc(score_sig, 1)
            for tile in range(SHARED_T + 2, SHARED_T + 4):
                for half in range(2):
                    high(tile, half, WL * (tile // 4 + 1), True)
            for m in range(2):
                act.wait_ge(half_used, 2 * SHARED_T + 2 * m + 2)
                nc.scalar.activation(hsT[:, m, :], PS[:, m, 0:TOK], ACT.Silu).then_inc(shared_silu, 1)
            act.wait_ge(half_used, 2 * SHARED_T + 8)
            for t in range(3):
                x = xs[0:ROWS[t], t, :].rearrange("p (c k) -> p k c", k=KD)
                nc.scalar.activation(xrows[0:ROWS[t], 0, t, :, :], x, ACT.Copy).then_inc(xrows_high, 1)
            act.wait_ge(pT_ps, 1)
            nc.scalar.activation(pT, PS[:, 0:2, 0:TOK], ACT.Copy).then_inc(pT_ready, 1)
            nc.scalar.preload_act_table(ACT.Silu)
            act.wait_ge(rounds_ready, 1)
            rounds = act.value_load(rounds_i[0:1, 0:1], min_val=1, max_val=MAX_ROUNDS)

            def gathered(n, g):
                act.wait_ge(gather_ps, 4 * n + g + 1)
                nc.scalar.activation(xgT[:, 2 * g:2 * g + 2, :].rearrange("p k s -> p (k s)"), PS[:, g % 2, :], ACT.Copy)\
                    .then_inc(gathered_ready, 1)

            for g in range(4):
                gathered(0, g)
            with act.Fori(0, rounds) as r:
                with act.Fori(0, STEPS) as i:
                    n = r * STEPS + i

                    def silu(j):
                        act.wait_ge(up_done[j], n + 1)
                        nc.scalar.activation(act_h[:, j, :], PS[:, 2 + j, 0:HID], ACT.Silu).then_inc(silu_done, 1)

                    def hidden_T(j):
                        act.wait_ge(hidT_ps, 2 * n + j + 1)
                        nc.scalar.activation(hidT[:, j, :, :].rearrange("p k s -> p (k s)"),
                                             PS[:, 4, HID * j:HID * (j + 1)], ACT.Copy).then_inc(hidT_ready, 1)

                    def high(j, half):
                        act.wait_ge(y_ps, 4 * n + 2 * j + half + 1)
                        nc.scalar.activation(ysplit[:, j, 0, 512 * half:512 * half + 512], PS[:, 5 + half, :], ACT.Copy)\
                            .then_inc(y_high, 1)

                    silu(0)
                    hidden_T(0)
                    silu(1)
                    high(0, 0)
                    hidden_T(1)
                    high(0, 1)
                    gathered(n + 1, 0)
                    gathered(n + 1, 1)
                    high(1, 0)
                    gathered(n + 1, 2)
                    high(1, 1)
                    gathered(n + 1, 3)
            act.wait_ge(gate_loaded, 32)
            act.wait_ge(scat_ps, rounds * (6 * STEPS))
            for tile in range(2):
                for half in range(2):
                    nc.scalar.activation(split[:, 2 * tile + half, 0, :].rearrange("p (k n) -> p k n", k=4),
                                         gate_w[half][:, :, P * tile:P * (tile + 1)], ACT.Copy).then_inc(gate_high, 1)
            for t in range(3):
                act.wait_ge(ple_ps, t + 1)
                nc.scalar.activation(ple[0:ROWS[t], t, :], PS[0:ROWS[t], 2 + 2 * t:4 + 2 * t, :].rearrange("p b s -> p (b s)"),
                                     ACT.Copy).then_inc(ple_ready, 1)
            norm_std(4)
            high_xT(x2T_ps, x2T_high, lambda t: 2 * t)
            nc.scalar.preload_act_table(ACT.Sigmoid)

            def high_gate(tile, place, reused):
                for half in range(2):
                    if reused:
                        act.wait_ge(gate_used, 2 * tile - 4 + half + 1)
                    nc.scalar.activation(split[:, 2 * place + half, 0, :].rearrange("p (k n) -> p k n", k=4),
                                         gate_w[half][:, :, ds(P * tile, P)], ACT.Copy).then_inc(gate_high, 1)

            with act.Fori(0, KD // 2 - 1) as i:
                for b in range(2):
                    tile = 2 * i + b
                    high_gate(tile + 2, b, True)
                    act.wait_ge(gate_used, 2 * tile + 2)
                    nc.scalar.activation(sgT[:, ds(tile, 1), :].rearrange("p o t -> p (o t)"), PS[:, b, 0:TOK], ACT.Sigmoid)\
                        .then_inc(gate_sig, 1)
            for tile in range(KD - 2, KD):
                act.wait_ge(gate_used, 2 * tile + 2)
                nc.scalar.activation(sgT[:, tile, :], PS[:, tile % 2, 0:TOK], ACT.Sigmoid).then_inc(gate_sig, 1)

        @block.vector
        def _(dve):
            steps = {dve_step: 0, dve_last_step: 0}
            own = [dve_step]

            def step(ins):
                ins.then_inc(own[0], 1)
                steps[own[0]] += 1
                return steps[own[0]]

            def after(n):
                dve.wait_ge(own[0], n)

            def norm(x, width, vec, loaded, n):
                halves = width // 512
                for t in range(3):
                    for h in range(halves):
                        ins = nc.vector.bn_stats(stats[0:ROWS[t], t, h, :], x[0:ROWS[t], t, 512 * h:512 * h + 512])
                    done = step(ins)
                after(done)
                for t in range(3):
                    done = step(nc.vector.bn_aggr(meanvar[0:ROWS[t], t, :], stats[0:ROWS[t], t, 0:halves, :].rearrange("p a b -> p (a b)")))
                after(done)
                nc.vector.tensor_scalar(vareps[:, :], meanvar[:, :, 1], EPS, None, ALU.add).then_inc(var_ready, 1)
                dve.wait_ge(std_ready, n)
                after(step(nc.vector.reciprocal(rstd[:, :], std[:, :])))
                dve.wait_ge(*loaded)
                first = [0, 0, 0]

                def centre(t):
                    first[t] = step(nc.vector.scalar_tensor_tensor(
                        out=x[0:ROWS[t], t, :], in0=x[0:ROWS[t], t, :], scalar=meanvar[0:ROWS[t], t, 0:1],
                        in1=vec[0:ROWS[t], 0, :], op0=ALU.subtract, op1=ALU.mult))

                def scale(t):
                    after(first[t])
                    nc.vector.scalar_tensor_tensor(
                        out=x[0:ROWS[t], t, :], in0=x[0:ROWS[t], t, :], scalar=rstd[0:ROWS[t], t:t + 1],
                        in1=vec[0:ROWS[t], 1, :], op0=ALU.mult, op1=ALU.add).then_inc(ln_done, 1)

                centre(0)
                centre(1)
                scale(0)
                centre(2)
                scale(1)
                scale(2)

            def low(tile, half, place=None):
                place = (tile if place is None else place) % 4
                c = place // 2
                raw = wr[:, c, 4 * half:4 * half + 4, P * (place % 2):P * (place % 2) + P]
                parts = split[:, 2 * (place % 2) + half, :, :].rearrange("p h (k n) -> p h k n", k=4)
                dve.wait_ge(w_high, 2 * tile + half + 1)
                nc.vector.tensor_tensor(parts[:, 1, :, :], raw, parts[:, 0, :, :].bitcast(F32), ALU.subtract).then_inc(w_low, 1)

            def low_xT(high_sem, ready, bank):
                for t in range(3):
                    dve.wait_ge(high_sem, t + 1)
                    b = bank(t)
                    src = PS[:, b:b + 2, :].rearrange("p b (k s) -> p (b k) s", k=4)[:, :, 0:ROWS[t]]
                    nc.vector.tensor_tensor(xT[:, 1, :, cols(t)], src, xT[:, 0, :, cols(t)].bitcast(F32), ALU.subtract)\
                        .then_inc(ready, 1)

            after(step(nc.vector.memset(meanvar[:, :, :], 1.0)))
            dve.wait_ge(x_loaded, 32)
            norm(xs, D, lninvec, (lnin_loaded, 32), 1)
            low_xT(xT_high, xT_ready, lambda t: 2 * (t % 2))
            for tile in range(2):
                for half in range(2):
                    low(tile, half)

            for c in range(2):
                dve.wait_ge(prep_ps, c + 1)
                nc.vector.tensor_copy(ckT[:, :, P * c:P * (c + 1)], PS[:, 4 + c, :].rearrange("p (j s) -> p j s", j=4))\
                    .then_inc(prep_ready, 1)
            dve.wait_ge(prep_ps, 3)
            nc.vector.tensor_copy(wsT.rearrange("p g s -> p (g s)"), PS[:, 6:8, :].rearrange("p b s -> p (b s)"))\
                .then_inc(prep_ready, 1)
            dve.wait_ge(bias_loaded, 16 * 6)
            nc.vector.memset(prob1[0:64, :, 192:256], MASKED)
            masked = step(nc.vector.memset(prob0[0:64, :, 64:P], MASKED))
            after(masked)

            with dve.Fori(0, FIRST_STEPS) as i:
                for b in range(4):
                    for half in range(2):
                        low(4 * i + b + 2, half, b + 2)

            def scores(pr, ps, t):
                nc.vector.scalar_tensor_tensor(out=pr, in0=ps, scalar=SCALE, in1=pr, op0=ALU.mult, op1=ALU.add)\
                    .then_inc(score_ready, 1)

            dve.wait_ge(score_ps, 1)
            scores(prob1, PS[:, 0:4, :].rearrange("p b (i k) -> p (b i) k", i=2), 0)
            for t in range(3):
                dve.wait_ge(tok_ps, 4 + t)
                nc.vector.tensor_copy(v_tok[0:ROWS[t], t, :], PS[0:ROWS[t], (7, 4, 5)[t], :]).then_inc(tok_ready_dve, 1)
            dve.wait_ge(score_ps, 2)
            scores(prob0, PS[:, 0:2, :].rearrange("p b (i k) -> p (b i) k", i=4), 1)
            for w in range(2):
                dve.wait_ge(score_ps, 3 + w)
                for par in range(2):
                    nc.vector.scalar_tensor_tensor(
                        out=probs[:, 4 * par + 2 * w:4 * par + 2 * w + 2, :], in0=PS[0:DH, 4 + 2 * par:6 + 2 * par, 0:TOK],
                        scalar=SCALE, in1=probs[:, 4 * par + 2 * w:4 * par + 2 * w + 2, :], op0=ALU.mult, op1=ALU.add)\
                        .then_inc(score_ready, 1)
            group = ((prob1, P), (prob0, P), (probs, DH))

            def maximum(t):
                pr, n = group[t]
                m = step(nc.vector.tensor_reduce(smax[0:n, t, :], pr, AX.X, ALU.max))
                after(m)
                nc.vector.tensor_scalar(snegmax[0:n, t, :], smax[0:n, t, :], -1.0, None, ALU.mult).then_inc(negmax_ready, 1)

            def divide(t):
                pr, n = group[t]
                dve.wait_ge(exp_done, t + 1)
                after(step(nc.vector.reciprocal(srec[0:n, t, :], ssum[0:n, t, :])))
                nc.vector.tensor_tensor(pr, pr, srec[0:n, t, :].unsqueeze(2).to_broadcast([n, HEADS, pr.shape[2]]), ALU.mult)\
                    .then_inc(prob_ready, 1)

            dve.wait_ge(score_ready, 6)
            for i in range(4 * (CHUNK_STEPS - FIRST_STEPS)):
                if i < 3:
                    maximum(i)
                if i == 5:
                    divide(0)
                if i == 9:
                    divide(1)
                if i == 13:
                    dve.wait_ge(tok_ready_act, 6)
                    norm(vn, AW, mlpvec, (mlpvec_loaded, 32), 2)
                for half in range(2):
                    low(4 * FIRST_STEPS + i + 2, half)
            divide(2)
            dve.wait_ge(mix_ps, 1)
            dve.wait_ge(gelu_u, 1)
            nc.vector.tensor_tensor(obT, PS[:, 0:4, 0:TOK], obT, ALU.mult).then_inc(mix_ready, 1)
            dve.wait_ge(ob_high, 1)
            nc.vector.tensor_tensor(xT[:, 1, JW:KD, :], obT, xT[:, 0, JW:KD, :].bitcast(F32), ALU.subtract).then_inc(ob_low, 1)

            def sample_probT(j):
                dve.wait_ge(probT_ps, j + 1)
                b = 6 if j % 2 == 0 else 2
                ps = PS[:, b, 0:384].rearrange("p (e k) -> p e k", e=2)
                dst = probT[:, j, 2, :].rearrange("p (e k) -> p e k", e=2)
                nc.vector.tensor_copy(dst[:, :, 0:128], ps[:, :, 0:128])
                nc.vector.tensor_copy(dst[0:DH, :, 128:192], ps[0:DH, :, 128:192]).then_inc(probT_dve, 1)

            def attention_out(j):
                dve.wait_ge(oa_high, j + 1)
                nc.vector.tensor_tensor(xT[:, 1, j, :], PS[:, 7 if j % 2 == 0 else 3, 0:TOK], xT[:, 0, j, :].bitcast(F32),
                                        ALU.subtract).then_inc(oa_ready, 1)

            sample_probT(0)
            sample_probT(1)
            for j in range(4):
                attention_out(j)
                if j < 2:
                    sample_probT(j + 2)
            dve.wait_ge(sig_done, 1)
            base = steps[dve_step]
            with dve.Fori(0, 2) as i:
                for b in range(4):
                    tile = 4 * i + b
                    for half in range(2):
                        low(BRANCH_T + tile + 2, half, b + 2)
                    ga = zt[:, ds(V0 + 8 * i + b, 1), :].rearrange("p o t -> p (o t)")
                    gb = zt[:, ds(GB0 + tile, 1), :].rearrange("p o t -> p (o t)")
                    m = mT[:, ds(tile, 1), :].rearrange("p o t -> p (o t)")
                    dve.wait_ge(half_used, 2 * (BRANCH_T + tile) + 2)
                    nc.vector.tensor_tensor(ga, PS[:, 2 * b, 0:TOK], ga, ALU.mult)
                    nc.vector.tensor_tensor(gb, PS[:, 2 * b + 1, 0:TOK], gb, ALU.mult).then_inc(dve_step, 1)
                    dve.wait_ge(dve_step, base + tile + 1)
                    nc.vector.tensor_tensor(m, ga, gb, ALU.add).then_inc(branch_free, 1)
            steps[dve_step] = base + KD
            for j in range(2):
                dve.wait_ge(m_high, j + 1)
                k = slice(4 * j, 4 * j + 4)
                nc.vector.tensor_tensor(xT[:, 1, k, :], mT[:, k, :], xT[:, 0, k, :].bitcast(F32), ALU.subtract).then_inc(m_low, 1)
            with dve.Fori(0, 2) as i:
                for b in range(4):
                    for half in range(2):
                        low(OUT_T + 4 * i + b + 2, half, b + 2)
            for t in range(3):
                dve.wait_ge(out_ps, t + 1)
                b = (4, 6, 0)[t]
                x = xs[0:ROWS[t], t, :]
                nc.vector.scalar_tensor_tensor(out=x, in0=x, scalar=ALPHA, in1=PS[0:ROWS[t], b:b + 2, :].rearrange("p b s -> p (b s)"),
                                               op0=ALU.mult, op1=ALU.add).then_inc(residual, 1)
            dve.wait_ge(residual, 3)
            norm(xs, D, lnvec, (route_loaded, 64), 3)
            low_xT(x1T_high, x1T_ready, lambda t: 2 * t)
            for tile in range(SHARED_T + 2, SHARED_T + 4):
                for half in range(2):
                    low(tile, half)

            def stage(f):
                done = [step(f(t, ROWS[t])) for t in range(3)]
                after(done[-1])

            gm = lambda t, n: gmax[0:n, t, :]
            stage(lambda t, n: nc.vector.memset(rsmall[:, t, :], MASKED))
            for t in range(3):
                dve.wait_ge(score_sig, t + 1)
                m = step(nc.vector.tensor_tensor(sel[0:ROWS[t], t, :], score[0:ROWS[t], t, :], rbias[0:ROWS[t], :], ALU.add))
            after(m)
            for t in range(3):
                for g in range(GROUPS):
                    last = nc.vector.max(out=gmax[0:ROWS[t], t, 8 * g:8 * g + 8],
                                         in_=sel[0:ROWS[t], t, PER_GROUP * g:PER_GROUP * (g + 1)])
                m = step(last)
            after(m)
            stage(lambda t, n: nc.vector.tensor_tensor(rsmall[0:n, t, 0:8], gmax[0:n, t, 0:64:8], gmax[0:n, t, 1:64:8], ALU.add))
            stage(lambda t, n: nc.vector.max(out=rsmall[0:n, t, 16:24], in_=rsmall[0:n, t, 0:8]))
            stage(lambda t, n: nc.vector.memset(rsmall[0:n, t, 16 + KEEP_GROUPS:24], MASKED))
            stage(lambda t, n: nc.vector.match_replace(out=rsmall[0:n, t, 32:44], in_to_replace=rsmall[0:n, t, 16:24],
                                                       in_values=rsmall[0:n, t, 0:12], imm_value=2 * MASKED))
            stage(lambda t, n: nc.vector.tensor_scalar(rsmall[0:n, t, 48:56], rsmall[0:n, t, 32:40], 1.5 * MASKED, MASKED,
                                                       ALU.is_ge, ALU.mult))
            stage(lambda t, n: nc.vector.tensor_tensor(
                msel[0:n, t, :].rearrange("p (g i) -> p g i", g=GROUPS), sel[0:n, t, :].rearrange("p (g i) -> p g i", g=GROUPS),
                rsmall[0:n, t, 48:56].unsqueeze(2).to_broadcast([n, GROUPS, PER_GROUP]), ALU.add))
            stage(lambda t, n: nc.vector.max(out=rsmall[0:n, t, 16:24], in_=msel[0:n, t, :]))
            stage(lambda t, n: nc.vector.match_replace(out=replaced[0:n, t, :], in_to_replace=rsmall[0:n, t, 16:24],
                                                       in_values=msel[0:n, t, :], imm_value=3 * MASKED))
            stage(lambda t, n: nc.vector.tensor_scalar(maskf[0:n, t, :], replaced[0:n, t, :], 2 * MASKED, None, ALU.is_lt))
            for t in range(3):
                nc.vector.tensor_copy(mask[0:ROWS[t], t, :], maskf[0:ROWS[t], t, :]).then_inc(mask_ready, 1)
            stage(lambda t, n: nc.vector.tensor_tensor(wt[0:n, t, :], maskf[0:n, t, :], score[0:n, t, :], ALU.mult))
            stage(lambda t, n: nc.vector.tensor_reduce(rsmall[0:n, t, 60:61], wt[0:n, t, :], AX.X, ALU.add))
            stage(lambda t, n: nc.vector.reciprocal(rsmall[0:n, t, 61:62], rsmall[0:n, t, 60:61]))
            for at, k in ((0, NE), (NE, 4)):
                stage(lambda t, n: nc.vector.tensor_scalar(attrs[0:n, t, at:at + k, 0], wt[0:n, t, 0:k], rsmall[0:n, t, 61:62],
                                                           ROUTED_SCALE, ALU.mult, ALU.mult))
            for m in range(2):
                dve.wait_ge(shared_silu, m + 1)
                dve.wait_ge(half_used, 2 * SHARED_T + 2 * m + 6)
                nc.vector.tensor_tensor(hsT[:, m, :], hsT[:, m, :], PS[:, 2 + m, 0:TOK], ALU.mult).then_inc(shared_hid, 1)
            dve.wait_ge(pos_ps, 1)
            stage(lambda t, n: nc.vector.scalar_tensor_tensor(out=wres[0:n, t, :], in0=PS[0:n, 7, NE * t:NE * (t + 1)], scalar=1.0,
                                                              in1=maskf[0:n, t, :], op0=ALU.add, op1=ALU.mult))
            stage(lambda t, n: nc.vector.tensor_scalar(pos[0:n, t, 0:NE], wres[0:n, t, :], -1.0, None, ALU.add))
            stage(lambda t, n: nc.vector.tensor_scalar(pos[0:n, t, NE:NE + 8], wres[0:n, t, 0:8], -1.0 - SLOTS, None, ALU.add))
            after(step(nc.vector.tensor_reduce(rounds_f[:, 0:1], PS[0:1, 7, 3 * NE:4 * NE], AX.X, ALU.max)))
            dve.wait_ge(const_ready, 2)
            after(step(nc.vector.tensor_scalar(round_gt[:, :], round_thr[:, :], rounds_f[:, 0:1], None, ALU.is_lt)))
            after(step(nc.vector.tensor_reduce(rounds_f[:, 1:2], round_gt[:, :], AX.X, ALU.add)))
            nc.vector.tensor_scalar(rounds_i[:, :], rounds_f[:, 1:2], 1.0, None, ALU.add).then_inc(rounds_ready, 1)

            def picks(expert):
                for t in range(3):
                    k = ROWS[t]
                    nc.vector.tensor_tensor(
                        pick[0:k, t, :].rearrange("p (e s) -> p e s", s=SLOTS),
                        iota_slot[0:k, :].unsqueeze(1).to_broadcast([k, 4, SLOTS]),
                        pos[0:k, t, ds(expert, 4)].unsqueeze(2).to_broadcast([k, 4, SLOTS]), ALU.is_equal).then_inc(pick_ready, 1)

            def slot_values():
                for e in range(2):
                    h = slice(64 * e, 64 * e + 64)
                    nc.vector.tensor_copy(slots[h, :, :], PS[h, 4, 0:8].rearrange("p (j f) -> p j f", j=2)[:, :, 2 * e:2 * e + 2])\
                        .then_inc(slots_ready, 1)

            picks(0)
            for t in range(3):
                dve.wait_ge(xrows_ready, t + 1)
                dve.wait_ge(shared_ps, t + 1)
                x = acc[0:ROWS[t], t, :]
                nc.vector.scalar_tensor_tensor(out=x, in0=x, scalar=ALPHA, in1=PS[0:ROWS[t], 2 * t:2 * t + 2, :].rearrange("p b s -> p (b s)"),
                                               op0=ALU.mult, op1=ALU.add).then_inc(acc_init, 1)
            dve.wait_ge(acc_init, 3)
            dve.wait_ge(rounds_ready, 1)
            rounds = dve.value_load(rounds_i[0:1, 0:1], min_val=1, max_val=MAX_ROUNDS)
            dve.wait_ge(table_ps, 1)
            slot_values()
            picks(4)
            with dve.Fori(0, rounds) as r:
                dve.wait_ge(pos_moved, r + 1)
                dve.sem_inc(dve_rounds, 1)
                with dve.Fori(0, STEPS) as i:
                    n = r * STEPS + i
                    dve.wait_ge(slots_ready, 2 * n + 2)
                    dve.wait_ge(acc_added, 6 * n + 1)
                    for j in range(2):
                        nc.vector.tensor_scalar(scat[:, j, :], iota_tok, slots[:, j, 1:2], None, ALU.is_equal)\
                            .then_inc(scat_ready, 1)
                    for j in range(2):
                        dve.wait_ge(silu_done, 2 * n + j + 1)
                        nc.vector.scalar_tensor_tensor(out=hid[:, j, :], in0=PS[:, 2 + j, HID:2 * HID],
                                                       scalar=slots[:, j, 0:1], in1=act_h[:, j, :],
                                                       op0=ALU.mult, op1=ALU.mult).then_inc(hid_ready, 1)
                    for j in range(2):
                        for half in range(2):
                            dve.wait_ge(y_high, 4 * n + 2 * j + half + 1)
                            c = slice(512 * half, 512 * half + 512)
                            nc.vector.tensor_tensor(ysplit[:, j, 1, c], PS[:, 5 + half, :], ysplit[:, j, 0, c].bitcast(F32),
                                                    ALU.subtract).then_inc(y_low, 1)
                    dve.wait_ge(table_ps, n + 2)
                    slot_values()
                    picks(4 * i + 8)
                    for q in range(6):
                        t, half = q // 2, q % 2
                        dve.wait_ge(scat_ps, 6 * n + q + 1)
                        a = acc[0:ROWS[t], t, 512 * half:512 * half + 512]
                        nc.vector.tensor_tensor(a, a, PS[0:ROWS[t], SCAT_BANK[q], :], ALU.add).then_inc(acc_added, 1)
                dve.wait_ge(pick_ready, (r + 1) * (3 * STEPS) + 6)
                for t in range(3):
                    last = nc.vector.tensor_scalar(pos[0:ROWS[t], t, :], pos[0:ROWS[t], t, :], -float(SLOTS), None, ALU.add)
                last.then_inc(pos_moved, 1)
            dve.wait_ge(acc_added, rounds * (6 * STEPS) + 1)
            own[0] = dve_last_step

            def low_gate(tile, place):
                for half in range(2):
                    parts = split[:, 2 * place + half, :, :].rearrange("p h (k n) -> p h k n", k=4)
                    dve.wait_ge(gate_high, 2 * tile + half + 1)
                    nc.vector.tensor_tensor(parts[:, 1, :, :], gate_w[half][:, :, ds(P * tile, P)],
                                            parts[:, 0, :, :].bitcast(F32), ALU.subtract).then_inc(gate_low, 1)

            norm(xs, D, ln2vec, (ln2_loaded, 32), 4)
            low_gate(0, 0)
            low_xT(x2T_high, x2T_ready, lambda t: 2 * t)
            low_gate(1, 1)
            with dve.Fori(0, KD // 2 - 1) as i:
                for b in range(2):
                    low_gate(2 * i + b + 2, b)
            dve.wait_ge(ple_ready, 3)
            for half in range(2):
                c = slice(512 * half, 512 * half + 512)
                for t in range(3):
                    dve.wait_ge(gate_rows, 3 * half + t + 1)
                    p = ple[0:ROWS[t], t, c]
                    after(step(nc.vector.tensor_tensor(p, PS[0:ROWS[t], 2 + 3 * half + t, :], p, ALU.mult)))
                    nc.vector.tensor_tensor(xs[0:ROWS[t], t, c], xs[0:ROWS[t], t, c], p, ALU.add).then_inc(y_ready, 1)

        @block.tensor
        def _(pe):
            def transpose_rows(src, t, bank, signal):
                for k in range(KD):
                    ins = pe.transpose(PS[:, bank + k // 4, P * (k % 4):P * (k % 4) + ROWS[t]],
                                       src[0:ROWS[t], t, k::KD], ident[0:ROWS[t], 0:ROWS[t]])
                ins.then_inc(signal, 1)

            pe.wait_ge(const_ready, 1)
            for t in range(3):
                pe.wait_ge(ln_done, t + 1)
                if t == 2:
                    pe.wait_ge(xT_ready, 1)
                transpose_rows(xs, t, 2 * (t % 2), xT_ps)
            pe.wait_ge(cache_loaded, 32)
            for c in range(2):
                for j in range(JW):
                    ins = pe.transpose(PS[:, 4 + c, P * j:P * (j + 1)], ck[:, c, P * j:P * (j + 1)], ident[:, :])
                ins.then_inc(prep_ps, 1)
            pe.wait_ge(wsmask_ready, 1)
            for g in range(8):
                ins = pe.transpose(PS[:, 6 + g // 4, P * (g % 4):P * (g % 4 + 1)], ws[:, g, :], ident[:, :])
            ins.then_inc(prep_ps, 1)
            pe.wait_ge(xT_ready, 3)
            pe.sem_inc(proj_free, 4)

            def products(out, s, k0, start, stop, lhs=0):
                for k in range(4):
                    w = split[:, s, :, P * k:P * (k + 1)]
                    for wp, xp in ((0, 0), (0, 1), (1, 0)):
                        ins = pe.matmul(out, w[:, wp, :], xT[:, xp, k0 + k, :], start=(start and k == 0 and (wp, xp) == (0, 0)),
                                        stop=(stop and k == 3 and wp == 1))
                return ins

            def project(first, end, free, freed=0):
                with pe.Fori(first, end) as i:
                    for b in range(4):
                        pe.wait_ge(free, 4 * (i - first + freed) + b + 1)
                        for half in range(2):
                            pe.wait_ge(w_low, 2 * (4 * i + b) + half + 1)
                            products(PS[:, b, 0:TOK], 2 * (b % 2) + half, 4 * half, half == 0, half == 1).then_inc(half_used, 1)

            def rows_of(first, t, bank):
                for j in range(JW):
                    ins = pe.transpose(PS[0:ROWS[t], bank, P * j:P * (j + 1)], zt[:, first + j, cols(t)], ident[:, :])
                ins.then_inc(tok_ps, 1)

            def head(tile, h, c):
                return zt[64 * (h % 2):64 * (h % 2) + 64, tile + h // 2, c]

            project(0, FIRST_STEPS, proj_free)
            pe.wait_ge(proj_free, 4 + 4 * FIRST_STEPS)
            pe.wait_ge(prep_ready, 3)
            for t in range(3):
                rows_of(K0, t, 4 + t)
            for h in range(HEADS):
                par, i = h % 2, h // 2
                ins = pe.matmul(PS[:, 2 * par + i // 2, 256 * (i % 2):256 * (i % 2) + 256],
                                head(Q0, h, slice(P, 2 * P)), head(K0, h, slice(0, 2 * P)), start=True, stop=True)
            ins.then_inc(score_ps, 1)
            for t in range(3):
                if t:
                    pe.wait_ge(tok_ready_act, t)
                rows_of(V0, t, (7, 4, 5)[t])
            for t in range(3):
                if t < 2:
                    pe.wait_ge(*((tok_ready_act, 3), (tok_ready_dve, 1))[t])
                else:
                    pe.wait_ge(tok_ready_dve, 2)
                rows_of(S0, t, (6, 7, 4)[t])
            pe.wait_ge(score_ready, 1)
            for h in range(HEADS):
                ins = pe.matmul(PS[:, h % 2, P * (h // 2):P * (h // 2 + 1)],
                                head(Q0, h, slice(0, P)), head(K0, h, slice(0, P)), start=True, stop=True)
            ins.then_inc(score_ps, 1)
            pe.wait_ge(tok_ready_act, 6)
            pe.wait_ge(tok_ready_dve, 3)
            for w in range(2):
                if w:
                    pe.wait_ge(score_ready, 4)
                for h in range(4 * w, 4 * w + 4):
                    par, i = h % 2, h // 2
                    for c, (key, n) in enumerate(((ckT[64 * par:64 * par + 64, i, :], 256), (head(K0, h, slice(256, TOK)), DH))):
                        ins = pe.matmul(PS[0:DH, 4 + 2 * par + i % 2, 256 * c:256 * c + n], head(Q0, h, slice(256, TOK)), key,
                                        start=True, stop=True)
                ins.then_inc(score_ps, 1)
            pe.wait_ge(score_ready, 2)
            project(FIRST_STEPS, CHUNK_STEPS, proj_free, FIRST_STEPS)
            pe.wait_ge(ln_done, 6)
            pe.wait_ge(bs_loaded, 16)
            pe.wait_ge(proj_free, 4 + 4 * CHUNK_STEPS)
            for g in range(8):
                par = slice(64 * (g % 2), 64 * (g % 2) + 64)
                for t in range(3):
                    n = ROWS[t]
                    pe.matmul(PS[par, g // 2, cols(t)], ones[0:1, :], bsrow[0:1, g, 0:n], start=True, stop=False)
                    ins = pe.matmul(PS[par, g // 2, cols(t)], vn[0:n, t, 64 * g:64 * g + 64], wsT[0:n, g, 0:n],
                                    start=False, stop=True)
            ins.then_inc(mix_ps, 1)

            def turn_probs(j):
                b = 4 if j % 2 == 0 else 0
                for e in range(2):
                    h = 4 * e + j
                    pe.transpose(PS[:, b + e, 0:P], prob0[:, h, :], ident[:, :])
                    for c in range(2):
                        pe.transpose(PS[:, b + e, P * (c + 1):P * (c + 2)], prob1[:, h, P * c:P * (c + 1)], ident[:, :])
                        pe.transpose(PS[:, b + 2, 192 * e + 64 * c:192 * e + 64 * c + 64], probs[:, h, P * c:P * (c + 1)],
                                     ident[0:DH, 0:DH])
                    ins = pe.transpose(PS[0:DH, b + 2, 192 * e + 128:192 * e + 192], probs[:, h, 256:TOK], ident[0:DH, 0:DH])
                ins.then_inc(probT_ps, 1)

            def attend(j):
                pe.wait_ge(probT_act, j + 1)
                pe.wait_ge(probT_dve, j + 1)
                bank = 7 if j % 2 == 0 else 3
                if j >= 2:
                    pe.wait_ge(oa_ready, j - 1)
                for e in range(2):
                    rows, c = slice(64 * e, 64 * e + 64), slice(64 * (2 * j + e), 64 * (2 * j + e) + 64)
                    pt, ps = probT[:, j, e, :], probT[:, j, 2, :]
                    pe.matmul(PS[rows, bank, 0:P], v_tok[:, 0, c], pt[:, 0:P], start=True, stop=True)
                    pe.matmul(PS[rows, bank, P:2 * P], v_tok[:, 0, c], pt[:, P:2 * P], start=True, stop=False)
                    pe.matmul(PS[rows, bank, P:2 * P], v_tok[:, 1, c], pt[:, 2 * P:3 * P], start=False, stop=True)
                    o = 192 * e
                    pe.matmul(PS[rows, bank, 256:TOK], cv[:, 0, c], ps[:, o:o + 64], start=True, stop=False)
                    pe.matmul(PS[rows, bank, 256:TOK], cv[:, 1, c], ps[:, o + 64:o + 128], start=False, stop=False)
                    ins = pe.matmul(PS[rows, bank, 256:TOK], v_tok[0:DH, 2, c], ps[0:DH, o + 128:o + 192], start=False, stop=True)
                ins.then_inc(oa_ps, 1)

            pe.wait_ge(prob_ready, 3)
            turn_probs(0)
            pe.wait_ge(mix_ready, 1)
            turn_probs(1)
            for j in range(4):
                attend(j)
                if j < 2:
                    turn_probs(j + 2)
            pe.wait_ge(oa_ready, 4)
            pe.sem_inc(branch_free, 4)
            pe.wait_ge(ob_low, 1)
            with pe.Fori(0, 2) as i:
                for b in range(4):
                    pe.wait_ge(branch_free, 4 * i + b + 1)
                    for half in range(2):
                        pe.wait_ge(w_low, 2 * BRANCH_T + 8 * i + 2 * b + half + 1)
                        products(PS[:, 2 * b + half, 0:TOK], 2 * (b % 2) + half, 4 * half, True, True).then_inc(half_used, 1)
            pe.wait_ge(branch_free, 4 + KD)
            pe.sem_inc(out_free, 4)
            pe.wait_ge(m_low, 2)
            project(OUT_T // 4, OUT_T // 4 + 2, out_free)
            pe.wait_ge(out_free, 4 + KD)
            for t in range(3):
                for j in range(KD):
                    ins = pe.transpose(PS[0:ROWS[t], (4, 6, 0)[t] + j // 4, P * (j % 4):P * (j % 4 + 1)], woT[:, j, cols(t)], ident[:, :])
                ins.then_inc(out_ps, 1)
            pe.wait_ge(residual, 3)
            for t in range(3):
                pe.wait_ge(ln_done, 7 + t)
                transpose_rows(xs, t, 2 * t, x1T_ps)
            pe.wait_ge(route_loaded, 64)
            for t in range(3):
                pe.wait_ge(x1T_ready, t + 1)
                for k in range(KD):
                    for part in range(2):
                        ins = pe.matmul(PS[0:ROWS[t], 6, NE * t:NE * (t + 1)], xT[:, part, k, cols(t)].bitcast(F32), rw[:, k, :],
                                        start=(k == 0 and part == 0), stop=(k == KD - 1 and part == 1))
                ins.then_inc(logits_ps, 1)
            for b in range(4):
                for half in range(2):
                    pe.wait_ge(w_low, 2 * (SHARED_T + b) + half + 1)
                    products(PS[:, b, 0:TOK], 2 * (b % 2) + half, 4 * half, half == 0, half == 1).then_inc(half_used, 1)
            for t in range(3):
                pe.wait_ge(mask_ready, t + 1)
                for u in range(t + 1):
                    lhs = tri[0:ROWS[u], 0:ROWS[t]] if u == t else onesb[:, 0:ROWS[t]]
                    pe.matmul(PS[0:ROWS[t], 7, NE * t:NE * (t + 1)], lhs, mask[0:ROWS[u], u, :], start=(u == 0), stop=(u == t))
            for t in range(3):
                ins = pe.matmul(PS[:, 7, 3 * NE:4 * NE], onesb[0:ROWS[t], :], mask[0:ROWS[t], t, :], start=(t == 0), stop=(t == 2))
            ins.then_inc(pos_ps, 1)
            pe.wait_ge(sw2_loaded, 16)
            pe.wait_ge(shared_hid, 2)
            for t in range(3):
                for half in range(2):
                    for m in range(2):
                        ins = pe.matmul(PS[0:ROWS[t], 2 * t + half, :], hsT[:, m, cols(t)], sw2[:, m, 512 * half:512 * half + 512],
                                        start=(m == 0), stop=(m == 1))
                ins.then_inc(shared_ps, 1)
            pe.wait_ge(ple_loaded, 48)
            pe.wait_ge(acc_init, 1)
            for t in range(3):
                for m in range(2):
                    ins = pe.transpose(PS[:, m, cols(t)], p_tok[0:ROWS[t], t, P * m:P * (m + 1)], ident[0:ROWS[t], 0:ROWS[t]])
            ins.then_inc(pT_ps, 1)
            pe.wait_ge(rounds_ready, 1)
            pe.wait_ge(pT_ready, 1)
            pe.wait_ge(acc_init, 3)
            pe.sem_inc(acc_added, 1)
            pe.sem_inc(pos_moved, 1)

            def gather(n, g):
                for k in range(2):
                    for t in range(3):
                        for part in range(2):
                            ins = pe.matmul(PS[:, g % 2, 256 * k:256 * k + 256], xrows[0:ROWS[t], part, t, 2 * g + k, :],
                                            pick[0:ROWS[t], t, :], start=(t == 0 and part == 0), stop=(t == 2 and part == 1))
                ins.then_inc(gather_ps, 1)

            def slot_table(expert):
                for j in range(2):
                    for t in range(3):
                        ins = pe.matmul(PS[:, 4, 4 * j:4 * j + 4], pick[0:ROWS[t], t, P * j:P * (j + 1)].bitcast(F32),
                                        attrs[0:ROWS[t], t, ds(expert + 2 * j, 2), :].rearrange("p e f -> p (e f)"),
                                        start=(t == 0), stop=(t == 2))
                ins.then_inc(table_ps, 1)

            pe.wait_ge(pick_ready, 3)
            pe.wait_ge(xrows_ready, 3)
            for g in range(4):
                if g >= 2:
                    pe.wait_ge(gathered_ready, g - 1)
                gather(0, g)
            slot_table(0)
            rounds = pe.value_load(rounds_i[0:1, 0:1], min_val=1, max_val=MAX_ROUNDS)
            with pe.Fori(0, rounds) as r:
                with pe.Fori(0, STEPS) as i:
                    n = r * STEPS + i

                    def up(j, ks):
                        for k in ks:
                            for e in range(2):
                                c = slice(64 * e, 64 * e + 64)
                                ins = pe.matmul(PS[c, 2 + j, :], xgT[:, k, P * j + 64 * e:P * j + 64 * e + 64], w13(j, e, k),
                                                start=(k == 0), stop=(k == KD - 1))
                        if KD - 1 in ks:
                            ins.then_inc(up_done[j], 1)

                    def turn_hidden(j):
                        pe.wait_ge(hid_ready, 2 * n + j + 1)
                        for k in range(2):
                            ins = pe.transpose(PS[:, 4, HID * j + P * k:HID * j + P * (k + 1)], hid[:, j, k::2], ident[:, :])
                        ins.then_inc(hidT_ps, 1)

                    def down(j, half):
                        for k in range(2):
                            for e in range(2):
                                c = slice(64 * e, 64 * e + 64)
                                ins = pe.matmul(PS[c, 5 + half, :], hidT[:, j, k, c], w2(j, e, k, half), start=(k == 0), stop=(k == 1))
                        ins.then_inc(y_ps, 1)

                    pe.wait_ge(gathered_ready, 4 * n + 4)
                    pe.wait_ge(acc_added, 6 * n + 1)
                    pe.wait_ge(w13_loaded[0], 64 * (n + 1))
                    up(0, range(KD))
                    pe.wait_ge(w13_loaded[1], 64 * (n + 1))
                    up(1, range(4))
                    turn_hidden(0)
                    up(1, range(4, KD))
                    pe.wait_ge(hidT_ready, 2 * n + 1)
                    pe.wait_ge(w2_loaded[0], 32 * (n + 1))
                    down(0, 0)
                    turn_hidden(1)
                    down(0, 1)
                    pe.wait_ge(pick_ready, 3 * n + 6)
                    gather(n + 1, 0)
                    gather(n + 1, 1)
                    pe.wait_ge(hidT_ready, 2 * n + 2)
                    pe.wait_ge(w2_loaded[1], 32 * (n + 1))
                    for half in range(2):
                        pe.wait_ge(y_high, 4 * n + half + 1)
                        pe.wait_ge(y_low, 4 * n + half + 1)
                        down(1, half)
                        pe.wait_ge(gathered_ready, 4 * n + 5 + half)
                        gather(n + 1, 2 + half)
                    slot_table(4 * i + 4)
                    pe.wait_ge(scat_ready, 2 * n + 2)
                    pe.wait_ge(y_high, 4 * n + 4)
                    pe.wait_ge(y_low, 4 * n + 4)
                    for q in range(6):
                        t, half = q // 2, q % 2
                        if q >= 3:
                            pe.wait_ge(acc_added, 6 * n + q - 1)
                        for j in range(2):
                            for part in range(2):
                                ins = pe.matmul(PS[:, SCAT_BANK[q], :], scat[:, j, P * t:P * (t + 1)],
                                                ysplit[:, j, part, 512 * half:512 * half + 512],
                                                start=(j == 0 and part == 0), stop=(j == 1 and part == 1))
                        ins.then_inc(scat_ps, 1)
            pe.wait_ge(gathered_ready, rounds * (4 * STEPS) + 4)
            pe.wait_ge(slots_ready, rounds * (2 * STEPS) + 2)
            pe.wait_ge(acc_added, rounds * (6 * STEPS) + 1)
            for t in range(3):
                for half in range(2):
                    for m in range(2):
                        ins = pe.matmul(PS[0:ROWS[t], 2 + 2 * t + half, :], pT[:, m, cols(t)], proj_w[:, m, 512 * half:512 * half + 512],
                                        start=(m == 0), stop=(m == 1))
                ins.then_inc(ple_ps, 1)
            for t in range(3):
                pe.wait_ge(ln_done, 10 + t)
                if t:
                    pe.wait_ge(ple_ready, t)
                transpose_rows(xs, t, 2 * t, x2T_ps)
            pe.wait_ge(x2T_ready, 3)
            pe.sem_inc(gate_sig, 2)
            for h in range(2):
                with pe.Fori(2 * h, 2 * h + 2) as i:
                    for b in range(2):
                        tile = 2 * i + b
                        pe.wait_ge(gate_sig, tile + 1)
                        for half in range(2):
                            pe.wait_ge(gate_low, 2 * tile + half + 1)
                            products(PS[:, b, 0:TOK], 2 * b + half, 4 * half, half == 0, half == 1).then_inc(gate_used, 1)
                pe.wait_ge(gate_sig, 2 + 4 * h + 4)
                for t in range(3):
                    for j in range(4):
                        ins = pe.transpose(PS[0:ROWS[t], 2 + 3 * h + t, P * j:P * (j + 1)], sgT[:, 4 * h + j, cols(t)], ident[:, :])
                    ins.then_inc(gate_rows, 1)


_INS = ["x_prompt", "x_sample", "cache_attn_k", "cache_attn_v", "p_prompt", "p_sample", "ln_in_g", "ln_in_b", "w_in",
        "attn_rel_bias", "mlp_ln_g", "mlp_ln_b", "mlp_w_s", "mlp_b_s", "w_branch_a", "w_branch_b", "w_out", "ln1_g", "ln1_b",
        "router_w", "router_bias", "exp_w1", "exp_w3", "exp_w2", "shared_w1", "shared_w3", "shared_w2", "ln2_g", "ln2_b",
        "ple_w_gate", "ple_w_proj"]


def kernel(**inputs):
    import numpy as _np
    import concourse.bacc as _bacc
    from concourse import mybir as _mybir
    from concourse.bass_utils import run_bass_kernel_spmd as _run

    x, s = inputs["x_prompt"].shape, inputs["x_sample"].shape
    kv = inputs["cache_attn_k"].shape
    width = inputs["mlp_ln_g"].shape[-1]
    outs = [x, s, (1, x[0], x[1], *kv[3:]), (1, x[0], x[1], *kv[3:]), (1, s[0], s[1], *kv[3:]), (1, s[0], s[1], *kv[3:]),
            (1, x[0], 128, width), (1, s[0], s[1], width)]
    nc = _bacc.Bacc("TRN2", target_bir_lowering=False, num_devices=1)
    arrays, args = {}, []
    for name in _INS:
        a = _np.ascontiguousarray(inputs[name])
        arrays[f"in_{name}_dram"] = a
        args.append(nc.dram_tensor(f"in_{name}_dram", a.shape, _mybir.dt.from_np(a.dtype), kind="ExternalInput").ap())
    for i, shape in enumerate(outs):
        args.append(nc.dram_tensor(f"out_{i}_dram", shape, _mybir.dt.float32, kind="ExternalOutput").ap())
    trunk_step(nc, *args)
    r = _run(nc, [arrays], core_ids=[0])
    return tuple(r.results[0][f"out_{i}_dram"] for i in range(len(outs)))
```

```python
from contextlib import ExitStack

import concourse.bass as bass
from concourse import mybir

F32 = mybir.dt.float32
F32R = mybir.dt.float32r
BF16 = mybir.dt.bfloat16
I32 = mybir.dt.int32
ALU = mybir.AluOpType
ACT = mybir.ActivationFunctionType
AX = mybir.AxisListType
ds = bass.ds

P = 128
ROWS = (128, 128, 64)
TOK = sum(ROWS)
HEADS, DH = 8, 64
EPS = 1e-5
ALPHA = 2.0 ** 0.25
SCALE = DH ** -0.5
ROUTED_SCALE = 2.5
MASKED = -1.0e30


def trunk_step(nc, x_prompt, x_sample, cache_k, cache_v, p_prompt, p_sample, ln_in_g, ln_in_b, w_in,
               rel_bias, mlp_g, mlp_b, mlp_w_s, mlp_b_s, w_a, w_b, w_out, ln1_g, ln1_b, router_w,
               router_bias, exp_w1, exp_w3, exp_w2, sh_w1, sh_w3, sh_w2, ln2_g, ln2_b, ple_gate,
               ple_proj, y_prompt, y_sample, new_k_prompt, new_v_prompt, new_k_sample, new_v_sample,
               new_mlp_prompt, new_mlp_sample):
    D = x_prompt.shape[2]
    KD = D // P
    N_IN = w_in.shape[2]
    CH = 256
    AW = HEADS * DH
    JW = AW // P
    NE = router_w.shape[2]
    HID = exp_w1.shape[3]
    GROUPS, PER_GROUP, KEEP_GROUPS = 8, NE // 8, 4
    SLOTS = 64
    PAIRS = NE // 2
    STEPS = PAIRS // 2
    MAX_ROUNDS = -(-TOK // SLOTS)
    TP = 3 * P
    REL = rel_bias.shape[2]
    PAD = 64
    PEXP = 2 * KD * HID + 2 * D
    Q0, K0, V0, U0, S0 = 0, 4, 8, 12, 16
    ZT = 28
    GATE_A = [V0 + j for j in range(4)] + [S0 + j for j in range(4)]
    GB0 = 20
    W_TILES = N_IN // P
    BRANCH_T = W_TILES
    OUT_T = BRANCH_T + KD
    SHARED_T = OUT_T + KD

    with ExitStack() as ctx:
        def sb(name, shape, dt=F32):
            return ctx.enter_context(nc.sbuf_tensor(name, shape, dt))

        def sem(name):
            return ctx.enter_context(nc.semaphore(name))

        ring = sb("expert_ring", [P, 2 * 2 * PEXP])
        z = sb("z", [P, ZT * TOK])
        xs = sb("xs", [P, 3, D])
        parts = sb("parts", [P, 2 * 3 * D], F32R)
        xT = parts[:, 0:2 * KD * TOK].rearrange("p (h k t) -> p h k t", h=2, k=KD)
        xrows = parts[:, :].rearrange("p (h t k c) -> p h t k c", h=2, t=3, k=KD)
        wr = sb("weight_ring", [P, 2, KD, CH])
        split = sb("split", [P, 4, 2, 4 * P], F32R)
        ysplit = split[:, :, :, :].rearrange("p (a b) h c -> p a (b h c)", a=2).rearrange("p a (h c) -> p a h c", h=2)
        marks = sb("marks", [P, 2 * TP + 3 * 4 * SLOTS], F32R)
        scat = marks[:, 0:2 * TP].rearrange("p (j t) -> p j t", j=2)
        pick = marks[:, 2 * TP:].rearrange("p (t s) -> p t s", t=3)
        rparts = marks[:, 0:2 * KD * NE].rearrange("p (h k e) -> p h k e", h=2, k=KD)
        ident = sb("ident", [P, P])
        ones = sb("ones", [1, DH])
        tri = sb("tri", [P, P], BF16)
        onesb = sb("ones_bf", [P, P], BF16)
        stats = sb("stats", [P, 3, 2, 6])
        meanvar = sb("meanvar", [P, 3, 2])
        vareps = sb("vareps", [P, 3])
        std = sb("std", [P, 3])
        rstd = sb("rstd", [P, 3])
        smax = sb("smax", [P, 3, HEADS])
        snegmax = sb("snegmax", [P, 3, HEADS])
        ssum = sb("ssum", [P, 3, HEADS])
        srec = sb("srec", [P, 3, HEADS])
        acc_factor = sb("acc_factor", [P, 6])
        round_thr = sb("round_thr", [1, MAX_ROUNDS - 1])
        round_gt = sb("round_gt", [1, MAX_ROUNDS - 1])
        rounds_f = sb("rounds_f", [1, 2])
        rounds_i = sb("rounds_i", [1, 1], I32)
        PS = ctx.enter_context(nc.psum_tensor("PS", [P, 8, 512], F32))

        def early(at, *shape, rows=P):
            n = 1
            for s in shape:
                n *= s
            v = ring[0:rows, at:at + n]
            if len(shape) == 2:
                return v.rearrange("p (a b) -> p a b", a=shape[0])
            if len(shape) == 3:
                return v.rearrange("p (a b c) -> p a b c", a=shape[0], b=shape[1])
            return v

        prob1 = early(0, HEADS, 256)
        prob0 = early(2048, HEADS, P)
        probs = early(3072, HEADS, TOK, rows=DH)
        probT = early(5632, 4, 3, 384)
        relpad = early(5632, PAD + REL, rows=HEADS)
        v_tok = early(10240, 3, AW)
        k_tok = early(11776, 3, AW)
        ck = early(13312, 2, AW)
        cv = early(14336, 2, AW)
        ckT = early(15360, JW, 256)
        ws = early(16384, 8, P)
        wsT = early(17408, 8, P)
        vn = early(18432, 3, AW)
        mlpvec = early(19968, 2, AW)
        bsrow = early(20992, 8, P, rows=1)
        lninvec = early(22016, 2, D)

        zt = z[:, :].rearrange("p (a t) -> p a t", t=TOK)
        obT = zt[:, U0:U0 + JW, :]
        mT = zt[:, 0:KD, :]
        woT = zt[:, KD:2 * KD, :]

        def zv(at, n):
            return z[:, at:at + n]

        lnvec = zv(5376, 2 * D).rearrange("p (a d) -> p a d", a=2)
        hsT = zv(3456, 2 * TOK).rearrange("p (a t) -> p a t", a=2)
        rw = zv(640, KD * NE).rearrange("p (k e) -> p k e", k=KD)
        rbias = zv(1152, NE)
        rtemp = [zv(1280 + 192 * i, 192).rearrange("p (a e) -> p a e", a=3) for i in range(8)]
        score, sel, msel, replaced, maskf, wt, wres, gmax = rtemp
        rsmall = zv(1280 + 8 * 192, 192).rearrange("p (a e) -> p a e", a=3)
        scoreT = zv(5376, TOK)
        mask = zv(1280 + 9 * 192, 96).bitcast(BF16).rearrange("p (a e) -> p a e", a=3)
        xgT = zv(0, KD * 4 * SLOTS).rearrange("p (k s) -> p k s", k=KD)
        act_h = zv(4096, 2 * HID).rearrange("p (a d) -> p a d", a=2)
        hid = zv(4608, 2 * HID).rearrange("p (a d) -> p a d", a=2)
        hidT = zv(5120, 2 * HID).rearrange("p (a k s) -> p a k s", a=2, k=2)
        keep = ZT * TOK - 1600
        pos = zv(keep, 3 * (NE + 8)).rearrange("p (a e) -> p a e", a=3)
        attrs = zv(keep + 216, 3 * (NE + 4) * 5 // 2).bitcast(BF16).rearrange("p (a e f) -> p a e f", a=3, f=5)
        pick_bf = zv(keep + 1178, 3 * 4 * SLOTS // 2).bitcast(BF16).rearrange("p (t s) -> p t s", t=3)
        slots = zv(keep + 726, 4).rearrange("p (j f) -> p j f", j=2)
        iota_slot = zv(keep + 730, SLOTS)
        iota_tok = zv(keep + 794, TP)
        acc = xs

        gate_w = [ring[:, PEXP * e:PEXP * e + 4 * D].rearrange("p (k d) -> p k d", k=4) for e in range(2)]
        ple = ring[:, 2 * PEXP:2 * PEXP + 3 * D].rearrange("p (a d) -> p a d", a=3)
        ln2vec = ring[:, 2 * KD * HID:PEXP].rearrange("p (a d) -> p a d", a=2)
        sgT = ring[:, 3 * PEXP:3 * PEXP + KD * TOK].rearrange("p (a t) -> p a t", a=KD)
        wr0 = wr[:, 0, :, :].rearrange("p k c -> p (k c)")
        p_tok = zv(2048, 768).rearrange("p (a d) -> p a d", a=3)
        pT = zv(2816, 2 * TOK).rearrange("p (a t) -> p a t", a=2)
        proj_w = wr[:, 1, :, :].rearrange("p k c -> p (k c)").rearrange("p (k d) -> p k d", k=2)
        sw2 = wr0.rearrange("p (k d) -> p k d", k=2)

        def w13(pair, e, k):
            o = (2 * pair + e) * PEXP
            return ring[:, o:o + 2 * KD * HID].rearrange("p (m k h) -> p m k h", m=2, k=KD)[:, :, k, :]

        def w2(pair, e, k, half):
            o = (2 * pair + e) * PEXP + 2 * KD * HID + k * D + 512 * half
            return ring[:, o:o + 512]

        RW = PAD + REL
        rel_dram = nc.dram_tensor("rel_rows", (HEADS, P, RW), F32, kind="Internal")

        x_loaded = [sem(f"x_loaded{t}") for t in range(3)]
        lnin_loaded = sem("lnin_loaded")
        w_loaded = [sem(f"w_loaded{c}") for c in range(2)]
        cache_loaded = sem("cache_loaded")
        ws_loaded = sem("ws_loaded")
        mlpvec_loaded = sem("mlpvec_loaded")
        bs_loaded = sem("bs_loaded")
        rel_loaded = sem("rel_loaded")
        rel_padded = sem("rel_padded")
        rel_stored = sem("rel_stored")
        bias_loaded = sem("bias_loaded")
        route_loaded = sem("route_loaded")
        ln2_loaded = sem("ln2_loaded")
        sw2_loaded = sem("sw2_loaded")
        w13_loaded = [[sem(f"w13_loaded{j}{half}") for half in range(2)] for j in range(2)]
        w2_loaded = [sem(f"w2_loaded{j}") for j in range(2)]
        ple_loaded = sem("ple_loaded")
        gate_loaded = sem("gate_loaded")
        kv_stored = sem("kv_stored")
        y_stored = sem("y_stored")
        const_zero = sem("const_zero")
        const_ready = sem("const_ready")
        wsmask_ready = sem("wsmask_ready")
        dve_step = sem("dve_step")
        dve_last_step = sem("dve_last_step")
        var_ready = sem("var_ready")
        std_ready = sem("std_ready")
        ln_done = sem("ln_done")
        xT_ps = sem("xT_ps")
        xT_ready = sem("xT_ready")
        prep_ps = sem("prep_ps")
        prep_ready = sem("prep_ready")
        w_high = sem("w_high")
        w_low = sem("w_low")
        half_used = sem("half_used")
        xT_high = sem("xT_high")
        proj_free = sem("proj_free")
        tok_ps = sem("tok_ps")
        tok_ready_act = sem("tok_ready_act")
        tok_ready_dve = sem("tok_ready_dve")
        gelu_u = sem("gelu_u")
        score_ps = sem("score_ps")
        score_ready = sem("score_ready")
        negmax_ready = sem("negmax_ready")
        exp_done = sem("exp_done")
        prob_ready = sem("prob_ready")
        mix_ps = sem("mix_ps")
        mix_ready = sem("mix_ready")
        sig_done = sem("sig_done")
        ob_high = sem("ob_high")
        ob_low = sem("ob_low")
        probT_ps = sem("probT_ps")
        probT_act = sem("probT_act")
        probT_dve = sem("probT_dve")
        oa_ps = sem("oa_ps")
        oa_ready = sem("oa_ready")
        oa_high = sem("oa_high")
        m_high = sem("m_high")
        m_low = sem("m_low")
        branch_free = sem("branch_free")
        out_free = sem("out_free")
        out_ps = sem("out_ps")
        residual = sem("residual")
        x1T_ps = sem("x1T_ps")
        x1T_high = sem("x1T_high")
        x1T_ready = sem("x1T_ready")
        logits_ps = sem("logits_ps")
        router_high = sem("router_high")
        router_low = sem("router_low")
        scores_turned = sem("scores_turned")
        score_sig = sem("score_sig")
        shared_silu = sem("shared_silu")
        shared_hid = sem("shared_hid")
        factor_set = sem("factor_set")
        early_added = sem("early_added")
        shared_ps = sem("shared_ps")
        mask_ready = sem("mask_ready")
        pos_ps = sem("pos_ps")
        rounds_ready = sem("rounds_ready")
        pT_ps = sem("pT_ps")
        pT_ready = sem("pT_ready")
        table_ps = sem("table_ps")
        slots_ready = sem("slots_ready")
        dve_rounds = sem("dve_rounds")
        pos_moved = sem("pos_moved")
        pick_ready = sem("pick_ready")
        pick_bf_ready = sem("pick_bf_ready")
        xrows_high = sem("xrows_high")
        xrows_ready = sem("xrows_ready")
        gather_ps = sem("gather_ps")
        gathered_ready = sem("gathered_ready")
        up_done = [sem(f"up_done{j}") for j in range(2)]
        silu_done = sem("silu_done")
        hid_ready = sem("hid_ready")
        hidT_ps = sem("hidT_ps")
        hidT_ready = sem("hidT_ready")
        y_ps = sem("y_ps")
        y_high = sem("y_high")
        y_low = sem("y_low")
        scat_ready = sem("scat_ready")
        scat_ps = sem("scat_ps")
        acc_added = sem("acc_added")
        ple_ps = sem("ple_ps")
        ple_ready = sem("ple_ready")
        x2T_ps = sem("x2T_ps")
        x2T_high = sem("x2T_high")
        x2T_ready = sem("x2T_ready")
        gate_high = sem("gate_high")
        gate_low = sem("gate_low")
        gate_used = sem("gate_used")
        gate_sig = sem("gate_sig")
        gate_rows = sem("gate_rows")
        y_ready = sem("y_ready")

        PLE_BANK = (4, 2, 6)
        EARLY = (4, 5)
        WARM = (16, 24, 10)
        GATE_GROUPS = ((0, 4), (4, 6), (6, 8))
        SCAT_BANK = (2, 3, 7, 0, 1, 7)
        CHUNK_STEPS = N_IN // CH // 2
        FIRST_STEPS = (S0 + JW) * P // CH // 2
        WL = 32

        block = ctx.enter_context(nc.Block())

        def cols(t):
            return slice(P * t, P * t + ROWS[t])

        @block.sync
        def _(sp):
            for t in range(2):
                sp.dma_start(xs[:, t, :], x_prompt[0, P * t:P * (t + 1), :]).then_inc(x_loaded[t], 16)
            sp.dma_start(xs[0:ROWS[2], 2, :], x_sample[0]).then_inc(x_loaded[2], 16)
            for i, v in enumerate((ln_in_g, ln_in_b)):
                sp.dma_start(lninvec[:, i, :], v.partition_broadcast(P)).then_inc(lnin_loaded, 16)
            w_in_v = w_in[0].rearrange("(p k) n -> p k n", k=KD)

            def load_chunk(c, first, second):
                sp.dma_start(wr[:, c, 0:4, :], first).then_inc(w_loaded[c], 16)
                sp.dma_start(wr[:, c, 4:KD, :], second).then_inc(w_loaded[c], 16)

            for c in range(2):
                n = slice(c * CH, (c + 1) * CH)
                load_chunk(c, w_in_v[:, 0:4, n], w_in_v[:, 4:KD, n])
            with sp.Fori(0, CHUNK_STEPS - 1) as i:
                for c in range(2):
                    sp.wait_ge(w_low, 8 * i + 4 * c + 4)
                    n = ds((2 * i + c + 2) * CH, CH)
                    load_chunk(c, w_in_v[:, 0:4, n], w_in_v[:, 4:KD, n])

            w1_v = exp_w1[0].rearrange("e (p k) h -> e p (k h)", k=KD)
            w3_v = exp_w3[0].rearrange("e (p k) h -> e p (k h)", k=KD)
            w2_v = exp_w2[0].rearrange("e (p k) d -> e p (k d)", k=2)

            def up_loads(pair, half):
                n = KD * HID // 2
                for e in range(2):
                    for m, wv in enumerate((w1_v, w3_v)):
                        o = (2 * pair + e) * PEXP + m * KD * HID + half * n
                        yield (ring[:, o:o + n], wv[:, :, half * n:half * n + n], e, w13_loaded[pair][half])

            def down_loads(pair):
                for e in range(2):
                    o = (2 * pair + e) * PEXP + 2 * KD * HID
                    yield (ring[:, o:o + 2 * D], w2_v, e, w2_loaded[pair])

            first = [(2 * j, x) for j in range(2) for half in range(2) for x in up_loads(j, half)]
            first += [(2 * j, x) for j in range(2) for x in down_loads(j)]

            def first_expert_load(n=1):
                for _ in range(min(n, len(first))):
                    base, (dst, wv, e, s) = first.pop(0)
                    sp.dma_start(dst, wv[base + e]).then_inc(s, 16)

            wa_v = w_a[0].rearrange("(j p) n -> p j n", p=P)
            wb_v = w_b[0].rearrange("(j p) n -> p j n", p=P)
            for i in range(2):
                for c in range(2):
                    sp.wait_ge(w_low, 2 * BRANCH_T + 8 * i + 4 * c - 4)
                    n = slice((2 * i + c) * CH, (2 * i + c + 1) * CH)
                    load_chunk(c, wa_v[:, :, n], wb_v[:, :, n])
                    if i == 1:
                        if c == 0:
                            sp.wait_ge(oa_ps, 4)
                            sp.wait_ge(mix_ps, 1)
                            sp.wait_ge(kv_stored, 16 * 6)
                        first_expert_load(2)
            wo_v = w_out[0].rearrange("(j p) n -> p j n", p=P)
            for i in range(2):
                for c in range(2):
                    sp.wait_ge(w_low, 2 * OUT_T + 8 * i + 4 * c - 4)
                    n = slice((2 * i + c) * CH, (2 * i + c + 1) * CH)
                    load_chunk(c, wo_v[:, 0:4, n], wo_v[:, 4:KD, n])
                    first_expert_load(2 + 2 * c)
            sp.wait_ge(branch_free, 4 + KD)
            sp.dma_start(lnvec[:, 0, :], ln1_g[0].partition_broadcast(P)).then_inc(route_loaded, 16)
            sp.dma_start(lnvec[:, 1, :], ln1_b[0].partition_broadcast(P)).then_inc(route_loaded, 16)
            sp.wait_ge(m_low, KD)
            sp.dma_start(rw[:, :, :], router_w[0].rearrange("(p k) e -> p k e", k=KD)).then_inc(route_loaded, 16)
            sp.dma_start(rbias, router_bias[0].partition_broadcast(P)).then_inc(route_loaded, 16)
            for c, w in enumerate((sh_w1, sh_w3)):
                sp.wait_ge(w_low, 2 * SHARED_T + 4 * c - 4)
                w_v = w[0].rearrange("(p k) h -> p k h", k=KD)
                load_chunk(c, w_v[:, 0:4, :], w_v[:, 4:KD, :])
                first_expert_load()
            first_expert_load(len(first))
            sp.wait_ge(w_low, 2 * SHARED_T + 4)
            sp.dma_start(sw2, sh_w2[0].rearrange("(j p) d -> p j d", p=P)).then_inc(sw2_loaded, 16)
            sp.wait_ge(w_low, 2 * SHARED_T + 8)
            sp.dma_start(proj_w, ple_proj[0].rearrange("(j p) d -> p j d", p=P)).then_inc(ple_loaded, 16)
            sp.wait_ge(pick_bf_ready, 3)
            sp.dma_start(p_tok[:, 0:2, :], p_prompt[0, 0].rearrange("(a p) d -> p a d", p=P)).then_inc(ple_loaded, 16)
            sp.dma_start(p_tok[0:ROWS[2], 2, :], p_sample[0, 0]).then_inc(ple_loaded, 16)

            def expert_step(n, expert):
                for j in range(2):
                    for half in range(2):
                        sp.wait_ge(up_done[j], 2 * n - 1 + half)
                        for dst, wv, e, s in up_loads(j, half):
                            sp.dma_start(dst, wv[ds(expert + 2 * j + e, 1)].rearrange("o p n -> (o p) n")).then_inc(s, 16)
                for j in range(2):
                    sp.wait_ge(y_ps, 4 * n - 2 + 2 * j)
                    for dst, wv, e, s in down_loads(j):
                        sp.dma_start(dst, wv[ds(expert + 2 * j + e, 1)].rearrange("o p n -> (o p) n")).then_inc(s, 16)

            with sp.Fori(1, STEPS) as i:
                expert_step(i, 4 * i)
            more = sp.value_load(rounds_i[0:1, 0:1], min_val=0, max_val=MAX_ROUNDS - 1)
            with sp.If(more > 0):
                with sp.Fori(0, more) as r:
                    with sp.Fori(0, STEPS) as i:
                        expert_step((r + 1) * STEPS + i, 4 * i)
            sp.wait_ge(up_done[0], (more + 1) * (2 * STEPS))
            gw_v = ple_gate[0].rearrange("(p k) n -> p k n", k=KD)
            for e in range(2):
                sp.dma_start(gate_w[e], gw_v[:, 4 * e:4 * e + 4, :]).then_inc(gate_loaded, 16)
            sp.wait_ge(y_ps, (more + 1) * (4 * STEPS))
            sp.dma_start(ln2vec[:, 0, :], ln2_g[0].partition_broadcast(P)).then_inc(ln2_loaded, 16)
            sp.dma_start(ln2vec[:, 1, :], ln2_b[0].partition_broadcast(P)).then_inc(ln2_loaded, 16)
            for g, (k0, k1) in enumerate(GATE_GROUPS):
                c = slice(P * k0, P * k1)
                for t in range(3):
                    sp.wait_ge(y_ready, 3 * g + t + 1)
                    out = y_prompt[0, P * t:P * (t + 1), c] if t < 2 else y_sample[0, :, c]
                    sp.dma_start(out, xs[0:ROWS[t], t, c]).then_inc(y_stored, 16)
            sp.wait_ge(y_stored, 16 * 3 * len(GATE_GROUPS))

        @block.gpsimd
        def _(pool):
            pool.memset(ident[:, :], 0.0).then_inc(const_zero, 1)
            pool.memset(tri[:, :], 1.0).then_inc(const_zero, 1)
            pool.memset(onesb[:, :], 1.0)
            pool.memset(ones[:, :], 1.0)
            pool.wait_ge(const_zero, 2)
            pool.affine_select(out=ident[:, :], in_=ident[:, :], compare_op=ALU.not_equal, fill=1.0, base=0,
                               pattern=[[-1, P]], channel_multiplier=1)
            pool.affine_select(out=tri[:, :], in_=tri[:, :], compare_op=ALU.is_gt, fill=0.0, base=0,
                               pattern=[[1, P]], channel_multiplier=-1)
            pool.iota(round_thr[:, :], pattern=[[SLOTS, MAX_ROUNDS - 1]], base=SLOTS, channel_multiplier=0,
                      allow_small_or_imprecise_dtypes=True).then_inc(const_ready, 1)
            def low_half(raw, part, signal):
                part = part.rearrange("p h (k n) -> p h k n", k=4)
                pool.tensor_tensor(part[:, 1, :, :], raw, part[:, 0, :, :].bitcast(F32), ALU.subtract).then_inc(signal, 1)

            for half in range(2):
                pool.wait_ge(w_high, half + 1)
                low_half(wr[:, 0, 4 * half:4 * half + 4, 0:P], split[:, half, :, :], w_low)
            pool.wait_ge(rel_loaded, 16)
            pool.tensor_copy(relpad[:, 0:PAD], relpad[:, PAD:PAD + 1].to_broadcast([HEADS, PAD])).then_inc(rel_padded, 1)
            pool.wait_ge(rel_padded, 1)
            pool.dma_start(rel_dram.ap(), relpad.unsqueeze(1).to_broadcast([HEADS, P, RW])).then_inc(rel_stored, 16)
            pool.wait_ge(rel_stored, 16)

            def toeplitz(dst, rows, par, keys, first):
                src = bass.AP(tensor=rel_dram, offset=par * P * RW + first,
                              ap=[[RW - 1, rows], [2 * P * RW, 4], [1, keys]])
                pool.dma_start(dst, src).then_inc(bias_loaded, 16)

            for par in range(2):
                toeplitz(prob1[:, 4 * par:4 * par + 4, :], P, par, 256, PAD + 256 - P)
                toeplitz(prob0[:, 4 * par:4 * par + 4, :], P, par, P, PAD + 256)
                toeplitz(probs[:, 4 * par:4 * par + 4, :], DH, par, TOK, PAD)

            pool.wait_ge(ws_loaded, 16)
            pool.affine_select(out=ws, in_=ws, compare_op=ALU.is_ge, fill=0.0, base=0,
                               pattern=[[0, 8], [-1, P]], channel_multiplier=1).then_inc(wsmask_ready, 1)
            pool.wait_ge(tok_ready_act, 3)
            pool.dma_start(new_k_prompt[0, 0].rearrange("(a p) h d -> p a (h d)", p=P), k_tok[:, 0:2, :]).then_inc(kv_stored, 16)
            pool.dma_start(new_k_sample[0, 0].rearrange("p h d -> p (h d)"), k_tok[0:ROWS[2], 2, :]).then_inc(kv_stored, 16)
            pool.wait_ge(tok_ready_dve, 3)
            pool.dma_start(new_v_prompt[0, 0].rearrange("(a p) h d -> p a (h d)", p=P), v_tok[:, 0:2, :]).then_inc(kv_stored, 16)
            pool.dma_start(new_v_sample[0, 0].rearrange("p h d -> p (h d)"), v_tok[0:ROWS[2], 2, :]).then_inc(kv_stored, 16)
            pool.wait_ge(ln_done, 6)
            pool.dma_start(new_mlp_prompt[0, 0], vn[:, 1, :]).then_inc(kv_stored, 16)
            pool.dma_start(new_mlp_sample[0, 0], vn[0:ROWS[2], 2, :]).then_inc(kv_stored, 16)
            pool.wait_ge(branch_free, 4 + KD)
            pool.iota(iota_slot, pattern=[[1, SLOTS]], base=0, channel_multiplier=0, allow_small_or_imprecise_dtypes=True)
            pool.iota(iota_tok, pattern=[[1, TP]], base=0, channel_multiplier=0, allow_small_or_imprecise_dtypes=True)
            for t in range(3):
                pool.iota(attrs[:, t, :, 3], pattern=[[0, NE + 4]], base=0, channel_multiplier=1, allow_small_or_imprecise_dtypes=True)
                last = pool.memset(attrs[:, t, :, 4], float(P * t))
            last.then_inc(const_ready, 1)
            pool.wait_ge(router_high, 1)
            pool.tensor_tensor(rparts[:, 1, :, :], rw, rparts[:, 0, :, :].bitcast(F32), ALU.subtract).then_inc(router_low, 1)
            for tile in range(2):
                for half in range(2):
                    pool.wait_ge(w_high, 2 * (SHARED_T + 2 + tile) + half + 1)
                    low_half(wr[:, 1, 4 * half:4 * half + 4, P * tile:P * tile + P], split[:, 2 * tile + half, :, :], w_low)
            pool.wait_ge(xrows_high, 1)
            pool.tensor_tensor(xrows[:, 1, 0, :, :], xs[:, 0, :].rearrange("p (c k) -> p k c", k=KD),
                               xrows[:, 0, 0, :, :].bitcast(F32), ALU.subtract).then_inc(xrows_ready, 1)
            for tile in range(2):
                for half in range(2):
                    pool.wait_ge(gate_high, 2 * tile + half + 1)
                    low_half(gate_w[half][:, :, P * tile:P * (tile + 1)], split[:, 2 * tile + half, :, :], gate_low)

        @block.scalar
        def _(act):
            act.wait_ge(x_loaded[2], 16)
            act.dma_start(ck, cache_k[0, 0].rearrange("(a p) h d -> p a (h d)", p=P)).then_inc(cache_loaded, 16)
            act.dma_start(ws, mlp_w_s[0].rearrange("g t s -> t g s")).then_inc(ws_loaded, 16)
            act.dma_start(relpad[:, PAD:PAD + REL], rel_bias[0]).then_inc(rel_loaded, 16)
            act.dma_start(cv, cache_v[0, 0].rearrange("(a p) h d -> p a (h d)", p=P)).then_inc(cache_loaded, 16)
            for i, v in enumerate((mlp_g, mlp_b)):
                act.dma_start(mlpvec[:, i, :], v[0].partition_broadcast(P)).then_inc(mlpvec_loaded, 16)
            act.dma_start(bsrow, mlp_b_s[0:1]).then_inc(bs_loaded, 16)

            def norm_std(n):
                nc.scalar.preload_act_table(ACT.Sqrt)
                act.wait_ge(var_ready, n)
                nc.scalar.activation(std[:, :], vareps[:, :], ACT.Sqrt).then_inc(std_ready, 1)

            def high(tile, half, load, reused, place=None):
                place = (tile if place is None else place) % 4
                act.wait_ge(w_loaded[place // 2], load)
                if reused:
                    act.wait_ge(half_used, 2 * (tile - 2) + half + 1)
                c = place // 2
                raw = wr[:, c, 4 * half:4 * half + 4, P * (place % 2):P * (place % 2) + P]
                nc.scalar.activation(split[:, 2 * (place % 2) + half, 0, :].rearrange("p (k n) -> p k n", k=4), raw, ACT.Copy)\
                    .then_inc(w_high, 1)

            norm_std(1)
            for tile in range(2):
                for half in range(2):
                    high(tile, half, WL, False)
            def high_xT(ps_sem, ready, bank):
                for t in range(3):
                    act.wait_ge(ps_sem, t + 1)
                    b = bank(t)
                    src = PS[:, b:b + 2, :].rearrange("p b (k s) -> p (b k) s", k=4)[:, :, 0:ROWS[t]]
                    nc.scalar.activation(xT[:, 0, :, cols(t)], src, ACT.Copy).then_inc(ready, 1)

            high_xT(xT_ps, xT_high, lambda t: 2 * t)
            with act.Fori(0, FIRST_STEPS) as i:
                for b in range(4):
                    tile = 4 * i + b
                    for half in range(2):
                        high(tile + 2, half, WL * (i + 1) + WL * (b // 2), True, b + 2)
                    act.wait_ge(half_used, 2 * tile + 2)
                    nc.scalar.activation(zt[:, ds(tile, 1), :].rearrange("p o t -> p (o t)"), PS[:, b, 0:TOK], ACT.Copy)\
                        .then_inc(proj_free, 1)
            for t in range(3):
                act.wait_ge(tok_ps, t + 1)
                nc.scalar.activation(k_tok[0:ROWS[t], t, :], PS[0:ROWS[t], 4 + t, :], ACT.Copy).then_inc(tok_ready_act, 1)
            for t in range(3):
                act.wait_ge(tok_ps, 7 + t)
                nc.scalar.activation(vn[0:ROWS[t], t, :], PS[0:ROWS[t], (6, 7, 4)[t], :], ACT.Gelu_apprx_tanh)\
                    .then_inc(tok_ready_act, 1)
            act.wait_ge(proj_free, 4 + FIRST_STEPS * 4)
            nc.scalar.activation(obT, obT, ACT.Gelu_apprx_tanh).then_inc(gelu_u, 1)
            group = ((prob1, P), (prob0, P), (probs, DH))
            for i in range(4 * (CHUNK_STEPS - FIRST_STEPS)):
                tile = 4 * FIRST_STEPS + i
                for half in range(2):
                    high(tile + 2, half, WL * ((tile + 2) // 4 + 1), True)
                act.wait_ge(half_used, 2 * tile + 2)
                place = GATE_A[i] if i < KD else GB0 + i - KD
                nc.scalar.activation(zt[:, place, :], PS[:, i % 4, 0:TOK], ACT.Copy).then_inc(proj_free, 1)
                if i // 4 < 3:
                    t = i // 4
                    pr, n = group[t]
                    if i % 4 == 0:
                        act.wait_ge(negmax_ready, t + 1)
                    for h in (2 * (i % 4), 2 * (i % 4) + 1):
                        last = nc.scalar.activation(pr[:, h, :], pr[:, h, :], ACT.Exp, bias=snegmax[0:n, t, h:h + 1],
                                                    accum_out=ssum[0:n, t, h:h + 1])
                    if i % 4 == 3:
                        last.then_inc(exp_done, 1)
                if i == 12:
                    norm_std(2)
            act.wait_ge(proj_free, 4 + CHUNK_STEPS * 4)
            nc.scalar.activation(zt[:, V0:V0 + 4, :], zt[:, V0:V0 + 4, :], ACT.Sigmoid)
            nc.scalar.activation(zt[:, S0:ZT, :], zt[:, S0:ZT, :], ACT.Sigmoid).then_inc(sig_done, 1)
            act.wait_ge(mix_ready, 1)
            nc.scalar.activation(xT[:, 0, JW:KD, :], obT, ACT.Copy).then_inc(ob_high, 1)

            def turned_probs(j):
                act.wait_ge(probT_ps, j + 1)
                b = 4 if j % 2 == 0 else 0
                nc.scalar.activation(probT[:, j, 0:2, :], PS[:, b:b + 2, 0:384], ACT.Copy).then_inc(probT_act, 1)

            turned_probs(0)
            turned_probs(1)
            for j in range(4):
                act.wait_ge(oa_ps, j + 1)
                nc.scalar.activation(xT[:, 0, j, :], PS[:, 7 if j % 2 == 0 else 3, 0:TOK], ACT.Copy).then_inc(oa_high, 1)
                if j < 2:
                    turned_probs(j + 2)
            with act.Fori(0, 2) as i:
                for b in range(4):
                    for half in range(2):
                        high(BRANCH_T + 4 * i + b + 2, half, WL * (BRANCH_T // 4 + b // 2) + WL * (i + 1), True, b + 2)
            act.wait_ge(half_used, 2 * (BRANCH_T + KD))
            for tile in range(KD):
                act.wait_ge(branch_free, 4 + tile + 1)
                nc.scalar.activation(xT[:, 0, tile, :], mT[:, tile, :], ACT.Copy).then_inc(m_high, 1)
            with act.Fori(0, 2) as i:
                for b in range(4):
                    tile = OUT_T + 4 * i + b
                    for half in range(2):
                        high(tile + 2, half, WL * (OUT_T // 4 + b // 2) + WL * (i + 1), True, b + 2)
                    act.wait_ge(half_used, 2 * tile + 2)
                    nc.scalar.activation(woT[:, ds(4 * i + b, 1), :].rearrange("p o t -> p (o t)"), PS[:, b, 0:TOK], ACT.Copy)\
                        .then_inc(out_free, 1)
            act.wait_ge(route_loaded, 64)
            nc.scalar.activation(rparts[:, 0, :, :], rw, ACT.Copy)
            nc.scalar.activation(marks[:, 2 * KD * NE:2 * KD * NE + NE], rbias, ACT.Copy).then_inc(router_high, 1)
            norm_std(3)
            high_xT(x1T_ps, x1T_high, lambda t: 2 * t)
            act.wait_ge(logits_ps, 1)
            nc.scalar.activation(scoreT[0:NE, :], PS[0:NE, 6, 0:TOK], ACT.Sigmoid).then_inc(score_sig, 1)
            for tile in range(SHARED_T + 2, SHARED_T + 4):
                for half in range(2):
                    high(tile, half, WL * (tile // 4 + 1), True)
            for m in range(2):
                act.wait_ge(half_used, 2 * SHARED_T + 2 * m + 2)
                nc.scalar.activation(hsT[:, m, :], PS[:, m, 0:TOK], ACT.Silu).then_inc(shared_silu, 1)
            act.wait_ge(half_used, 2 * SHARED_T + 8)
            for t in range(3):
                x = xs[0:ROWS[t], t, :].rearrange("p (c k) -> p k c", k=KD)
                nc.scalar.activation(xrows[0:ROWS[t], 0, t, :, :], x, ACT.Copy).then_inc(xrows_high, 1)

            def gathered(n, g):
                act.wait_ge(gather_ps, 4 * n + g + 1)
                nc.scalar.activation(xgT[:, 2 * g:2 * g + 2, :].rearrange("p k s -> p (k s)"), PS[:, g % 2, :], ACT.Copy)\
                    .then_inc(gathered_ready, 1)

            for g in range(4):
                gathered(0, g)
            nc.scalar.preload_act_table(ACT.Silu)
            def expert_step(n, last=False):
                def silu(j):
                    act.wait_ge(up_done[j], 2 * n + 2)
                    nc.scalar.activation(act_h[:, j, :], PS[:, 2 + j, 0:HID], ACT.Silu).then_inc(silu_done, 1)

                def hidden_T(j):
                    act.wait_ge(hidT_ps, 2 * n + j + 1)
                    nc.scalar.activation(hidT[:, j, :, :].rearrange("p k s -> p (k s)"),
                                         PS[:, 4, HID * j:HID * (j + 1)], ACT.Copy).then_inc(hidT_ready, 1)

                def high(j, half):
                    act.wait_ge(y_ps, 4 * n + 2 * j + half + 1)
                    nc.scalar.activation(ysplit[:, j, 0, 512 * half:512 * half + 512], PS[:, 5 + half, :], ACT.Copy)\
                        .then_inc(y_high, 1)

                silu(0)
                hidden_T(0)
                silu(1)
                if not last:
                    gathered(n + 1, 0)
                    gathered(n + 1, 1)
                hidden_T(1)
                high(0, 0)
                high(0, 1)
                if not last:
                    gathered(n + 1, 2)
                    gathered(n + 1, 3)
                high(1, 0)
                high(1, 1)

            with act.Fori(0, STEPS - 1) as i:
                expert_step(i)
            act.wait_ge(rounds_ready, 1)
            more = act.value_load(rounds_i[0:1, 0:1], min_val=0, max_val=MAX_ROUNDS - 1)
            with act.If(more > 0):
                with act.Fori(0, more) as r:
                    with act.Fori(0, STEPS) as i:
                        expert_step(r * STEPS + i + STEPS - 1)
            expert_step(more * STEPS + STEPS - 1, last=True)
            act.wait_ge(pT_ps, 1)
            nc.scalar.activation(pT, PS[:, 5:7, 0:TOK], ACT.Copy).then_inc(pT_ready, 1)
            act.wait_ge(gate_loaded, 32)
            act.wait_ge(scat_ps, (more + 1) * (6 * STEPS))
            for tile in range(2):
                for half in range(2):
                    nc.scalar.activation(split[:, 2 * tile + half, 0, :].rearrange("p (k n) -> p k n", k=4),
                                         gate_w[half][:, :, P * tile:P * (tile + 1)], ACT.Copy).then_inc(gate_high, 1)
            norm_std(4)
            def embedding(t):
                act.wait_ge(ple_ps, t + 1)
                nc.scalar.activation(ple[0:ROWS[t], t, :], PS[0:ROWS[t], PLE_BANK[t]:PLE_BANK[t] + 2, :].rearrange("p b s -> p (b s)"),
                                     ACT.Copy).then_inc(ple_ready, 1)

            embedding(0)
            embedding(1)
            high_xT(x2T_ps, x2T_high, lambda t: 2 * t)
            embedding(2)
            nc.scalar.preload_act_table(ACT.Sigmoid)

            def high_gate(tile, place, reused):
                for half in range(2):
                    if reused:
                        act.wait_ge(gate_used, 2 * tile - 4 + half + 1)
                    nc.scalar.activation(split[:, 2 * place + half, 0, :].rearrange("p (k n) -> p k n", k=4),
                                         gate_w[half][:, :, ds(P * tile, P)], ACT.Copy).then_inc(gate_high, 1)

            with act.Fori(0, KD // 2 - 1) as i:
                for b in range(2):
                    tile = 2 * i + b
                    high_gate(tile + 2, b, True)
                    act.wait_ge(gate_used, 2 * tile + 2)
                    nc.scalar.activation(sgT[:, ds(tile, 1), :].rearrange("p o t -> p (o t)"), PS[:, b, 0:TOK], ACT.Sigmoid)\
                        .then_inc(gate_sig, 1)
            for tile in range(KD - 2, KD):
                act.wait_ge(gate_used, 2 * tile + 2)
                nc.scalar.activation(sgT[:, tile, :], PS[:, tile % 2, 0:TOK], ACT.Sigmoid).then_inc(gate_sig, 1)

        @block.vector
        def _(dve):
            steps = {dve_step: 0, dve_last_step: 0}
            own = [dve_step]

            def step(ins):
                ins.then_inc(own[0], 1)
                steps[own[0]] += 1
                return steps[own[0]]

            def after(n):
                dve.wait_ge(own[0], n)

            def norm_statistics(x, width, rows_loaded=None):
                halves = width // 512
                for t in range(3):
                    if rows_loaded:
                        dve.wait_ge(rows_loaded[t], 16)
                    for h in range(halves):
                        ins = nc.vector.bn_stats(stats[0:ROWS[t], t, h, :], x[0:ROWS[t], t, 512 * h:512 * h + 512])
                    done = step(ins)
                after(done)
                for t in range(3):
                    done = step(nc.vector.bn_aggr(meanvar[0:ROWS[t], t, :], stats[0:ROWS[t], t, 0:halves, :].rearrange("p a b -> p (a b)")))
                after(done)
                nc.vector.tensor_scalar(vareps[:, :], meanvar[:, :, 1], EPS, None, ALU.add).then_inc(var_ready, 1)

            def centre(x, vec, t):
                return step(nc.vector.scalar_tensor_tensor(
                    out=x[0:ROWS[t], t, :], in0=x[0:ROWS[t], t, :], scalar=meanvar[0:ROWS[t], t, 0:1],
                    in1=vec[0:ROWS[t], 0, :], op0=ALU.subtract, op1=ALU.mult))

            def inverse_std(n):
                dve.wait_ge(std_ready, n)
                return step(nc.vector.reciprocal(rstd[:, :], std[:, :]))

            def scale(x, vec, t):
                nc.vector.scalar_tensor_tensor(
                    out=x[0:ROWS[t], t, :], in0=x[0:ROWS[t], t, :], scalar=rstd[0:ROWS[t], t:t + 1],
                    in1=vec[0:ROWS[t], 1, :], op0=ALU.mult, op1=ALU.add).then_inc(ln_done, 1)

            def norm(x, width, vec, loaded, n, rows_loaded=None):
                norm_statistics(x, width, rows_loaded)
                dve.wait_ge(*loaded)
                centre(x, vec, 0)
                inverse = inverse_std(n)
                centred = centre(x, vec, 1)
                after(inverse)
                scale(x, vec, 0)
                last = centre(x, vec, 2)
                after(centred)
                scale(x, vec, 1)
                after(last)
                scale(x, vec, 2)

            def low(tile, half, place=None):
                place = (tile if place is None else place) % 4
                c = place // 2
                raw = wr[:, c, 4 * half:4 * half + 4, P * (place % 2):P * (place % 2) + P]
                parts = split[:, 2 * (place % 2) + half, :, :].rearrange("p h (k n) -> p h k n", k=4)
                dve.wait_ge(w_high, 2 * tile + half + 1)
                nc.vector.tensor_tensor(parts[:, 1, :, :], raw, parts[:, 0, :, :].bitcast(F32), ALU.subtract).then_inc(w_low, 1)

            def low_xT(high_sem, ready, bank):
                for t in range(3):
                    dve.wait_ge(high_sem, t + 1)
                    b = bank(t)
                    src = PS[:, b:b + 2, :].rearrange("p b (k s) -> p (b k) s", k=4)[:, :, 0:ROWS[t]]
                    nc.vector.tensor_tensor(xT[:, 1, :, cols(t)], src, xT[:, 0, :, cols(t)].bitcast(F32), ALU.subtract)\
                        .then_inc(ready, 1)

            after(step(nc.vector.memset(meanvar[:, :, :], 1.0)))
            norm(xs, D, lninvec, (lnin_loaded, 32), 1, x_loaded)
            low_xT(xT_high, xT_ready, lambda t: 2 * t)
            dve.wait_ge(w_low, 2)
            for half in range(2):
                low(1, half)
            for c in range(2):
                dve.wait_ge(prep_ps, c + 1)
                nc.vector.tensor_copy(ckT[:, :, P * c:P * (c + 1)], PS[:, 6 + c, :].rearrange("p (j s) -> p j s", j=4))\
                    .then_inc(prep_ready, 1)
            with dve.Fori(0, FIRST_STEPS) as i:
                for b in range(4):
                    for half in range(2):
                        low(4 * i + b + 2, half, b + 2)
            dve.wait_ge(prep_ps, 3)
            nc.vector.tensor_copy(wsT.rearrange("p g s -> p (g s)"), PS[:, 6:8, :].rearrange("p b s -> p (b s)"))\
                .then_inc(prep_ready, 1)
            dve.wait_ge(bias_loaded, 16 * 6)
            nc.vector.memset(prob1[0:64, :, 192:256], MASKED)
            after(step(nc.vector.memset(prob0[0:64, :, 64:P], MASKED)))

            def scores(pr, ps, t):
                nc.vector.scalar_tensor_tensor(out=pr, in0=ps, scalar=SCALE, in1=pr, op0=ALU.mult, op1=ALU.add)\
                    .then_inc(score_ready, 1)

            dve.wait_ge(score_ps, 1)
            scores(prob1, PS[:, 0:4, :].rearrange("p b (i k) -> p (b i) k", i=2), 0)
            for t in range(3):
                dve.wait_ge(tok_ps, 4 + t)
                nc.vector.tensor_copy(v_tok[0:ROWS[t], t, :], PS[0:ROWS[t], (7, 4, 5)[t], :]).then_inc(tok_ready_dve, 1)
            dve.wait_ge(score_ps, 2)
            scores(prob0, PS[:, 0:2, :].rearrange("p b (i k) -> p (b i) k", i=4), 1)
            for w in range(2):
                dve.wait_ge(score_ps, 3 + w)
                for par in range(2):
                    nc.vector.scalar_tensor_tensor(
                        out=probs[:, 4 * par + 2 * w:4 * par + 2 * w + 2, :], in0=PS[0:DH, 4 + 2 * par:6 + 2 * par, 0:TOK],
                        scalar=SCALE, in1=probs[:, 4 * par + 2 * w:4 * par + 2 * w + 2, :], op0=ALU.mult, op1=ALU.add)\
                        .then_inc(score_ready, 1)
            group = ((prob1, P), (prob0, P), (probs, DH))

            def maximum(t):
                pr, n = group[t]
                m = step(nc.vector.tensor_reduce(smax[0:n, t, :], pr, AX.X, ALU.max))
                after(m)
                nc.vector.tensor_scalar(snegmax[0:n, t, :], smax[0:n, t, :], -1.0, None, ALU.mult).then_inc(negmax_ready, 1)

            def divide(t):
                pr, n = group[t]
                dve.wait_ge(exp_done, t + 1)
                after(step(nc.vector.reciprocal(srec[0:n, t, :], ssum[0:n, t, :])))
                nc.vector.tensor_tensor(pr, pr, srec[0:n, t, :].unsqueeze(2).to_broadcast([n, HEADS, pr.shape[2]]), ALU.mult)\
                    .then_inc(prob_ready, 1)

            dve.wait_ge(score_ready, 6)
            for i in range(4 * (CHUNK_STEPS - FIRST_STEPS)):
                if i < 3:
                    maximum(i)
                if i == 5:
                    divide(0)
                if i == 9:
                    divide(1)
                if i == 11:
                    dve.wait_ge(tok_ready_act, 6)
                    norm_statistics(vn, AW)
                if i >= 13:
                    dve.wait_ge(mlpvec_loaded, 32)
                    centred = centre(vn, mlpvec, i - 13)
                    if i == 13:
                        after(inverse_std(2))
                    after(centred)
                    scale(vn, mlpvec, i - 13)
                for half in range(2):
                    low(4 * FIRST_STEPS + i + 2, half)
            divide(2)
            dve.wait_ge(mix_ps, 1)
            dve.wait_ge(gelu_u, 1)
            nc.vector.tensor_tensor(obT, PS[:, 0:4, 0:TOK], obT, ALU.mult).then_inc(mix_ready, 1)
            dve.wait_ge(ob_high, 1)
            nc.vector.tensor_tensor(xT[:, 1, JW:KD, :], obT, xT[:, 0, JW:KD, :].bitcast(F32), ALU.subtract).then_inc(ob_low, 1)

            def sample_probT(j):
                dve.wait_ge(probT_ps, j + 1)
                b = 6 if j % 2 == 0 else 2
                ps = PS[:, b, 0:384].rearrange("p (e k) -> p e k", e=2)
                dst = probT[:, j, 2, :].rearrange("p (e k) -> p e k", e=2)
                nc.vector.tensor_copy(dst[:, :, 0:128], ps[:, :, 0:128])
                nc.vector.tensor_copy(dst[0:DH, :, 128:192], ps[0:DH, :, 128:192]).then_inc(probT_dve, 1)

            def attention_out(j):
                dve.wait_ge(oa_high, j + 1)
                nc.vector.tensor_tensor(xT[:, 1, j, :], PS[:, 7 if j % 2 == 0 else 3, 0:TOK], xT[:, 0, j, :].bitcast(F32),
                                        ALU.subtract).then_inc(oa_ready, 1)

            sample_probT(0)
            sample_probT(1)
            for j in range(4):
                attention_out(j)
                if j < 2:
                    sample_probT(j + 2)
            dve.wait_ge(sig_done, 1)

            def low_m(tile):
                dve.wait_ge(m_high, tile + 1)
                nc.vector.tensor_tensor(xT[:, 1, tile, :], mT[:, tile, :], xT[:, 0, tile, :].bitcast(F32), ALU.subtract)\
                    .then_inc(m_low, 1)

            for tile in range(KD):
                for half in range(2):
                    low(BRANCH_T + tile + 2, half)
                ga, gb, b = zt[:, GATE_A[tile], :], zt[:, GB0 + tile, :], tile % 4
                dve.wait_ge(half_used, 2 * (BRANCH_T + tile) + 2)
                nc.vector.tensor_tensor(ga, PS[:, 2 * b, 0:TOK], ga, ALU.mult)
                after(step(nc.vector.tensor_tensor(gb, PS[:, 2 * b + 1, 0:TOK], gb, ALU.mult)))
                nc.vector.tensor_tensor(mT[:, tile, :], ga, gb, ALU.add).then_inc(branch_free, 1)
            for tile in range(KD):
                low_m(tile)
            with dve.Fori(0, 2) as i:
                for b in range(4):
                    for half in range(2):
                        low(OUT_T + 4 * i + b + 2, half, b + 2)
            for t in range(3):
                dve.wait_ge(out_ps, t + 1)
                b = (4, 6, 0)[t]
                x = xs[0:ROWS[t], t, :]
                nc.vector.scalar_tensor_tensor(out=x, in0=x, scalar=ALPHA, in1=PS[0:ROWS[t], b:b + 2, :].rearrange("p b s -> p (b s)"),
                                               op0=ALU.mult, op1=ALU.add).then_inc(residual, 1)
            dve.wait_ge(residual, 3)
            norm(xs, D, lnvec, (route_loaded, 64), 3)
            low_xT(x1T_high, x1T_ready, lambda t: 2 * t)

            def stage(f):
                done = [step(f(t, ROWS[t])) for t in range(3)]
                after(done[-1])

            gm = lambda t, n: gmax[0:n, t, :]
            stage(lambda t, n: nc.vector.memset(rsmall[:, t, :], MASKED))
            dve.wait_ge(scores_turned, 1)
            stage(lambda t, n: nc.vector.tensor_tensor(sel[0:n, t, :], PS[0:n, 7, NE * t:NE * (t + 1)], rbias[0:n, :], ALU.add))
            stage(lambda t, n: nc.vector.tensor_copy(score[0:n, t, :], PS[0:n, 7, NE * t:NE * (t + 1)]))
            for t in range(3):
                for g in range(GROUPS):
                    last = nc.vector.max(out=gmax[0:ROWS[t], t, 8 * g:8 * g + 8],
                                         in_=sel[0:ROWS[t], t, PER_GROUP * g:PER_GROUP * (g + 1)])
                m = step(last)
            after(m)
            stage(lambda t, n: nc.vector.tensor_tensor(rsmall[0:n, t, 0:8], gmax[0:n, t, 0:64:8], gmax[0:n, t, 1:64:8], ALU.add))
            stage(lambda t, n: nc.vector.max(out=rsmall[0:n, t, 16:24], in_=rsmall[0:n, t, 0:8]))
            stage(lambda t, n: nc.vector.memset(rsmall[0:n, t, 16 + KEEP_GROUPS:24], MASKED))
            stage(lambda t, n: nc.vector.match_replace(out=rsmall[0:n, t, 32:44], in_to_replace=rsmall[0:n, t, 16:24],
                                                       in_values=rsmall[0:n, t, 0:12], imm_value=2 * MASKED))
            stage(lambda t, n: nc.vector.tensor_scalar(rsmall[0:n, t, 48:56], rsmall[0:n, t, 32:40], 1.5 * MASKED, MASKED,
                                                       ALU.is_ge, ALU.mult))
            stage(lambda t, n: nc.vector.tensor_tensor(
                msel[0:n, t, :].rearrange("p (g i) -> p g i", g=GROUPS), sel[0:n, t, :].rearrange("p (g i) -> p g i", g=GROUPS),
                rsmall[0:n, t, 48:56].unsqueeze(2).to_broadcast([n, GROUPS, PER_GROUP]), ALU.add))
            stage(lambda t, n: nc.vector.max(out=rsmall[0:n, t, 16:24], in_=msel[0:n, t, :]))
            stage(lambda t, n: nc.vector.match_replace(out=replaced[0:n, t, :], in_to_replace=rsmall[0:n, t, 16:24],
                                                       in_values=msel[0:n, t, :], imm_value=3 * MASKED))
            stage(lambda t, n: nc.vector.tensor_scalar(maskf[0:n, t, :], replaced[0:n, t, :], 2 * MASKED, None, ALU.is_lt))
            for t in range(3):
                nc.vector.tensor_copy(mask[0:ROWS[t], t, :], maskf[0:ROWS[t], t, :]).then_inc(mask_ready, 1)
            stage(lambda t, n: nc.vector.tensor_tensor(wt[0:n, t, :], maskf[0:n, t, :], score[0:n, t, :], ALU.mult))
            stage(lambda t, n: nc.vector.tensor_reduce(rsmall[0:n, t, 60:61], wt[0:n, t, :], AX.X, ALU.add))
            stage(lambda t, n: nc.vector.reciprocal(rsmall[0:n, t, 61:62], rsmall[0:n, t, 60:61]))
            stage(lambda t, n: nc.vector.tensor_scalar(wt[0:n, t, :], wt[0:n, t, :], rsmall[0:n, t, 61:62], ROUTED_SCALE,
                                                       ALU.mult, ALU.mult))
            def shared_hidden(m):
                dve.wait_ge(shared_silu, m + 1)
                dve.wait_ge(half_used, 2 * SHARED_T + 2 * m + 6)
                nc.vector.tensor_tensor(hsT[:, m, :], hsT[:, m, :], PS[:, 2 + m, 0:TOK], ALU.mult).then_inc(shared_hid, 1)

            shared_hidden(0)
            dve.wait_ge(pos_ps, 1)
            stage(lambda t, n: nc.vector.scalar_tensor_tensor(out=wres[0:n, t, :], in0=PS[0:n, 7, NE * t:NE * (t + 1)], scalar=1.0,
                                                              in1=maskf[0:n, t, :], op0=ALU.add, op1=ALU.mult))
            stage(lambda t, n: nc.vector.tensor_scalar(pos[0:n, t, 0:NE], wres[0:n, t, :], -1.0, None, ALU.add))
            stage(lambda t, n: nc.vector.tensor_scalar(pos[0:n, t, NE:NE + 8], wres[0:n, t, 0:8], -1.0 - SLOTS, None, ALU.add))
            shared_hidden(1)
            after(step(nc.vector.tensor_reduce(rounds_f[:, 0:1], PS[0:1, 7, 3 * NE:4 * NE], AX.X, ALU.max)))
            dve.wait_ge(const_ready, 2)
            after(step(nc.vector.tensor_scalar(round_gt[:, :], round_thr[:, :], rounds_f[:, 0:1], None, ALU.is_lt)))
            after(step(nc.vector.tensor_reduce(rounds_f[:, 1:2], round_gt[:, :], AX.X, ALU.add)))
            nc.vector.tensor_copy(rounds_i[:, :], rounds_f[:, 1:2]).then_inc(rounds_ready, 1)

            def picks(expert, to, signal):
                for t in range(3):
                    k = ROWS[t]
                    nc.vector.tensor_tensor(
                        to[0:k, t, :].rearrange("p (e s) -> p e s", s=SLOTS),
                        iota_slot[0:k, :].unsqueeze(1).to_broadcast([k, 4, SLOTS]),
                        pos[0:k, t, ds(expert, 4)].unsqueeze(2).to_broadcast([k, 4, SLOTS]), ALU.is_equal).then_inc(signal, 1)

            def slot_values():
                for e in range(2):
                    h = slice(64 * e, 64 * e + 64)
                    ps = PS[h, 4, 0:20].rearrange("p (j f) -> p j f", j=2)
                    nc.vector.tensor_reduce(slots[h, :, 0], ps[:, :, 5 * e:5 * e + 3], AX.X, ALU.add).then_inc(slots_ready, 1)
                    nc.vector.tensor_reduce(slots[h, :, 1], ps[:, :, 5 * e + 3:5 * e + 5], AX.X, ALU.add).then_inc(slots_ready, 1)

            picks(0, pick, pick_ready)
            for t in range(1, 3):
                dve.wait_ge(xrows_high, t + 1)
                x = xs[0:ROWS[t], t, :].rearrange("p (c k) -> p k c", k=KD)
                nc.vector.tensor_tensor(xrows[0:ROWS[t], 1, t, :, :], x, xrows[0:ROWS[t], 0, t, :, :].bitcast(F32), ALU.subtract)\
                    .then_inc(xrows_ready, 1)
            for i in range(3):
                for at, k in ((0, NE), (NE, 4)):
                    for t in range(3):
                        done = step(nc.vector.tensor_copy(attrs[0:ROWS[t], t, at:at + k, i], wt[0:ROWS[t], t, 0:k]))
                after(done)
                if i < 2:
                    stage(lambda t, n: nc.vector.tensor_tensor(wt[0:n, t, :], wt[0:n, t, :], attrs[0:n, t, 0:NE, i], ALU.subtract))
            picks(0, pick_bf, pick_bf_ready)
            nc.vector.memset(acc_factor[:, 0:EARLY[0]], ALPHA)
            nc.vector.memset(acc_factor[:, EARLY[0]:6], 1.0).then_inc(factor_set, 1)
            dve.wait_ge(xrows_ready, 3)
            for i, q in enumerate(EARLY):
                dve.wait_ge(shared_ps, i + 1)
                t, half = q // 2, q % 2
                a = acc[0:ROWS[t], t, 512 * half:512 * half + 512]
                nc.vector.scalar_tensor_tensor(out=a, in0=a, scalar=ALPHA, in1=PS[0:ROWS[t], 5 + i, :], op0=ALU.mult, op1=ALU.add)\
                    .then_inc(early_added, 1)
            dve.wait_ge(table_ps, 1)
            slot_values()
            dve.wait_ge(gather_ps, 4)
            picks(4, pick, pick_ready)
            picks(4, pick_bf, pick_bf_ready)

            def expert_step(n, expert, last=False):
                dve.wait_ge(slots_ready, 4 * n + 4)
                dve.wait_ge(acc_added, 6 * n + 1)
                for j in range(2):
                    nc.vector.tensor_scalar(scat[:, j, :], iota_tok, slots[:, j, 1:2], None, ALU.is_equal)\
                        .then_inc(scat_ready, 1)
                for j in range(2):
                    dve.wait_ge(silu_done, 2 * n + j + 1)
                    nc.vector.scalar_tensor_tensor(out=hid[:, j, :], in0=PS[:, 2 + j, HID:2 * HID],
                                                   scalar=slots[:, j, 0:1], in1=act_h[:, j, :],
                                                   op0=ALU.mult, op1=ALU.mult).then_inc(hid_ready, 1)
                for j in range(2):
                    if j and not last:
                        dve.wait_ge(table_ps, n + 2)
                        slot_values()
                        picks(expert, pick, pick_ready)
                    for half in range(2):
                        dve.wait_ge(y_high, 4 * n + 2 * j + half + 1)
                        c = slice(512 * half, 512 * half + 512)
                        nc.vector.tensor_tensor(ysplit[:, j, 1, c], PS[:, 5 + half, :], ysplit[:, j, 0, c].bitcast(F32),
                                                ALU.subtract).then_inc(y_low, 1)
                dve.wait_ge(factor_set, n + 1)
                dve.wait_ge(early_added, len(EARLY))
                for q in range(6):
                    t, half = q // 2, q % 2
                    dve.wait_ge(scat_ps, 6 * n + q + 1)
                    a = acc[0:ROWS[t], t, 512 * half:512 * half + 512]
                    nc.vector.scalar_tensor_tensor(out=a, in0=a, scalar=acc_factor[0:ROWS[t], q:q + 1],
                                                   in1=PS[0:ROWS[t], SCAT_BANK[q], :], op0=ALU.mult, op1=ALU.add)\
                        .then_inc(acc_added, 1)
                if not last:
                    picks(expert, pick_bf, pick_bf_ready)
                dve.wait_ge(acc_added, 6 * n + 7)
                nc.vector.memset(acc_factor[:, :], 1.0).then_inc(factor_set, 1)

            with dve.Fori(0, STEPS - 1) as i:
                expert_step(i, 4 * i + 8)
            dve.wait_ge(rounds_ready, 1)
            more = dve.value_load(rounds_i[0:1, 0:1], min_val=0, max_val=MAX_ROUNDS - 1)
            with dve.If(more > 0):
                with dve.Fori(0, more) as r:
                    dve.wait_ge(pick_ready, r * (3 * STEPS) + 3 * STEPS + 3)
                    dve.wait_ge(pick_bf_ready, r * (3 * STEPS) + 3 * STEPS + 3)
                    for t in range(3):
                        moved = nc.vector.tensor_scalar(pos[0:ROWS[t], t, :], pos[0:ROWS[t], t, :], -float(SLOTS), None, ALU.add)
                    moved.then_inc(pos_moved, 1)
                    dve.wait_ge(pos_moved, r + 1)
                    dve.sem_inc(dve_rounds, 1)
                    with dve.Fori(0, STEPS) as i:
                        expert_step(r * STEPS + i + STEPS - 1, 4 * i + 4)
            expert_step(more * STEPS + STEPS - 1, None, last=True)
            dve.wait_ge(acc_added, (more + 1) * (6 * STEPS) + 1)
            own[0] = dve_last_step

            def low_gate(tile, place):
                for half in range(2):
                    parts = split[:, 2 * place + half, :, :].rearrange("p h (k n) -> p h k n", k=4)
                    dve.wait_ge(gate_high, 2 * tile + half + 1)
                    nc.vector.tensor_tensor(parts[:, 1, :, :], gate_w[half][:, :, ds(P * tile, P)],
                                            parts[:, 0, :, :].bitcast(F32), ALU.subtract).then_inc(gate_low, 1)

            norm(xs, D, ln2vec, (ln2_loaded, 32), 4)
            low_xT(x2T_high, x2T_ready, lambda t: 2 * t)
            dve.wait_ge(gate_low, 4)
            with dve.Fori(0, KD // 2 - 1) as i:
                for b in range(2):
                    low_gate(2 * i + b + 2, b)
            dve.wait_ge(ple_ready, 3)
            for g, (k0, k1) in enumerate(GATE_GROUPS):
                c = slice(P * k0, P * k1)
                for t in range(3):
                    dve.wait_ge(gate_rows, 3 * g + t + 1)
                    p = ple[0:ROWS[t], t, c]
                    after(step(nc.vector.tensor_tensor(p, PS[0:ROWS[t], 2 + 3 * (g % 2) + t, 0:P * (k1 - k0)], p, ALU.mult)))
                    nc.vector.tensor_tensor(xs[0:ROWS[t], t, c], xs[0:ROWS[t], t, c], p, ALU.add).then_inc(y_ready, 1)

        @block.tensor
        def _(pe):
            def transpose_rows(src, t, bank, signal):
                for k in range(KD):
                    ins = pe.transpose(PS[:, bank + k // 4, P * (k % 4):P * (k % 4) + ROWS[t]],
                                       src[0:ROWS[t], t, k::KD], ident[0:ROWS[t], 0:ROWS[t]])
                ins.then_inc(signal, 1)

            def keep_warm(n, bank):
                for _ in range(n):
                    pe.matmul(PS[:, bank, 0:P], ident[:, :], ident[:, :], start=True, stop=True)

            pe.wait_ge(const_ready, 1)
            pe.wait_ge(var_ready, 1)
            keep_warm(WARM[0], 7)
            for t in range(3):
                pe.wait_ge(ln_done, t + 1)
                transpose_rows(xs, t, 2 * t, xT_ps)
            pe.wait_ge(cache_loaded, 32)
            for c in range(2):
                for j in range(JW):
                    ins = pe.transpose(PS[:, 6 + c, P * j:P * (j + 1)], ck[:, c, P * j:P * (j + 1)], ident[:, :])
                ins.then_inc(prep_ps, 1)
            pe.wait_ge(xT_ready, 3)
            pe.sem_inc(proj_free, 4)

            def products(out, s, k0, start, stop, ready=None):
                for k in range(4):
                    if ready:
                        pe.wait_ge(ready, k0 + k + 1)
                    w = split[:, s, :, P * k:P * (k + 1)]
                    for wp, xp in ((0, 0), (0, 1), (1, 0)):
                        ins = pe.matmul(out, w[:, wp, :], xT[:, xp, k0 + k, :], start=(start and k == 0 and (wp, xp) == (0, 0)),
                                        stop=(stop and k == 3 and wp == 1))
                return ins

            def project(first, end, free, freed=0):
                with pe.Fori(first, end) as i:
                    for b in range(4):
                        pe.wait_ge(free, 4 * (i - first + freed) + b + 1)
                        for half in range(2):
                            pe.wait_ge(w_low, 2 * (4 * i + b) + half + 1)
                            products(PS[:, b, 0:TOK], 2 * (b % 2) + half, 4 * half, half == 0, half == 1).then_inc(half_used, 1)

            def rows_of(first, t, bank):
                for j in range(JW):
                    ins = pe.transpose(PS[0:ROWS[t], bank, P * j:P * (j + 1)], zt[:, first + j, cols(t)], ident[:, :])
                ins.then_inc(tok_ps, 1)

            def head(tile, h, c):
                return zt[64 * (h % 2):64 * (h % 2) + 64, tile + h // 2, c]

            project(0, FIRST_STEPS, proj_free)
            pe.wait_ge(proj_free, 4 + 4 * FIRST_STEPS)
            pe.wait_ge(wsmask_ready, 1)
            pe.wait_ge(prep_ready, 2)
            for g in range(8):
                ins = pe.transpose(PS[:, 6 + g // 4, P * (g % 4):P * (g % 4 + 1)], ws[:, g, :], ident[:, :])
            ins.then_inc(prep_ps, 1)
            for t in range(3):
                if t == 2:
                    pe.wait_ge(prep_ready, 3)
                rows_of(K0, t, 4 + t)
            for h in range(HEADS):
                par, i = h % 2, h // 2
                ins = pe.matmul(PS[:, 2 * par + i // 2, 256 * (i % 2):256 * (i % 2) + 256],
                                head(Q0, h, slice(P, 2 * P)), head(K0, h, slice(0, 2 * P)), start=True, stop=True)
            ins.then_inc(score_ps, 1)
            for t in range(3):
                if t:
                    pe.wait_ge(tok_ready_act, t)
                rows_of(V0, t, (7, 4, 5)[t])
            for t in range(3):
                if t < 2:
                    pe.wait_ge(*((tok_ready_act, 3), (tok_ready_dve, 1))[t])
                else:
                    pe.wait_ge(tok_ready_dve, 2)
                rows_of(S0, t, (6, 7, 4)[t])
            pe.wait_ge(score_ready, 1)
            for h in range(HEADS):
                ins = pe.matmul(PS[:, h % 2, P * (h // 2):P * (h // 2 + 1)],
                                head(Q0, h, slice(0, P)), head(K0, h, slice(0, P)), start=True, stop=True)
            ins.then_inc(score_ps, 1)
            pe.wait_ge(tok_ready_act, 6)
            pe.wait_ge(tok_ready_dve, 3)
            for w in range(2):
                if w:
                    pe.wait_ge(score_ready, 4)
                for h in range(4 * w, 4 * w + 4):
                    par, i = h % 2, h // 2
                    for c, (key, n) in enumerate(((ckT[64 * par:64 * par + 64, i, :], 256), (head(K0, h, slice(256, TOK)), DH))):
                        ins = pe.matmul(PS[0:DH, 4 + 2 * par + i % 2, 256 * c:256 * c + n], head(Q0, h, slice(256, TOK)), key,
                                        start=True, stop=True)
                ins.then_inc(score_ps, 1)
            pe.wait_ge(score_ready, 2)
            project(FIRST_STEPS, CHUNK_STEPS, proj_free, FIRST_STEPS)
            pe.wait_ge(ln_done, 6)
            pe.wait_ge(bs_loaded, 16)
            pe.wait_ge(proj_free, 4 + 4 * CHUNK_STEPS)
            for g in range(8):
                par = slice(64 * (g % 2), 64 * (g % 2) + 64)
                for t in range(3):
                    n = ROWS[t]
                    pe.matmul(PS[par, g // 2, cols(t)], ones[0:1, :], bsrow[0:1, g, 0:n], start=True, stop=False)
                    ins = pe.matmul(PS[par, g // 2, cols(t)], vn[0:n, t, 64 * g:64 * g + 64], wsT[0:n, g, 0:n],
                                    start=False, stop=True)
            ins.then_inc(mix_ps, 1)

            def turn_probs(j):
                b = 4 if j % 2 == 0 else 0
                for e in range(2):
                    h = 4 * e + j
                    pe.transpose(PS[:, b + e, 0:P], prob0[:, h, :], ident[:, :])
                    for c in range(2):
                        pe.transpose(PS[:, b + e, P * (c + 1):P * (c + 2)], prob1[:, h, P * c:P * (c + 1)], ident[:, :])
                        pe.transpose(PS[:, b + 2, 192 * e + 64 * c:192 * e + 64 * c + 64], probs[:, h, P * c:P * (c + 1)],
                                     ident[0:DH, 0:DH])
                    ins = pe.transpose(PS[0:DH, b + 2, 192 * e + 128:192 * e + 192], probs[:, h, 256:TOK], ident[0:DH, 0:DH])
                ins.then_inc(probT_ps, 1)

            def attend(j):
                pe.wait_ge(probT_act, j + 1)
                pe.wait_ge(probT_dve, j + 1)
                bank = 7 if j % 2 == 0 else 3
                if j >= 2:
                    pe.wait_ge(oa_ready, j - 1)
                for e in range(2):
                    rows, c = slice(64 * e, 64 * e + 64), slice(64 * (2 * j + e), 64 * (2 * j + e) + 64)
                    pt, ps = probT[:, j, e, :], probT[:, j, 2, :]
                    pe.matmul(PS[rows, bank, 0:P], v_tok[:, 0, c], pt[:, 0:P], start=True, stop=True)
                    pe.matmul(PS[rows, bank, P:2 * P], v_tok[:, 0, c], pt[:, P:2 * P], start=True, stop=False)
                    pe.matmul(PS[rows, bank, P:2 * P], v_tok[:, 1, c], pt[:, 2 * P:3 * P], start=False, stop=True)
                    o = 192 * e
                    pe.matmul(PS[rows, bank, 256:TOK], cv[:, 0, c], ps[:, o:o + 64], start=True, stop=False)
                    pe.matmul(PS[rows, bank, 256:TOK], cv[:, 1, c], ps[:, o + 64:o + 128], start=False, stop=False)
                    ins = pe.matmul(PS[rows, bank, 256:TOK], v_tok[0:DH, 2, c], ps[0:DH, o + 128:o + 192], start=False, stop=True)
                ins.then_inc(oa_ps, 1)

            pe.wait_ge(prob_ready, 3)
            turn_probs(0)
            pe.wait_ge(mix_ready, 1)
            turn_probs(1)
            for j in range(4):
                attend(j)
                if j < 2:
                    turn_probs(j + 2)
            pe.wait_ge(oa_ready, 4)
            pe.sem_inc(branch_free, 4)
            pe.wait_ge(ob_low, 1)
            with pe.Fori(0, 2) as i:
                for b in range(4):
                    pe.wait_ge(branch_free, 4 * i + b + 1)
                    for half in range(2):
                        pe.wait_ge(w_low, 2 * BRANCH_T + 8 * i + 2 * b + half + 1)
                        products(PS[:, 2 * b + half, 0:TOK], 2 * (b % 2) + half, 4 * half, True, True).then_inc(half_used, 1)
            pe.wait_ge(branch_free, 4 + KD)
            pe.sem_inc(out_free, 4)
            for tile in range(KD):
                pe.wait_ge(out_free, tile + 1)
                for half in range(2):
                    pe.wait_ge(w_low, 2 * (OUT_T + tile) + half + 1)
                    products(PS[:, tile % 4, 0:TOK], 2 * (tile % 2) + half, 4 * half, half == 0, half == 1,
                             None if tile else m_low).then_inc(half_used, 1)
            pe.wait_ge(out_free, 4 + KD)
            for t in range(3):
                for j in range(KD):
                    ins = pe.transpose(PS[0:ROWS[t], (4, 6, 0)[t] + j // 4, P * (j % 4):P * (j % 4 + 1)], woT[:, j, cols(t)], ident[:, :])
                ins.then_inc(out_ps, 1)
            pe.wait_ge(residual, 3)
            keep_warm(WARM[1], 7)
            for t in range(3):
                pe.wait_ge(ln_done, 7 + t)
                transpose_rows(xs, t, 2 * t, x1T_ps)
            keep_warm(WARM[2], 7)
            pe.wait_ge(router_low, 1)
            pe.wait_ge(x1T_ready, 3)
            for k in range(KD):
                for wp, xp in ((0, 0), (0, 1), (1, 0)):
                    at = (wp * KD + k) * NE
                    ins = pe.matmul(PS[:, 6, 0:TOK], marks[:, at:at + P], xT[:, xp, k, :], start=(k == 0 and (wp, xp) == (0, 0)),
                                    stop=(k == KD - 1 and wp == 1))
            ins.then_inc(logits_ps, 1)

            def shared_tile(b, halves=(0, 1)):
                for half in halves:
                    pe.wait_ge(w_low, 2 * (SHARED_T + b) + half + 1)
                    products(PS[:, b, 0:TOK], 2 * (b % 2) + half, 4 * half, half == 0, half == 1).then_inc(half_used, 1)

            shared_tile(0, (0,))
            pe.wait_ge(score_sig, 1)
            for t in range(3):
                ins = pe.transpose(PS[0:ROWS[t], 7, NE * t:NE * (t + 1)], scoreT[0:NE, cols(t)], ident[0:NE, 0:NE])
            ins.then_inc(scores_turned, 1)
            shared_tile(0, (1,))
            shared_tile(1)
            shared_tile(2)
            for t in range(3):
                pe.wait_ge(mask_ready, t + 1)
                for u in range(t + 1):
                    lhs = tri[0:ROWS[u], 0:ROWS[t]] if u == t else onesb[:, 0:ROWS[t]]
                    pe.matmul(PS[0:ROWS[t], 7, NE * t:NE * (t + 1)], lhs, mask[0:ROWS[u], u, :], start=(u == 0), stop=(u == t))
            for t in range(3):
                ins = pe.matmul(PS[:, 7, 3 * NE:4 * NE], onesb[0:ROWS[t], :], mask[0:ROWS[t], t, :], start=(t == 0), stop=(t == 2))
            ins.then_inc(pos_ps, 1)
            shared_tile(3)
            pe.sem_inc(acc_added, 1)

            def gather(n, g):
                for k in range(2):
                    for t in range(3):
                        for part in range(2):
                            ins = pe.matmul(PS[:, g % 2, 256 * k:256 * k + 256], xrows[0:ROWS[t], part, t, 2 * g + k, :],
                                            pick[0:ROWS[t], t, :], start=(t == 0 and part == 0), stop=(t == 2 and part == 1))
                ins.then_inc(gather_ps, 1)

            def slot_table(expert):
                for j in range(2):
                    for t in range(3):
                        ins = pe.matmul(PS[:, 4, 10 * j:10 * j + 10], pick_bf[0:ROWS[t], t, P * j:P * (j + 1)],
                                        attrs[0:ROWS[t], t, ds(expert + 2 * j, 2), :].rearrange("p e f -> p (e f)"),
                                        start=(t == 0), stop=(t == 2))
                ins.then_inc(table_ps, 1)

            def shared_down(q, bank, start, stop):
                t, half = q // 2, q % 2
                for m in range(2):
                    ins = pe.matmul(PS[0:ROWS[t], bank, :], hsT[:, m, cols(t)], sw2[:, m, 512 * half:512 * half + 512],
                                    start=(start and m == 0), stop=(stop and m == 1))
                return ins

            def expert_step(n, expert, first=False, last=False):
                def up(j, ks):
                    for k in ks:
                        if k % 4 == 0:
                            pe.wait_ge(w13_loaded[j][k // 4], 64 * (n + 1))
                        for e in range(2):
                            c = slice(64 * e, 64 * e + 64)
                            ins = pe.matmul(PS[c, 2 + j, :], xgT[:, k, P * j + 64 * e:P * j + 64 * e + 64], w13(j, e, k),
                                            start=(k == 0), stop=(k == KD - 1))
                        if k % 4 == 3:
                            ins.then_inc(up_done[j], 1)

                def turn_hidden(j):
                    pe.wait_ge(hid_ready, 2 * n + j + 1)
                    for k in range(2):
                        ins = pe.transpose(PS[:, 4, HID * j + P * k:HID * j + P * (k + 1)], hid[:, j, k::2], ident[:, :])
                    ins.then_inc(hidT_ps, 1)

                def down(j, half):
                    for k in range(2):
                        for e in range(2):
                            c = slice(64 * e, 64 * e + 64)
                            ins = pe.matmul(PS[c, 5 + half, :], hidT[:, j, k, c], w2(j, e, k, half), start=(k == 0), stop=(k == 1))
                    ins.then_inc(y_ps, 1)

                def gather_next(g):
                    if g >= 2:
                        pe.wait_ge(gathered_ready, 4 * n + g + 3)
                    gather(n + 1, g)

                def scatter(q, j):
                    t, half = q // 2, q % 2
                    for part in range(2):
                        ins = pe.matmul(PS[:, SCAT_BANK[q], :], scat[:, j, P * t:P * (t + 1)],
                                        ysplit[:, j, part, 512 * half:512 * half + 512],
                                        start=(j == 0 and part == 0 and not (last and q in (2, 3))),
                                        stop=(j == 1 and part == 1))
                    if first and j == 0 and q < 2:
                        shared_down(q, SCAT_BANK[q], False, False)
                    if j == 1:
                        ins.then_inc(scat_ps, 1)

                if first:
                    pe.wait_ge(shared_hid, 2)
                    pe.wait_ge(sw2_loaded, 16)
                    for b, q in enumerate(EARLY):
                        shared_down(q, 5 + b, True, True).then_inc(shared_ps, 1)
                    pe.wait_ge(pick_ready, 3)
                    pe.wait_ge(xrows_ready, 3)
                    gather(0, 0)
                    gather(0, 1)
                    pe.wait_ge(pick_bf_ready, 3)
                    slot_table(0)
                    for g in range(4):
                        pe.wait_ge(gathered_ready, g + 1)
                        up(0, range(2 * g, 2 * g + 2))
                        if g < 2:
                            gather(0, g + 2)
                else:
                    pe.wait_ge(gathered_ready, 4 * n + 4)
                    pe.wait_ge(acc_added, 6 * n - 3)
                    up(0, range(KD))
                up(1, range(4))
                turn_hidden(0)
                up(1, range(4, KD))
                pe.wait_ge(acc_added, 6 * n + 1)
                if not last:
                    pe.wait_ge(pick_ready, 3 * n + 6)
                    gather_next(0)
                    gather_next(1)
                else:
                    shared_down(2, SCAT_BANK[2], True, False)
                turn_hidden(1)
                pe.wait_ge(hidT_ready, 2 * n + 1)
                pe.wait_ge(w2_loaded[0], 32 * (n + 1))
                if first:
                    pe.wait_ge(early_added, len(EARLY))
                down(0, 0)
                down(0, 1)
                if last:
                    shared_down(3, SCAT_BANK[3], True, False)
                if not last:
                    gather_next(2)
                    gather_next(3)
                pe.wait_ge(hidT_ready, 2 * n + 2)
                if not last:
                    pe.wait_ge(pick_bf_ready, 3 * n + 6)
                    slot_table(expert)
                ahead, before = (5, 3) if last else (3, 0)
                if last:
                    pe.wait_ge(y_high, 4 * n + 2)
                    pe.wait_ge(y_low, 4 * n + 2)
                    pe.wait_ge(scat_ready, 2 * n + 2)
                    for q in range(before):
                        scatter(q, 0)
                pe.wait_ge(w2_loaded[1], 32 * (n + 1))
                for half in range(2):
                    pe.wait_ge(y_high, 4 * n + half + 1)
                    pe.wait_ge(y_low, 4 * n + half + 1)
                    down(1, half)
                if not last:
                    pe.wait_ge(scat_ready, 2 * n + 2)
                for q in range(before, ahead):
                    scatter(q, 0)
                for q in range(6):
                    if q == 3 and not last:
                        pe.wait_ge(gathered_ready, 4 * n + 8)
                    if q == 5:
                        pe.wait_ge(acc_added, 6 * n + 4)
                    if q >= ahead:
                        scatter(q, 0)
                    pe.wait_ge(y_high, 4 * n + 3 + (q > 0))
                    pe.wait_ge(y_low, 4 * n + 3 + (q > 0))
                    scatter(q, 1)

            expert_step(0, 4, first=True)
            with pe.Fori(1, STEPS - 1) as i:
                expert_step(i, 4 * i + 4)
            more = pe.value_load(rounds_i[0:1, 0:1], min_val=0, max_val=MAX_ROUNDS - 1)
            with pe.If(more > 0):
                with pe.Fori(0, more) as r:
                    with pe.Fori(0, STEPS) as i:
                        expert_step(r * STEPS + i + STEPS - 1, 4 * i)
            expert_step(more * STEPS + STEPS - 1, None, last=True)
            pe.wait_ge(ple_loaded, 48)
            for t in range(3):
                for m in range(2):
                    ins = pe.transpose(PS[:, 5 + m, cols(t)], p_tok[0:ROWS[t], t, P * m:P * (m + 1)], ident[0:ROWS[t], 0:ROWS[t]])
            ins.then_inc(pT_ps, 1)
            pe.wait_ge(pT_ready, 1)
            def embed(t):
                for half in range(2):
                    for m in range(2):
                        ins = pe.matmul(PS[0:ROWS[t], PLE_BANK[t] + half, :], pT[:, m, cols(t)], proj_w[:, m, 512 * half:512 * half + 512],
                                        start=(m == 0), stop=(m == 1))
                ins.then_inc(ple_ps, 1)

            embed(0)
            pe.wait_ge(acc_added, (more + 1) * (6 * STEPS) + 1)
            embed(1)
            for t in range(3):
                pe.wait_ge(ln_done, 10 + t)
                if t:
                    pe.wait_ge(ple_ready, 2)
                transpose_rows(xs, t, 2 * t, x2T_ps)
            embed(2)
            pe.wait_ge(x2T_ready, 3)
            pe.sem_inc(gate_sig, 2)

            def gate_turn(g):
                k0, k1 = GATE_GROUPS[g]
                pe.wait_ge(gate_sig, 2 + k1)
                if g == 2:
                    pe.wait_ge(y_ready, 3)
                for t in range(3):
                    for j in range(k0, k1):
                        ins = pe.transpose(PS[0:ROWS[t], 2 + 3 * (g % 2) + t, P * (j - k0):P * (j - k0 + 1)], sgT[:, j, cols(t)],
                                           ident[:, :])
                    ins.then_inc(gate_rows, 1)

            for tile in range(KD):
                pe.wait_ge(gate_sig, tile + 1)
                for half in range(2):
                    pe.wait_ge(gate_low, 2 * tile + half + 1)
                    products(PS[:, tile % 2, 0:TOK], 2 * (tile % 2) + half, 4 * half, half == 0, half == 1).then_inc(gate_used, 1)
                for g in range(2):
                    if tile == GATE_GROUPS[g][1]:
                        gate_turn(g)
            gate_turn(2)


_INS = ["x_prompt", "x_sample", "cache_attn_k", "cache_attn_v", "p_prompt", "p_sample", "ln_in_g", "ln_in_b", "w_in",
        "attn_rel_bias", "mlp_ln_g", "mlp_ln_b", "mlp_w_s", "mlp_b_s", "w_branch_a", "w_branch_b", "w_out", "ln1_g", "ln1_b",
        "router_w", "router_bias", "exp_w1", "exp_w3", "exp_w2", "shared_w1", "shared_w3", "shared_w2", "ln2_g", "ln2_b",
        "ple_w_gate", "ple_w_proj"]


def kernel(**inputs):
    import numpy as _np
    import concourse.bacc as _bacc
    from concourse import mybir as _mybir
    from concourse.bass_utils import run_bass_kernel_spmd as _run

    x, s = inputs["x_prompt"].shape, inputs["x_sample"].shape
    kv = inputs["cache_attn_k"].shape
    width = inputs["mlp_ln_g"].shape[-1]
    outs = [x, s, (1, x[0], x[1], *kv[3:]), (1, x[0], x[1], *kv[3:]), (1, s[0], s[1], *kv[3:]), (1, s[0], s[1], *kv[3:]),
            (1, x[0], 128, width), (1, s[0], s[1], width)]
    nc = _bacc.Bacc("TRN2", target_bir_lowering=False, num_devices=1)
    arrays, args = {}, []
    for name in _INS:
        a = _np.ascontiguousarray(inputs[name])
        arrays[f"in_{name}_dram"] = a
        args.append(nc.dram_tensor(f"in_{name}_dram", a.shape, _mybir.dt.from_np(a.dtype), kind="ExternalInput").ap())
    for i, shape in enumerate(outs):
        args.append(nc.dram_tensor(f"out_{i}_dram", shape, _mybir.dt.float32, kind="ExternalOutput").ap())
    trunk_step(nc, *args)
    r = _run(nc, [arrays], core_ids=[0])
    return tuple(r.results[0][f"out_{i}_dram"] for i in range(len(outs)))
```
